# Optimizing a Trainium2 kernel written in Bass

```python
import math
import jax, jax.numpy as jnp
from jax import lax
import numpy as np

D_MODEL = 1024
BATCH = 1
SEQ = 2048
DEPTH = 1

CTX_LEN = 256
GRID_W = 64
MIX_W = 2 * D_MODEL
SSD_W = MIX_W // 2
HY_W = MIX_W - SSD_W
SSD_HEADDIM = 64
SSD_HEADS = SSD_W // SSD_HEADDIM
SSD_GROUPS = 2
SSD_STATE = 128
SSD_CONV = 3
CHUNK = 128
HY_CONV = 3
HY_EMB = 33
HY_BANDS = (HY_EMB - 1) // 2
HY_FILT_W = 64
HY_TARGET = 1e-2
HY_FAST_PCT = 0.3
HY_SLOW_PCT = 1.5
HY_MIN_DECAY = math.log(HY_TARGET) / HY_SLOW_PCT
HY_MAX_DECAY = math.log(HY_TARGET) / HY_FAST_PCT
EPS = 1e-6

XBC_W = SSD_W + 2 * SSD_GROUPS * SSD_STATE
COL_ZS = 0
COL_XBC = COL_ZS + SSD_W
COL_DT = COL_XBC + XBC_W
COL_ZH = COL_DT + 2 * SSD_HEADS
COL_HY = COL_ZH + HY_W
IN_W = COL_HY + 3 * HY_W

kernel_name = 'hymba_ssd_hyena_prefix_dit'

def rmsnorm(u, w):
    uf = u.astype(jnp.float32)
    uf = uf * lax.rsqrt(jnp.mean(uf * uf, axis=-1, keepdims=True) + EPS)
    return uf.astype(u.dtype) * w

def seq_conv(u, w, b):
    k = w.shape[0]
    out = lax.conv_general_dilated(
        u, w[:, None, :].astype(u.dtype), window_strides=(1,),
        padding=[(k // 2, k // 2)], dimension_numbers=('NWC', 'WIO', 'NWC'),
        feature_group_count=u.shape[-1])
    return out + b

def grid_row_conv(u, w, b):
    bsz, n_tok, ch = u.shape
    rows = n_tok // GRID_W
    return seq_conv(u.reshape(bsz * rows, GRID_W, ch), w, b).reshape(bsz, n_tok, ch)

def ssd_chunked(xs, dt, A, Bm, Cm, h0):
    b, L, H, P = xs.shape
    G, N = Bm.shape[2], Bm.shape[3]
    Hg = H // G
    nc = L // CHUNK
    x_c = xs.reshape(b, nc, CHUNK, G, Hg, P)
    dt_c = dt.reshape(b, nc, CHUNK, G, Hg)
    B_c = Bm.reshape(b, nc, CHUNK, G, N)
    C_c = Cm.reshape(b, nc, CHUNK, G, N)
    a_cum = jnp.cumsum(dt_c * A.reshape(G, Hg), axis=2)
    lower = jnp.tril(jnp.ones((CHUNK, CHUNK), dtype=bool))
    seg = a_cum[:, :, :, None] - a_cum[:, :, None, :]
    decay = jnp.exp(jnp.where(lower[:, :, None, None], seg, -jnp.inf))
    xdt = dt_c[..., None] * x_c
    cb = jnp.einsum('bcign,bcjgn->bcijg', C_c, B_c)
    y_intra = jnp.einsum('bcijg,bcijgh,bcjghp->bcighp', cb, decay, xdt)
    to_end = jnp.exp(a_cum[:, :, -1:] - a_cum)
    states = jnp.einsum('bcjgn,bcjghp->bcghpn', B_c, to_end[..., None] * xdt)
    chunk_decay = jnp.exp(a_cum[:, :, -1])

    def carry(h, inp):
        s_c, d_c = inp
        return d_c[..., None, None] * h + s_c, h

    h_last, h_prev = lax.scan(carry, h0, (jnp.moveaxis(states, 1, 0),
                                          jnp.moveaxis(chunk_decay, 1, 0)))
    h_prev = jnp.moveaxis(h_prev, 0, 1)
    y_inter = jnp.einsum('bcign,bcigh,bcghpn->bcighp', C_c, jnp.exp(a_cum), h_prev)
    return (y_intra + y_inter).reshape(b, L, H, P), h_last

def ssd_direction(xs, dt_raw, Bm, Cm, dt_bias, a_log, d_skip, h0):
    dt = jax.nn.softplus(dt_raw.astype(jnp.float32) + dt_bias)
    A = -jnp.exp(a_log.astype(jnp.float32))
    y, h = ssd_chunked(xs, dt, A, Bm, Cm, h0)
    return y + d_skip[:, None] * xs, h

def ssd_mixer(xbc_raw, dt_raw, conv_fn, conv_w, conv_b, dt_bias, a_log, d_skip, h0_f, h0_b):
    xbc = jax.nn.silu(conv_fn(xbc_raw, conv_w, conv_b))
    bsz, L, _ = xbc.shape
    gn = SSD_GROUPS * SSD_STATE
    xs = xbc[..., :SSD_W].reshape(bsz, L, SSD_HEADS, SSD_HEADDIM)
    Bm = xbc[..., SSD_W:SSD_W + gn].reshape(bsz, L, SSD_GROUPS, SSD_STATE)
    Cm = xbc[..., SSD_W + gn:].reshape(bsz, L, SSD_GROUPS, SSD_STATE)
    rev = lambda t: jnp.flip(t, axis=1)
    y_f, h_f = ssd_direction(xs, dt_raw[..., :SSD_HEADS], Bm, Cm,
                             dt_bias[0], a_log[0], d_skip[0], h0_f)
    y_b, h_b = ssd_direction(rev(xs), rev(dt_raw[..., SSD_HEADS:]), rev(Bm), rev(Cm),
                             dt_bias[1], a_log[1], d_skip[1], h0_b)
    y = (y_f + rev(y_b)).reshape(bsz, L, SSD_W)
    return y, h_f, h_b

def hyena_filters(L, w1, b1, w2, b2, w3, b3, w4, freq):
    t = jnp.linspace(0.0, 1.0, L, dtype=jnp.float32)[:, None]
    w = (2.0 * math.pi / L) * jnp.arange(L, dtype=jnp.float32)[:, None]
    f = jnp.linspace(1e-4, HY_BANDS - 1, HY_BANDS, dtype=jnp.float32)[None, :]
    feats = jnp.concatenate([t, jnp.cos(f * w), -jnp.sin(f * w)], axis=-1)
    fr = freq.astype(jnp.float32)
    h = jnp.sin(fr * (feats @ w1 + b1))
    h = jnp.sin(fr * (h @ w2 + b2))
    h = jnp.sin(fr * (h @ w3 + b3))
    h = (h @ w4).astype(jnp.float32)
    deltas = jnp.abs(jnp.linspace(HY_MIN_DECAY, HY_MAX_DECAY, HY_W, dtype=jnp.float32))
    window = jnp.exp(-t * deltas)
    return h[:, :HY_W] * window, h[:, HY_W:] * window

def bidir_fft_conv(u, h_f, h_b, skip):
    L = u.shape[1]
    filt = jnp.concatenate([h_f, jnp.zeros((1, h_f.shape[1]), jnp.float32),
                            jnp.flip(h_b[1:], axis=0)], axis=0)
    U = jnp.fft.rfft(u.astype(jnp.float32), n=2 * L, axis=1)
    F = jnp.fft.rfft(filt, n=2 * L, axis=0)
    y = jnp.fft.irfft(U * F[None], n=2 * L, axis=1)[:, :L]
    return (y + u.astype(jnp.float32) * skip).astype(u.dtype)

def hyena_mixer(u_raw, conv_fn, conv_w, conv_b, w1, b1, w2, b2, w3, b3, w4, freq, skip):
    u = conv_fn(u_raw, conv_w, conv_b)
    x0, x1, v = jnp.split(u, 3, axis=-1)
    h_f, h_b = hyena_filters(u.shape[1], w1, b1, w2, b2, w3, b3, w4, freq)
    return x0 * bidir_fft_conv(x1 * v, h_f, h_b, skip)

def merge_groups(p, y_s, y_h, gw):
    ys = rmsnorm(y_s * jax.nn.silu(p[..., COL_ZS:COL_XBC]), gw[:SSD_W])
    yh = rmsnorm(y_h * jax.nn.silu(p[..., COL_ZH:COL_HY]), gw[SSD_W:])
    return jnp.concatenate([ys, yh], axis=-1)

def setup_inputs(seed: int = 0) -> dict:
    key = jax.random.key(seed)
    ks = jax.random.split(key, 27)
    nrm = lambda k, shape, s: jax.random.normal(k, shape, jnp.float32) * s
    dt0 = jnp.exp(jax.random.uniform(ks[10], (DEPTH, 2, SSD_HEADS), jnp.float32,
                                     math.log(1e-3), math.log(1e-1)))
    dt_bias = dt0 + jnp.log(-jnp.expm1(-dt0))
    a_log = jnp.log(jax.random.uniform(ks[11], (DEPTH, 2, SSD_HEADS), jnp.float32, 1.0, 16.0))
    return {
        'x': nrm(ks[0], (BATCH, SEQ, D_MODEL), 1.0),
        'c': nrm(ks[1], (BATCH, D_MODEL), 1.0),
        'ctx': nrm(ks[2], (BATCH, CTX_LEN, D_MODEL), 1.0),
        'c_ctx': nrm(ks[3], (D_MODEL,), 1.0),
        'norm_w': 1.0 + nrm(ks[4], (DEPTH, D_MODEL), 0.02),
        'ada_w': nrm(ks[5], (DEPTH, D_MODEL, 3 * D_MODEL), 0.5 * D_MODEL ** -0.5),
        'ada_b': nrm(ks[6], (DEPTH, 3 * D_MODEL), 0.02),
        'w_in': nrm(ks[7], (DEPTH, D_MODEL, IN_W), D_MODEL ** -0.5),
        'ssd_conv_w': nrm(ks[8], (DEPTH, SSD_CONV, XBC_W), SSD_CONV ** -0.5),
        'ssd_conv_b': nrm(ks[9], (DEPTH, XBC_W), 0.02),
        'dt_bias': dt_bias,
        'a_log': a_log,
        'd_skip': 1.0 + nrm(ks[12], (DEPTH, 2, SSD_HEADS), 0.02),
        'hy_conv_w': nrm(ks[13], (DEPTH, HY_CONV, 3 * HY_W), HY_CONV ** -0.5),
        'hy_conv_b': nrm(ks[14], (DEPTH, 3 * HY_W), 0.02),
        'filt_w1': nrm(ks[15], (DEPTH, HY_EMB, HY_FILT_W), HY_EMB ** -0.5),
        'filt_b1': nrm(ks[16], (DEPTH, HY_FILT_W), 0.02),
        'filt_w2': nrm(ks[17], (DEPTH, HY_FILT_W, HY_FILT_W), HY_FILT_W ** -0.5),
        'filt_b2': nrm(ks[18], (DEPTH, HY_FILT_W), 0.02),
        'filt_w3': nrm(ks[19], (DEPTH, HY_FILT_W, HY_FILT_W), HY_FILT_W ** -0.5),
        'filt_b3': nrm(ks[20], (DEPTH, HY_FILT_W), 0.02),
        'filt_w4': nrm(ks[21], (DEPTH, HY_FILT_W, 2 * HY_W), HY_FILT_W ** -0.5),
        'filt_freq': 1.0 + nrm(ks[22], (DEPTH, HY_FILT_W), 0.02),
        'hy_bias': nrm(ks[23], (DEPTH, HY_W), 0.5),
        'gnorm_w': 1.0 + nrm(ks[24], (DEPTH, MIX_W), 0.02),
        'w_out': nrm(ks[25], (DEPTH, MIX_W, D_MODEL), MIX_W ** -0.5),
        'final_norm_w': 1.0 + nrm(ks[26], (D_MODEL,), 0.02),
    }

def reference(x, c, ctx, c_ctx, norm_w, ada_w, ada_b, w_in, ssd_conv_w, ssd_conv_b,
              dt_bias, a_log, d_skip, hy_conv_w, hy_conv_b, filt_w1, filt_b1, filt_w2,
              filt_b2, filt_w3, filt_b3, filt_w4, filt_freq, hy_bias, gnorm_w, w_out,
              final_norm_w):
    bsz = x.shape[0]
    hc = ctx
    s_lat = jax.nn.silu(c)
    s_ctx = jax.nn.silu(c_ctx)
    for l in range(DEPTH):
        shift_x, scale_x, gate_x = jnp.split(s_lat @ ada_w[l] + ada_b[l], 3, axis=-1)
        shift_c, scale_c, gate_c = jnp.split(s_ctx @ ada_w[l] + ada_b[l], 3, axis=-1)
        p_x = (rmsnorm(x, norm_w[l]) * (1.0 + scale_x[:, None]) + shift_x[:, None]) @ w_in[l]
        p_c = (rmsnorm(hc, norm_w[l]) * (1.0 + scale_c) + shift_c) @ w_in[l]
        ssd_p = (ssd_conv_w[l], ssd_conv_b[l], dt_bias[l], a_log[l], d_skip[l])
        hy_p = (hy_conv_w[l], hy_conv_b[l], filt_w1[l], filt_b1[l], filt_w2[l], filt_b2[l],
                filt_w3[l], filt_b3[l], filt_w4[l], filt_freq[l], hy_bias[l])
        h0 = jnp.zeros((bsz, SSD_GROUPS, SSD_HEADS // SSD_GROUPS, SSD_HEADDIM, SSD_STATE),
                       jnp.float32)
        y_sc, hf_c, hb_c = ssd_mixer(p_c[..., COL_XBC:COL_DT], p_c[..., COL_DT:COL_ZH],
                                     seq_conv, *ssd_p, h0, h0)
        y_sx, _, _ = ssd_mixer(p_x[..., COL_XBC:COL_DT], p_x[..., COL_DT:COL_ZH],
                               grid_row_conv, *ssd_p, hf_c, hb_c)
        y_hx = hyena_mixer(p_x[..., COL_HY:], grid_row_conv, *hy_p)
        x = x + gate_x[:, None] * (merge_groups(p_x, y_sx, y_hx, gnorm_w[l]) @ w_out[l])
        if l < DEPTH - 1:
            y_hc = hyena_mixer(p_c[..., COL_HY:], seq_conv, *hy_p)
            hc = hc + gate_c * (merge_groups(p_c, y_sc, y_hc, gnorm_w[l]) @ w_out[l])
    return rmsnorm(x, final_norm_w)


_drawn_inputs = setup_inputs


def setup_inputs(seed=0):
    import zlib

    import numpy as np

    out = dict(_drawn_inputs(seed))
    spreads = {}
    factors = {'ctx': 8.0,
     'c_ctx': 8.0,
     'norm_w': 6.018,
     'ssd_conv_b': 22.735,
     'd_skip': 64.0,
     'hy_conv_b': 15.9,
     'filt_b1': 7.172,
     'filt_b2': 5.603,
     'filt_b3': 5.047,
     'filt_freq': 8.0,
     'hy_bias': 4.791,
     'gnorm_w': 25.735,
     'final_norm_w': 8.552}
    for name, (base, spread) in spreads.items():
        noise = np.random.default_rng([zlib.crc32(name.encode()), seed]).standard_normal(out[name].shape)
        drawn = base * np.exp(spread * noise) if base else spread * noise
        out[name] = __import__('jax').numpy.asarray(drawn.astype(out[name].dtype))
    for name, factor in factors.items():
        out[name] = (out[name] * factor).astype(out[name].dtype)
    return out
```

```python
from contextlib import ExitStack

import numpy as np
import concourse.bass as bass
from concourse import mybir

F32 = mybir.dt.float32
BF16 = mybir.dt.bfloat16
ALU = mybir.AluOpType
ACT = mybir.ActivationFunctionType

P = 128
BANK = 512
D = 1024
KT = D // P
SEQ, CTX = 2048, 256
TOK = SEQ + CTX
CHUNK = 128
NC_LAT, NC_CTX = SEQ // CHUNK, CTX // CHUNK
NCH = NC_LAT + NC_CTX
GRID_W = 64
HEADS, HEADDIM, GROUPS, STATE = 16, 64, 2, 128
HPG = HEADS // GROUPS
XBC_T = (D + 2 * GROUPS * STATE) // P
COL_ZS = 0
COL_XBC = COL_ZS + D
COL_DT = COL_XBC + XBC_T * P
COL_ZH = COL_DT + 2 * HEADS
COL_HY = COL_ZH + D
EPS = 1e-6
FW = 64
EMB = 33
N_FFT = 2 * SEQ
RIN, ROUT = 16, 256
FG = 4
NG = P // FG
PI = 3.1415925
TWO_PI = 2.0 * np.pi
ROUNDER = 1.5 * 2.0 ** 23
PI_A = 6.28125
PI_B = float(np.float32(np.floor((TWO_PI - PI_A) * 2 ** 20) / 2 ** 20))
PI_C = float(np.float32(TWO_PI - PI_A - PI_B))


def chained(eng, sem, start=0):
    count = [0]

    def step(ins):
        count[0] += 1
        ins.then_inc(sem, 1)
        eng.wait_ge(sem, start + count[0])
    return step


LEAD = 20


def lead(eng, *sems, unit=1):
    for s in sems:
        eng.sem_inc(s, LEAD * unit)


def nth(n, unit=1):
    return (n + LEAD + 1) * unit


def dft_tables():
    f32 = np.float32
    q, k1 = np.arange(P), np.arange(P)

    def first(rows):
        ang = 2 * np.pi * ((rows[:, None] * k1) % ROUT) / ROUT
        re, im = np.cos(ang), -np.sin(ang)
        im[:, 0] = (-1.0) ** rows
        return np.stack([re, im], 1)
    fwd = np.stack([first(q), first(ROUT - 1 - q)], 1)
    n2, j = np.arange(RIN), np.arange(RIN)
    mats = np.zeros((NG, 5, 2, FG, RIN, 2, FG, RIN))
    S, A, B, G1, G2 = (mats[:, m] for m in range(5))
    for g in range(NG):
        for l in range(FG):
            k = FG * g + l
            low = j < RIN // 2
            bins = k + ROUT * j if k else np.where(low, ROUT * j, P + ROUT * (j - RIN // 2))
            ang = 2 * np.pi * ((n2[:, None] * bins) % N_FFT) / N_FFT
            c, s = np.cos(ang), np.sin(ang)
            if k:
                S[g, 0, l, :, 0, l], S[g, 1, l, :, 0, l] = c, s
                S[g, 0, l, :, 1, l], S[g, 1, l, :, 1, l] = -s, c
            else:
                for r, m in ((0, low), (1, ~low)):
                    S[g, r, l, :, 0, l], S[g, r, l, :, 1, l] = c * m, -s * m
                S[g, :, l, :, 1, l, 0] = 0
                S[g, 0, l, :, 1, l, 0] = (-1.0) ** n2
            for r in range(2):
                A[g, :, l, :, r, l] = S[g, :, l, :, 0, l]
                B[g, :, l, :, r, l] = S[g, :, l, :, 1, l]
            if k:
                yre, yim = np.stack([c.T, s.T], 1), np.stack([-s.T, c.T], 1)
            else:
                A[g, :, l, :, 1, l, 0] = S[g, :, l, :, 1, l, 0]
                B[g, :, l, :, :, l, 0] = 0
                yre, yim = np.zeros((RIN, 2, RIN)), np.zeros((RIN, 2, RIN))
                for r, m in ((0, low), (1, ~low)):
                    yre[m, r], yim[m, r] = 2 * c.T[m], -2 * s.T[m]
                yre[0, 0], yim[0, 0], yim[0, 1] = 1, (-1.0) ** n2, 0
            G1[g, 0, l, :, :, l], G1[g, 1, l, :, :, l] = yre, yim
            G2[g, 1, l, :, :, l], G2[g, 0, l, :, :, l] = -yre, yim
            if not k:
                G2[g, :, l, 0] = 0
    mats = mats.reshape(NG, 5, P, P).transpose(0, 2, 1, 3)
    ang = 2 * np.pi * ((k1[:, None] * q) % ROUT) / ROUT
    er, ei = 2 * np.cos(ang) / N_FFT, -2 * np.sin(ang) / N_FFT
    er[0], ei[0] = 1 / N_FFT, (-1.0) ** q / N_FFT
    return fwd.astype(f32), np.ascontiguousarray(mats, dtype=f32), np.stack([er, ei], 1).astype(f32)


def shape_constants():
    f32 = np.float32
    fwd, mats, back = dft_tables()
    t = np.linspace(0.0, 1.0, SEQ, dtype=f32)[:, None]
    w = (f32(2.0 * np.pi / SEQ) * np.arange(SEQ, dtype=f32))[:, None]
    f = np.linspace(1e-4, (EMB - 1) // 2 - 1, (EMB - 1) // 2, dtype=f32)[None, :]
    feats = np.concatenate([t, np.cos(f * w), -np.sin(f * w)], axis=1)
    lo, hi = np.log(1e-2) / 1.5, np.log(1e-2) / 0.3
    deltas = np.abs(np.linspace(lo, hi, D, dtype=f32))
    q, n2 = np.arange(P)[:, None], np.arange(RIN)[None, :]
    mt = np.stack([-(RIN * q + n2), -(RIN * q + RIN - n2)], 2) / (SEQ - 1)
    i = np.arange(P)
    upto, since = (i[:, None] <= i[None, :]), (i[:, None] >= i[None, :])
    tri = np.stack([upto, since], 1)
    return {
        "k_fwd": fwd, "k_mats": mats, "k_back": back,
        "k_feats": np.ascontiguousarray(feats.T, dtype=f32), "k_deltas": deltas[None, :],
        "k_mt": mt.astype(f32), "k_eye": np.eye(P, dtype=f32), "k_tri": tri.astype(f32),
    }
def prepare(nc, t, keep):
    with ExitStack() as ph:
        def sem(name):
            return nc.alloc_semaphore(name)

        def sb(name, shape, dt=F32):
            return ph.enter_context(nc.sbuf_tensor("p_" + name, shape, dt))

        def psum(name, shape):
            return ph.enter_context(nc.psum_tensor("p_" + name, shape, F32))

        xnT, hT, eye, gate_row = keep["xnT"], keep["hT"], keep["eye"], keep["gate_row"]
        RING = 3
        c_col = sb("c_col", [P, KT, 2])
        s_col = sb("s_col", [P, KT, 2])
        s_wide = sb("s_wide", [P, KT, P])
        ada = sb("ada", [P, RING, 3 * D])
        ada_b_col = sb("ada_b_col", [P, 2 * KT])
        ada_b_gate = sb("ada_b_gate", [P, D])
        norm_w = sb("norm_w", [P, KT])
        mod = sb("mod", [P, 2, 2, KT])
        xg = sb("xg", [P, 2, 4, D])
        squares = sb("squares", [P, D])
        ss = sb("ss", [P, NCH])
        rstd = sb("rstd", [P, NCH])
        halves = sb("halves", [P, NCH])
        feats = sb("feats", [EMB, SEQ])
        w1 = sb("w1", [EMB, FW])
        w23 = sb("w23", [FW, 2, FW])
        fb = sb("fb", [FW, 3])
        freq = sb("freq", [FW, 1])
        ang = sb("ang", [FW, SEQ])
        turns = sb("turns", [FW, SEQ])
        mod_ps = psum("mod_ps", [P, 2 * KT, 2])
        gate_ps = psum("gate_ps", [P, D])
        net_ps = psum("net_ps", [FW, 2, BANK])
        tr = psum("tr", [P, 2, BANK])

        c_in, net_in, small_in, silu_done, wide_done = (sem(n) for n in ("c_in", "net_in", "small_in", "silu_done", "wide_done"))
        ada_in = [sem(f"ada_in{i}") for i in range(RING)]
        x_in = [sem(f"x_in{i}") for i in range(2)]
        ada_used, mod_done, mod_ready, v_step = (sem(n) for n in ("ada_used", "mod_done", "mod_ready", "p_v_step"))
        net_mm, net_out, net_ang, sin_done = (sem(n) for n in ("net_mm", "net_out", "net_ang", "sin_done"))
        sq_done, rstd_done, x_scaled, tr_done, tr_used, pool_step = (
            sem(n) for n in ("sq_done", "rstd_done", "x_scaled", "tr_done", "tr_used", "pool_step"))
        tiles = [4, 4, 4, 4, NC_CTX]
        x_dram = [t["x"][0].rearrange("(g a p) d -> g p a d", a=4, p=P)[g] for g in range(4)]
        x_dram.append(t["ctx"][0].rearrange("(a p) d -> p a d", p=P))
        block = ph.enter_context(nc.Block())

        @block.sync
        def _(sp):
            with nc.allow_non_contiguous_dma(reason="small vectors by column"):
                sp.dma_start(c_col[:, :, 0], t["c"][0].rearrange("(k p) -> p k", p=P)).then_inc(c_in, 16)
                sp.dma_start(c_col[:, :, 1], t["c_ctx"].rearrange("(k p) -> p k", p=P)).then_inc(c_in, 16)
            ada_k = t["ada_w"][0].rearrange("(k p) n -> k p n", p=P)
            for k in range(KT):
                if k >= RING:
                    sp.wait_ge(ada_used, k - RING + 1)
                sp.dma_start(ada[:, k % RING], ada_k[k]).then_inc(ada_in[k % RING], 16)
                if k == RING - 1:
                    for g in range(2):
                        sp.dma_start(xg[:, g], x_dram[g]).then_inc(x_in[g], 16)
            for g in range(2, 5):
                sp.wait_ge(tr_done, KT * (g - 1))
                sp.dma_start(xg[:, g % 2, 0:tiles[g]], x_dram[g]).then_inc(x_in[g % 2], 16)

        @block.gpsimd
        def _(pool):
            with nc.allow_non_contiguous_dma(reason="small vectors by column"):
                pool.dma_start(feats[:], t["k_feats"]).then_inc(net_in, 16)
                pool.dma_start(w1[:], t["filt_w1"][0]).then_inc(net_in, 16)
                pool.dma_start(w23[:, 0], t["filt_w2"][0]).then_inc(net_in, 16)
                pool.dma_start(w23[:, 1], t["filt_w3"][0]).then_inc(net_in, 16)
                for n in range(3):
                    pool.dma_start(fb[:, n:n + 1], t[f"filt_b{n + 1}"].rearrange("a c -> c a")).then_inc(net_in, 16)
                pool.dma_start(freq[:], t["filt_freq"].rearrange("a c -> c a")).then_inc(net_in, 16)
                pool.dma_start(eye[:], t["k_eye"]).then_inc(small_in, 16)
                pool.dma_start(norm_w[:], t["norm_w"][0].rearrange("(k p) -> p k", p=P)).then_inc(small_in, 16)
                pool.dma_start(ada_b_col[:], t["ada_b"][0, 0:2 * D].rearrange("(k p) -> p k", p=P)).then_inc(small_in, 16)
                pool.dma_start(ada_b_gate[:], t["ada_b"][0, 2 * D:3 * D].partition_broadcast(P)).then_inc(small_in, 16)
            step = chained(pool, pool_step)
            step(pool.memset(halves[:], -0.5))
            for g in range(5):
                a = slice(4 * g, 4 * g + tiles[g])
                pool.wait_ge(sq_done, 4 * g + tiles[g])
                step(pool.tensor_scalar(rstd[:, a], ss[:, a], 1.0 / D, EPS, ALU.mult, ALU.add))
                pool.tensor_tensor(rstd[:, a], rstd[:, a], halves[:, a], ALU.pow).then_inc(rstd_done, 1)

        @block.scalar
        def _(act):
            def squares_of(g):
                act.wait_ge(x_in[g % 2], 16 * (g // 2 + 1))
                for a in range(tiles[g]):
                    n = 4 * g + a
                    act.activation(squares[:], xg[:, g % 2, a], ACT.Square, accum_out=ss[:, n:n + 1]).then_inc(sq_done, 1)
                    act.wait_ge(sq_done, n + 1)

            def sines(layer):
                act.wait_ge(net_ang, layer + 1)
                act.activation(hT[:, 0:SEQ], ang[:], ACT.Sin).then_inc(sin_done, 1)

            def modulate(g):
                r = 0 if g < 4 else 1
                for k in range(KT):
                    w = P * tiles[g]
                    act.wait_ge(tr_done, KT * g + k + 1)
                    act.activation(xnT[:, k, g * BANK:g * BANK + w], tr[:, k % 2, 0:w], ACT.Identity,
                                   bias=mod[:, 0, r, k:k + 1], scale=mod[:, 1, r, k:k + 1]).then_inc(tr_used, 1)

            act.wait_ge(c_in, 32)
            act.activation(s_col[:], c_col[:], ACT.Silu).then_inc(silu_done, 1)
            sines(0)
            squares_of(0)
            squares_of(1)
            sines(1)
            act.wait_ge(mod_ready, 1)
            modulate(0)
            squares_of(2)
            modulate(1)
            squares_of(3)
            sines(2)
            modulate(2)
            squares_of(4)
            modulate(3)
            modulate(4)

        @block.tensor
        def _(pe):
            def net(layer):
                w = w1[:] if layer == 0 else w23[:, layer - 1]
                if layer:
                    pe.wait_ge(sin_done, layer)
                for c in range(4):
                    n = 4 * layer + c
                    if n >= 2:
                        pe.wait_ge(net_out, n - 1)
                    src = feats if layer == 0 else hT
                    pe.matmul(net_ps[:, n % 2], w, src[:, c * BANK:(c + 1) * BANK], start=True, stop=True).then_inc(net_mm, 1)

            def transposes(g):
                pe.wait_ge(x_scaled, g + 1)
                for k in range(KT):
                    n = KT * g + k
                    if n >= 2:
                        pe.wait_ge(tr_used, n - 1)
                    for a in range(tiles[g]):
                        ins = pe.transpose(tr[:, n % 2, a * P:(a + 1) * P], xg[:, g % 2, a, k * P:(k + 1) * P], eye[:])
                    ins.then_inc(tr_done, 1)

            pe.wait_ge(net_in, 16 * 8)
            net(0)
            pe.wait_ge(wide_done, 1)
            for k in range(KT):
                pe.wait_ge(ada_in[k % RING], 16 * (k // RING + 1))
                for m in range(2 * KT):
                    pe.matmul(mod_ps[:, m], ada[:, k % RING, m * P:(m + 1) * P], s_col[:, k],
                              start=(k == 0 and m == 0), stop=(k == KT - 1 and m == 2 * KT - 1), skip_group_check=True)
                for h in range(2):
                    ins = pe.matmul(gate_ps[:, h * BANK:(h + 1) * BANK], s_wide[:, k],
                                    ada[:, k % RING, 2 * D + h * BANK:2 * D + (h + 1) * BANK], start=(k == 0), stop=(k == KT - 1))
                ins.then_inc(ada_used, 1)
            net(1)
            pe.wait_ge(small_in, 64)
            transposes(0)
            transposes(1)
            net(2)
            for g in range(2, 5):
                transposes(g)

        @block.vector
        def _(dve):
            step = chained(dve, v_step)

            def angles(layer):
                for c in range(4):
                    n = 4 * layer + c
                    dve.wait_ge(net_mm, n + 1)
                    dve.tensor_scalar(ang[:, c * BANK:(c + 1) * BANK], net_ps[:, n % 2], fb[:, layer:layer + 1], freq[:, 0:1],
                                      ALU.add, ALU.mult).then_inc(net_out, 1)
                dve.wait_ge(net_out, 4 * layer + 4)
                step(dve.tensor_scalar(turns[:], ang[:], 1.0 / TWO_PI, ROUNDER, ALU.mult, ALU.add))
                step(dve.tensor_scalar(turns[:], turns[:], -ROUNDER, None, ALU.add))
                for part in (PI_A, PI_B, PI_C):
                    step(dve.scalar_tensor_tensor(ang[:], turns[:], -part, ang[:], ALU.mult, ALU.add))
                dve.tensor_scalar(ang[:], ang[:], PI, -PI, ALU.min, ALU.max).then_inc(net_ang, 1)

            def scale_tokens(g):
                dve.wait_ge(rstd_done, g + 1)
                for a in range(tiles[g]):
                    n = 4 * g + a
                    ins = dve.tensor_scalar(xg[:, g % 2, a], xg[:, g % 2, a], rstd[:, n:n + 1], None, ALU.mult)
                ins.then_inc(x_scaled, 1)

            dve.memset(hT[:, SEQ:SEQ + 1], 0.0)
            dve.wait_ge(silu_done, 1)
            dve.tensor_copy(s_wide[:], s_col[:, :, 0:1].to_broadcast([P, KT, P])).then_inc(wide_done, 1)
            dve.wait_ge(net_in, 16 * 8)
            angles(0)
            dve.wait_ge(ada_used, KT)
            dve.wait_ge(small_in, 64)
            for r in range(2):
                step(dve.tensor_tensor(mod[:, 0, r], mod_ps[:, 0:KT, r], ada_b_col[:, 0:KT], ALU.add))
                step(dve.tensor_tensor(mod[:, 1, r], mod_ps[:, KT:2 * KT, r], ada_b_col[:, KT:2 * KT], ALU.add))
                step(dve.scalar_tensor_tensor(mod[:, 1, r], mod[:, 1, r], 1.0, norm_w[:], ALU.add, ALU.mult))
            dve.tensor_tensor(gate_row[:], gate_ps[:], ada_b_gate[:], ALU.add).then_inc(mod_ready, 1)
            angles(1)
            scale_tokens(0)
            scale_tokens(1)
            angles(2)
            for g in range(2, 5):
                scale_tokens(g)


def filter_first_stage(nc, t, keep):
    with ExitStack() as ph:
        def sem(name):
            return nc.alloc_semaphore(name)

        def sb(name, shape, dt=F32):
            return ph.enter_context(nc.sbuf_tensor("f_" + name, shape, dt))

        def psum(name, shape):
            return ph.enter_context(nc.psum_tensor("f_" + name, shape, F32))

        hT = keep["hT"]
        w4 = sb("w4", [FW, 2, D])
        fwd = sb("fwd", [P, 2, 2, P])
        deltas = sb("deltas", [P, D])
        mt = sb("mt", [P, RIN, 2])
        mt_now = sb("mt_now", [P, 2])
        h_now = sb("h_now", [FW, 2, P])
        window = sb("window", [P, 2, 2, BANK])
        taps = sb("taps", [P, 2, 2, BANK])
        out = sb("out", [P, 2, 2, BANK])
        h_ps = psum("h_ps", [P, 2, 2, BANK])
        f_ps = psum("f_ps", [P, 2, 2, BANK])
        w_in_, net_now, mt_done, h_mm, win_done, taps_done, f_mm = (
            sem(n) for n in ("f_consts", "f_net_now", "f_mt_done", "f_h_mm", "f_win_done", "f_taps_done", "f_mm"))
        out_re, out_im = sem("f_out_re"), sem("f_out_im")
        stored = [sem(f"f_stored{h}") for h in range(2)]
        block = ph.enter_context(nc.Block())

        @block.sync
        def _(sp):
            sp.dma_start(w4[:], t["filt_w4"][0].rearrange("p (s d) -> p s d", s=2)).then_inc(w_in_, 16)
            sp.dma_start(fwd[:], t["k_fwd"]).then_inc(w_in_, 16)
            sp.dma_start(deltas[:], t["k_deltas"][0].partition_broadcast(P)).then_inc(w_in_, 16)
            sp.dma_start(mt[:], t["k_mt"]).then_inc(w_in_, 16)
            lead(sp, *stored, unit=16)
            with sp.Fori(0, RIN) as n2:
                for h in range(2):
                    sp.wait_ge(out_re, nth(2 * n2 + h))
                    sp.wait_ge(out_im, nth(2 * n2 + h))
                    sp.dma_start(t["f_spec"][n2][:, :, h * BANK:(h + 1) * BANK].rearrange("r k c -> k r c"),
                                 out[:, h]).then_inc(stored[h], 16)
            for h in range(2):
                sp.wait_ge(stored[h], nth(RIN - 1, 16))

        @block.tensor
        def _(pe):
            lead(pe, h_mm, f_mm)
            pe.wait_ge(w_in_, 64)
            with pe.Fori(0, RIN) as n2:
                pe.wait_ge(net_now, n2 + 1)
                for h in range(2):
                    for s in range(2):
                        ins = pe.matmul(h_ps[:, h, s], h_now[:, s], w4[:, s, h * BANK:(h + 1) * BANK], start=True, stop=True)
                    ins.then_inc(h_mm, 1)
                for h in range(2):
                    n = 2 * n2 + h
                    pe.wait_ge(taps_done, nth(n))
                    pe.wait_ge(out_re, nth(n - 2))
                    pe.wait_ge(out_im, nth(n - 2))
                    for r in range(2):
                        for s in range(2):
                            ins = pe.matmul(f_ps[:, h, r], fwd[:, s, r], taps[:, h, s], start=(s == 0), stop=(s == 1))
                    ins.then_inc(f_mm, 1)

        @block.scalar
        def _(act):
            lead(act, win_done, out_re)
            act.wait_ge(w_in_, 64)
            with act.Fori(0, RIN) as n2:
                act.wait_ge(mt_done, n2 + 1)
                for h in range(2):
                    act.wait_ge(taps_done, nth(2 * n2 + h - 2))
                    for s in range(2):
                        ins = act.activation(window[:, h, s], deltas[:, h * BANK:(h + 1) * BANK], ACT.Exp, scale=mt_now[:, s:s + 1])
                    ins.then_inc(win_done, 1)
                for h in range(2):
                    n = 2 * n2 + h
                    act.wait_ge(f_mm, nth(n))
                    act.wait_ge(stored[h], nth(n2 - 1, 16))
                    act.activation(out[:, h, 0], f_ps[:, h, 0], ACT.Copy).then_inc(out_re, 1)

        @block.vector
        def _(dve):
            lead(dve, taps_done, out_im)
            dve.wait_ge(w_in_, 64)
            with dve.Fori(0, RIN) as n2:
                dve.wait_ge(h_mm, nth(2 * n2 - 1))
                dve.tensor_copy(h_now[:, 0], hT[:, bass.ds(n2, P, step=RIN)])
                dve.tensor_copy(h_now[:, 1], hT[:, bass.ds(RIN - n2, P, step=RIN)]).then_inc(net_now, 1)
                dve.wait_ge(win_done, nth(2 * n2 - 1))
                dve.tensor_copy(mt_now[:], mt[:, bass.ds(n2, 1)].rearrange("p a s -> p (a s)")).then_inc(mt_done, 1)
                for h in range(2):
                    n = 2 * n2 + h
                    dve.wait_ge(h_mm, nth(n))
                    dve.wait_ge(win_done, nth(n))
                    dve.wait_ge(f_mm, nth(n - 2))
                    for s in range(2):
                        ins = dve.tensor_tensor(taps[:, h, s], h_ps[:, h, s], window[:, h, s], ALU.mult)
                    ins.then_inc(taps_done, 1)
                for h in range(2):
                    n = 2 * n2 + h
                    dve.wait_ge(f_mm, nth(n))
                    dve.wait_ge(stored[h], nth(n2 - 1, 16))
                    dve.tensor_copy(out[:, h, 1], f_ps[:, h, 1]).then_inc(out_im, 1)
def conv_taps(dve, step, tile, ps, taps, rows, width):
    a = tile.rearrange("p (r w) -> p r w", w=width)
    b = ps.rearrange("p (r w) -> p r w", w=width)
    step(dve.scalar_tensor_tensor(a[:, :, 1:width], b[:, :, 0:width - 1], taps[:, 0:1], a[:, :, 1:width], ALU.mult, ALU.add))
    return dve.scalar_tensor_tensor(a[:, :, 0:width - 1], b[:, :, 1:width], taps[:, 2:3], a[:, :, 0:width - 1], ALU.mult, ALU.add)


def project_hyena(nc, t, keep):
    with ExitStack() as ph:
        def sem(name):
            return nc.alloc_semaphore(name)

        def sb(name, shape, dt=F32):
            return ph.enter_context(nc.sbuf_tensor("h_" + name, shape, dt))

        def psum(name, shape):
            return ph.enter_context(nc.psum_tensor("h_" + name, shape, F32))

        xnT, eye = keep["xnT"], keep["eye"]
        HY_T = D // P
        KINDS = (COL_HY + D, COL_HY + 2 * D, COL_HY, COL_ZH)
        CONV_AT = (1, 2, 0)
        w = sb("w", [P, 4, KT, P])
        taps = sb("taps", [P, 3, HY_T, 4])
        taps_now = sb("taps_now", [P, 3, 4])
        fwd = sb("fwd", [P, 2, P])
        part = sb("part", [P, 4, SEQ])
        vv = sb("vv", [P, SEQ])
        gate = sb("gate", [P, SEQ])
        u = sb("u", [P, RIN, P])
        spec = sb("spec", [P, 2, RIN, P])
        pj = psum("pj", [P, 4, BANK])
        tr = psum("tr", [P, 2, BANK])
        st = psum("st", [P, 2, BANK])
        w_in_ = [sem(f"h_w_in{j}") for j in range(4)]
        consts, taps_ready, pj_mm, cv_mid, cv_side, cv_done, z_done, vv_done, gate_done = (sem("h_" + n) for n in (
            "consts", "taps_ready", "pj_mm", "cv_mid", "cv_side", "cv_done", "z_done", "vv_done", "gate_done"))
        tr_mm, u_done, st_mm, re_done, im_done, vv_out, gate_out, spec_out = (sem("h_" + n) for n in (
            "tr_mm", "u_done", "st_mm", "re_done", "im_done", "vv_out", "gate_out", "spec_out"))
        w_cols = t["w_in"][0].rearrange("(k p) n -> p k n", p=P)
        block = ph.enter_context(nc.Block())

        @block.gpsimd
        def _(pool):
            with pool.Fori(0, HY_T) as c:
                for j in range(4):
                    pool.wait_ge(pj_mm, nth(16 * (c - 1) + 4 * j + 3))
                    pool.dma_start(w[:, j], w_cols[:, :, bass.ds(KINDS[j] + c * P, P)]).then_inc(w_in_[j], 16)

        @block.sync
        def _(sp):
            with nc.allow_non_contiguous_dma(reason="taps by channel"):
                for a in range(3):
                    cols = slice(a * D, (a + 1) * D)
                    for k in range(3):
                        sp.dma_start(taps[:, a, :, k], t["hy_conv_w"][0, k, cols].rearrange("(m p) -> p m", p=P)).then_inc(consts, 16)
                    sp.dma_start(taps[:, a, :, 3], t["hy_conv_b"][0, cols].rearrange("(m p) -> p m", p=P)).then_inc(consts, 16)
                sp.dma_start(fwd[:], t["k_fwd"][:, 0]).then_inc(consts, 16)
            lead(sp, vv_out, gate_out, unit=16)
            lead(sp, spec_out, unit=32)
            with sp.Fori(0, HY_T) as c:
                sp.wait_ge(vv_done, nth(c))
                sp.dma_start(t["vv_t"][c], vv[:]).then_inc(vv_out, 16)
                sp.wait_ge(gate_done, nth(c))
                sp.dma_start(t["gate_t"][c], gate[:]).then_inc(gate_out, 16)
                sp.wait_ge(re_done, nth(4 * c + 3))
                sp.wait_ge(im_done, nth(4 * c + 3))
                for r in range(2):
                    sp.dma_start(t["u_spec"][:, r, :, bass.ds(c * P, P)].rearrange("n k c -> k n c"), spec[:, r]).then_inc(spec_out, 16)
            sp.wait_ge(vv_out, nth(HY_T - 1, 16))
            sp.wait_ge(gate_out, nth(HY_T - 1, 16))
            sp.wait_ge(spec_out, nth(HY_T - 1, 32))

        @block.tensor
        def _(pe):
            lead(pe, pj_mm, tr_mm, st_mm)
            pe.wait_ge(consts, 16 * 13)
            with pe.Fori(0, HY_T) as c:
                for j in range(4):
                    pe.wait_ge(w_in_[j], 16 * c + 16)
                    for q in range(4):
                        if j == 0:
                            pe.wait_ge(z_done, nth(4 * (c - 1) + q))
                        else:
                            pe.wait_ge(cv_done, nth(12 * c + 4 * (j - 1) + q))
                        for k in range(KT):
                            ins = pe.matmul(pj[:, q], w[:, j, k], xnT[:, k, q * BANK:(q + 1) * BANK], start=(k == 0), stop=(k == KT - 1))
                        ins.then_inc(pj_mm, 1)
                    if j == 2:
                        pe.wait_ge(vv_done, nth(c))
                        for n in range(4):
                            pe.wait_ge(u_done, nth(4 * c + n - 2))
                            for a in range(4):
                                ins = pe.transpose(tr[:, n % 2, a * P:(a + 1) * P], vv[:, 4 * n + a::RIN], eye[:])
                            ins.then_inc(tr_mm, 1)
                for n in range(4):
                    pe.wait_ge(u_done, nth(4 * c + n))
                    pe.wait_ge(re_done, nth(4 * c + n - 1))
                    pe.wait_ge(im_done, nth(4 * c + n - 1))
                    for r in range(2):
                        ins = pe.matmul(st[:, r], fwd[:, r], u[:, 4 * n:4 * n + 4].rearrange("p a c -> p (a c)"), start=True, stop=True)
                    ins.then_inc(st_mm, 1)

        @block.scalar
        def _(act):
            lead(act, z_done, u_done, re_done, cv_mid)
            act.wait_ge(consts, 16 * 13)
            with act.Fori(0, HY_T) as c:
                act.wait_ge(taps_ready, c + 1)
                for j in range(4):
                    if j in (0, 1):
                        act.wait_ge(vv_done, nth(c - 1))
                    else:
                        act.wait_ge(gate_done, nth(c - 1))
                    for q in range(4):
                        act.wait_ge(pj_mm, nth(16 * c + 4 * j + q))
                        cols = part[:, j, q * BANK:(q + 1) * BANK]
                        if j == 3:
                            act.activation(cols, pj[:, q], ACT.Silu).then_inc(z_done, 1)
                        else:
                            act.activation(cols, pj[:, q], ACT.Identity, bias=taps_now[:, j, 3:4], scale=taps_now[:, j, 1:2]).then_inc(cv_mid, 1)
                    if j == 2:
                        act.wait_ge(st_mm, nth(4 * (c - 1) + 3))
                        for n in range(4):
                            act.wait_ge(tr_mm, nth(4 * c + n))
                            act.activation(u[:, 4 * n:4 * n + 4].rearrange("p a c -> p (a c)"), tr[:, n % 2], ACT.Copy).then_inc(u_done, 1)
                act.wait_ge(spec_out, nth(c - 1, 32))
                for n in range(4):
                    act.wait_ge(st_mm, nth(4 * c + n))
                    act.activation(spec[:, 0, 4 * n:4 * n + 4].rearrange("p a c -> p (a c)"), st[:, 0], ACT.Copy).then_inc(re_done, 1)

        @block.vector
        def _(dve):
            lead(dve, cv_done, im_done, vv_done, gate_done)
            dve.wait_ge(consts, 16 * 13)
            with dve.Fori(0, HY_T) as c:
                dve.wait_ge(cv_mid, nth(12 * c - 1))
                dve.wait_ge(cv_done, nth(12 * c - 1))
                for j in range(3):
                    ins = dve.tensor_copy(taps_now[:, j], taps[:, CONV_AT[j], bass.ds(c, 1)].rearrange("p a k -> p (a k)"))
                ins.then_inc(taps_ready, 1)
                step = chained(dve, cv_side, 12 * c)
                dve.wait_ge(taps_ready, c + 1)
                for j in range(3):
                    for q in range(4):
                        n = 12 * c + 4 * j + q
                        dve.wait_ge(cv_mid, nth(n))
                        conv_taps(dve, step, part[:, j, q * BANK:(q + 1) * BANK], pj[:, q], taps_now[:, j], BANK // GRID_W, GRID_W).then_inc(cv_done, 1)
                    if j == 1:
                        dve.wait_ge(cv_done, nth(12 * c + 7))
                        dve.wait_ge(tr_mm, nth(4 * (c - 1) + 3))
                        dve.wait_ge(vv_out, nth(c - 1, 16))
                        dve.tensor_tensor(vv[:], part[:, 0], part[:, 1], ALU.mult).then_inc(vv_done, 1)
                dve.wait_ge(cv_done, nth(12 * c + 11))
                dve.wait_ge(z_done, nth(4 * c + 3))
                dve.wait_ge(gate_out, nth(c - 1, 16))
                dve.tensor_tensor(gate[:], part[:, 2], part[:, 3], ALU.mult).then_inc(gate_done, 1)
                dve.wait_ge(spec_out, nth(c - 1, 32))
                for n in range(4):
                    dve.wait_ge(st_mm, nth(4 * c + n))
                    dve.tensor_copy(spec[:, 1, 4 * n:4 * n + 4].rearrange("p a c -> p (a c)"), st[:, 1]).then_inc(im_done, 1)


def project_ssd(nc, t, keep):
    project_xbc(nc, t, keep, "s", 0, D // P, True)
    project_xbc(nc, t, keep, "b", D // P, XBC_T - D // P, False)


def project_xbc(nc, t, keep, pre, first, tiles, with_z):
    with ExitStack() as ph:
        def sem(name):
            return nc.alloc_semaphore(name)

        def sb(name, shape, dt=F32):
            return ph.enter_context(nc.sbuf_tensor(f"{pre}_{name}", shape, dt))

        def psum(name, shape):
            return ph.enter_context(nc.psum_tensor(f"{pre}_{name}", shape, F32))

        xnT, eye, dt_raw = keep["xnT"], keep["eye"], keep["dt_raw"]
        MM = 9 if with_z else 5
        QUADS = (NCH + 3) // 4
        w = sb("w", [P, 2, 2, KT, P])
        taps = sb("taps", [P, tiles, 4])
        taps_now = sb("taps_now", [P, 4])
        conv = sb("conv", [P, TOK])
        xt = sb("xt", [P, TOK])
        zt = sb("zt", [P, SEQ])
        xk = sb("xk", [P, NCH, P])
        w_dt = sb("w_dt", [P, KT, 2 * HEADS])
        dtT = sb("dtT", [2 * HEADS, TOK])
        pj = psum("pj", [P, 4, BANK])
        pc = psum("pc", [P, BANK])
        tr = psum("tr", [P, 2, BANK])
        w_in_ = sem(pre + "_w_in")
        z_in = sem(pre + "_z_in")
        consts, taps_ready, mm, cv_mid, cv_side, cv_done, x_done, z_done = (sem(f"{pre}_{n}") for n in (
            "consts", "taps_ready", "mm", "cv_mid", "cv_side", "cv_done", "x_done", "z_done"))
        tr_mm, xk_done, xt_out, xk_out, z_out, dt_done, dt_tr, dt_copied = (sem(f"{pre}_{n}") for n in (
            "tr_mm", "xk_done", "xt_out", "xk_out", "z_out", "dt_done", "dt_tr", "dt_copied"))
        w_cols = t["w_in"][0].rearrange("(k p) n -> p k n", p=P)
        block = ph.enter_context(nc.Block())
        chunks = [(q, q * BANK, BANK) for q in range(4)] + [(4, SEQ, CTX)]

        def bank(q):
            return pj[:, q] if q < 4 else pc[:, 0:CTX]

        @block.gpsimd
        def _(pool):
            with pool.Fori(0, tiles) as c:
                pool.wait_ge(mm, nth(MM * (c - 1) + 4))
                pool.dma_start(w[:, 0, 0], w_cols[:, :, bass.ds(COL_XBC + (first + c) * P, P)]).then_inc(w_in_, 16)
                if with_z:
                    pool.wait_ge(mm, nth(MM * (c - 1) + 8))
                    pool.dma_start(w[:, 0, 1], w_cols[:, :, bass.ds(COL_ZS + c * P, P)]).then_inc(z_in, 16)

        @block.sync
        def _(sp):
            with nc.allow_non_contiguous_dma(reason="taps by channel"):
                cols = slice(first * P, (first + tiles) * P)
                for k in range(3):
                    sp.dma_start(taps[:, :, k], t["ssd_conv_w"][0, k, cols].rearrange("(m p) -> p m", p=P)).then_inc(consts, 16)
                sp.dma_start(taps[:, :, 3], t["ssd_conv_b"][0, cols].rearrange("(m p) -> p m", p=P)).then_inc(consts, 16)
                sp.dma_start(w_dt[:], w_cols[:, :, COL_DT:COL_DT + 2 * HEADS]).then_inc(consts, 16)
            lead(sp, xt_out, xk_out, z_out, unit=16)
            with sp.Fori(0, tiles) as c:
                sp.wait_ge(x_done, nth(c))
                sp.dma_start(t["xbc_t"][first + c], xt[:]).then_inc(xt_out, 16)
                if with_z:
                    sp.wait_ge(z_done, nth(4 * c + 3))
                    sp.dma_start(t["zs_t"][c], zt[:]).then_inc(z_out, 16)
                sp.wait_ge(xk_done, nth(QUADS * c + QUADS - 1))
                sp.dma_start(t["xbc"][:, :, bass.ds((first + c) * P, P)].rearrange("n p c -> p n c"), xk[:]).then_inc(xk_out, 16)
            sp.wait_ge(xt_out, nth(tiles - 1, 16))
            sp.wait_ge(xk_out, nth(tiles - 1, 16))
            if with_z:
                sp.wait_ge(z_out, nth(tiles - 1, 16))

        @block.tensor
        def _(pe):
            lead(pe, mm, tr_mm)
            pe.wait_ge(consts, 16 * 5)
            with pe.Fori(0, tiles) as c:
                pe.wait_ge(w_in_, 16 * c + 16)
                for q, at, width in chunks:
                    if q < 4 and with_z:
                        pe.wait_ge(z_done, nth(4 * (c - 1) + q))
                    else:
                        pe.wait_ge(cv_done, nth(5 * (c - 1) + q))
                    for k in range(KT):
                        ins = pe.matmul(bank(q), w[:, 0, 0, k], xnT[:, k, at:at + width], start=(k == 0), stop=(k == KT - 1))
                    ins.then_inc(mm, 1)
                if with_z:
                    pe.wait_ge(z_in, 16 * c + 16)
                    for q in range(4):
                        pe.wait_ge(cv_done, nth(5 * c + q))
                        for k in range(KT):
                            ins = pe.matmul(pj[:, q], w[:, 0, 1, k], xnT[:, k, q * BANK:(q + 1) * BANK], start=(k == 0), stop=(k == KT - 1))
                        ins.then_inc(mm, 1)
                pe.wait_ge(x_done, nth(c))
                for n in range(QUADS):
                    pe.wait_ge(xk_done, nth(QUADS * c + n - 2))
                    for a in range(min(4, NCH - 4 * n)):
                        m = 4 * n + a
                        ins = pe.transpose(tr[:, n % 2, a * P:(a + 1) * P], xt[:, m * P:(m + 1) * P], eye[:])
                    ins.then_inc(tr_mm, 1)
            if not with_z:
                for q, at, width in chunks:
                    pe.wait_ge(cv_done, nth(5 * tiles - 5 + q))
                    for k in range(KT):
                        ins = pe.matmul(bank(q)[0:2 * HEADS], w_dt[:, k], xnT[:, k, at:at + width], start=(k == 0), stop=(k == KT - 1))
                    ins.then_inc(mm, 1)
                pe.wait_ge(dt_done, 5)
                pe.wait_ge(xk_done, nth(QUADS * tiles - 1))
                for n in range(NCH):
                    ins = pe.transpose(tr[:, n // 16, 32 * (n % 16):32 * (n % 16) + 32], dtT[:, n * P:(n + 1) * P], eye[0:32, 0:32])
                ins.then_inc(dt_tr, 1)

        @block.scalar
        def _(act):
            lead(act, z_done, x_done, cv_mid)
            act.wait_ge(consts, 16 * 5)
            with act.Fori(0, tiles) as c:
                act.wait_ge(taps_ready, c + 1)
                act.wait_ge(x_done, nth(c - 1))
                for q, at, width in chunks:
                    act.wait_ge(mm, nth(MM * c + q))
                    act.activation(conv[:, at:at + width], bank(q), ACT.Identity, bias=taps_now[:, 3:4], scale=taps_now[:, 1:2]).then_inc(cv_mid, 1)
                act.wait_ge(cv_done, nth(5 * c + 4))
                act.wait_ge(tr_mm, nth(QUADS * c - 1))
                act.wait_ge(xt_out, nth(c - 1, 16))
                act.activation(xt[:], conv[:], ACT.Silu).then_inc(x_done, 1)
                if with_z:
                    act.wait_ge(z_out, nth(c - 1, 16))
                    for q in range(4):
                        act.wait_ge(mm, nth(MM * c + 5 + q))
                        act.activation(zt[:, q * BANK:(q + 1) * BANK], pj[:, q], ACT.Silu).then_inc(z_done, 1)
            if not with_z:
                for q, at, width in chunks:
                    act.wait_ge(mm, nth(MM * tiles + q))
                    act.activation(dtT[:, at:at + width], bank(q)[0:2 * HEADS], ACT.Copy).then_inc(dt_done, 1)

        @block.vector
        def _(dve):
            lead(dve, cv_done, xk_done)
            dve.wait_ge(consts, 16 * 5)
            with dve.Fori(0, tiles) as c:
                dve.wait_ge(cv_mid, nth(5 * c - 1))
                dve.tensor_copy(taps_now[:], taps[:, bass.ds(c, 1)].rearrange("p a k -> p (a k)")).then_inc(taps_ready, 1)
                dve.wait_ge(taps_ready, c + 1)
                step = chained(dve, cv_side, 5 * c)
                for q, at, width in chunks:
                    dve.wait_ge(cv_mid, nth(5 * c + q))
                    row = GRID_W if q < 4 else CTX
                    conv_taps(dve, step, conv[:, at:at + width], bank(q), taps_now, width // row, row).then_inc(cv_done, 1)
                dve.wait_ge(xk_out, nth(c - 1, 16))
                for n in range(QUADS):
                    m = min(4, NCH - 4 * n)
                    dve.wait_ge(tr_mm, nth(QUADS * c + n))
                    dve.tensor_copy(xk[:, 4 * n:4 * n + m].rearrange("p a c -> p (a c)"), tr[:, n % 2, 0:m * P]).then_inc(xk_done, 1)
            if not with_z:
                dve.wait_ge(dt_tr, 1)
                dve.tensor_copy(dt_raw[:].rearrange("p n h -> p (n h)")[:, 0:BANK], tr[:, 0])
                dve.tensor_copy(dt_raw[:].rearrange("p n h -> p (n h)")[:, BANK:32 * NCH], tr[:, 1, 0:32 * NCH - BANK]).then_inc(dt_copied, 1)
                dve.wait_ge(dt_copied, 1)
def spectra(nc, t, keep):
    with ExitStack() as ph:
        def sem(name):
            return nc.alloc_semaphore(name)

        def sb(name, shape, dt=F32):
            return ph.enter_context(nc.sbuf_tensor("g_" + name, shape, dt))

        def psum(name, shape):
            return ph.enter_context(nc.psum_tensor("g_" + name, shape, F32))

        SLOTS = 2
        sig = sb("sig", [P, SLOTS, D])
        fil = sb("fil", [P, SLOTS, D])
        mats = sb("mats", [P, SLOTS, 5, P])
        ab = sb("ab", [P, 2, 2, BANK])
        prod = sb("prod", [P, 2, 2, BANK])
        back = sb("back", [P, SLOTS, 2, BANK])
        xab = psum("xab", [P, 2, 3, BANK])
        v_ps = psum("v_ps", [P, 2, BANK])
        loaded = [sem(f"g_loaded{s}") for s in range(SLOTS)]
        stored = [sem(f"g_stored{s}") for s in range(SLOTS)]
        x_mm, ab_done, prod_done, v_mm, v_done = (sem("g_" + n) for n in ("x_mm", "ab_done", "prod_done", "v_mm", "v_done"))
        block = ph.enter_context(nc.Block())

        def rows(name, g, r):
            return t[name][:, r, bass.ds(g * FG, FG), :].rearrange("n k c -> k n c")

        @block.gpsimd
        def _(pool):
            with pool.Fori(0, NG // SLOTS) as i:
                for s in range(SLOTS):
                    g = SLOTS * i + s
                    pool.wait_ge(v_mm, nth(2 * (g - SLOTS) + 1))
                    for r in range(2):
                        pool.dma_start(sig[64 * r:64 * r + 64, s], rows("u_spec", g, r)).then_inc(loaded[s], 16)
                        pool.dma_start(fil[64 * r:64 * r + 64, s], rows("f_spec", g, r)).then_inc(loaded[s], 16)
                    pool.dma_start(mats[:, s], t["k_mats"][g]).then_inc(loaded[s], 16)

        @block.sync
        def _(sp):
            lead(sp, *stored, unit=32)
            with sp.Fori(0, NG // SLOTS) as i:
                for s in range(SLOTS):
                    g = SLOTS * i + s
                    sp.wait_ge(v_done, nth(2 * g + 1))
                    for r in range(2):
                        sp.dma_start(rows("v_spec", g, r), back[64 * r:64 * r + 64, s].rearrange("p h c -> p (h c)")).then_inc(stored[s], 32 // 2)
            for s in range(SLOTS):
                sp.wait_ge(stored[s], nth(NG // SLOTS - 1, 32))

        @block.tensor
        def _(pe):
            lead(pe, x_mm, v_mm)

            def forward(g, s, h):
                cols = slice(h * BANK, (h + 1) * BANK)
                pe.matmul(xab[:, h, 0], mats[:, s, 0], sig[:, s, cols], start=True, stop=True)
                for m in (1, 2):
                    ins = pe.matmul(xab[:, h, m], mats[:, s, m], fil[:, s, cols], start=True, stop=True)
                ins.then_inc(x_mm, 1)

            def backward(g, s, h):
                n = 2 * g + h
                pe.wait_ge(prod_done, nth(n))
                pe.wait_ge(v_done, nth(n - 2))
                for m in range(2):
                    ins = pe.matmul(v_ps[:, h], mats[:, s, 3 + m], prod[:, h, m], start=(m == 0), stop=(m == 1))
                ins.then_inc(v_mm, 1)

            with pe.Fori(0, NG // SLOTS) as i:
                g = SLOTS * i
                pe.wait_ge(loaded[0], 80 * i + 80)
                forward(g, 0, 0)
                forward(g, 0, 1)
                backward(g, 0, 0)
                pe.wait_ge(loaded[1], 80 * i + 80)
                forward(g + 1, 1, 0)
                backward(g, 0, 1)
                forward(g + 1, 1, 1)
                backward(g + 1, 1, 0)
                backward(g + 1, 1, 1)

        @block.scalar
        def _(act):
            lead(act, ab_done, v_done)

            def filter_parts(n, h):
                act.wait_ge(x_mm, nth(n))
                act.wait_ge(prod_done, nth(n - 2))
                act.activation(ab[:, h], xab[:, h, 1:3], ACT.Copy).then_inc(ab_done, 1)

            def keep_back(n, i, s, h):
                act.wait_ge(v_mm, nth(n))
                act.wait_ge(stored[s], nth(i - 1, 32))
                act.activation(back[:, s, h], v_ps[:, h], ACT.Copy).then_inc(v_done, 1)

            with act.Fori(0, NG // SLOTS) as i:
                n = 2 * SLOTS * i
                filter_parts(n, 0)
                filter_parts(n + 1, 1)
                filter_parts(n + 2, 0)
                keep_back(n, i, 0, 0)
                filter_parts(n + 3, 1)
                keep_back(n + 1, i, 0, 1)
                keep_back(n + 2, i, 1, 0)
                keep_back(n + 3, i, 1, 1)

        @block.vector
        def _(dve):
            lead(dve, prod_done)
            with dve.Fori(0, NG // SLOTS) as i:
                for s in range(SLOTS):
                    for h in range(2):
                        n = 2 * SLOTS * i + 2 * s + h
                        dve.wait_ge(ab_done, nth(n))
                        dve.wait_ge(v_mm, nth(n - 2))
                        dve.tensor_tensor(prod[:, h, 0], xab[:, h, 0], ab[:, h, 0], ALU.mult)
                        dve.tensor_tensor(prod[:, h, 1], xab[:, h, 0], ab[:, h, 1], ALU.mult).then_inc(prod_done, 1)


def hyena_back(nc, t, keep):
    with ExitStack() as ph:
        def sem(name):
            return nc.alloc_semaphore(name)

        def sb(name, shape, dt=F32):
            return ph.enter_context(nc.sbuf_tensor("c_" + name, shape, dt))

        def psum(name, shape):
            return ph.enter_context(nc.psum_tensor("c_" + name, shape, F32))

        ssh = keep["ssh"]
        CT, SLOTS = D // P, 2
        back = sb("back", [P, 2, P])
        skip = sb("skip", [P, CT])
        skip_now = sb("skip_now", [P, SLOTS])
        z = sb("z", [P, SLOTS, 2, RIN, P])
        vv = sb("vv", [P, SLOTS, SEQ])
        gate = sb("gate", [P, SLOTS, SEQ])
        y = sb("y", [P, SLOTS, SEQ])
        sq = sb("sq", [P, SEQ])
        ones = sb("ones", [P, 1])
        y_ps = psum("y_ps", [P, 4, BANK])
        s_ps = psum("s_ps", [P, BANK])
        loaded = [sem(f"c_loaded{s}") for s in range(SLOTS)]
        stored = [sem(f"c_stored{s}") for s in range(SLOTS)]
        consts, y_mm, y_sum, y_done, sq_done, s_mm, s_done, skip_done, ones_done = (sem("c_" + n) for n in (
            "consts", "y_mm", "y_sum", "y_done", "sq_done", "s_mm", "s_done", "skip_done", "ones_done"))
        block = ph.enter_context(nc.Block())

        @block.gpsimd
        def _(pool):
            with pool.Fori(0, CT // SLOTS) as i:
                for s in range(SLOTS):
                    c = SLOTS * i + s
                    pool.wait_ge(y_done, nth(c - SLOTS))
                    for r in range(2):
                        pool.dma_start(z[:, s, r], t["v_spec"][:, r, :, bass.ds(c * P, P)].rearrange("n k c -> k n c")).then_inc(loaded[s], 16)
                    pool.dma_start(vv[:, s], t["vv_t"][c]).then_inc(loaded[s], 16)
                    pool.dma_start(gate[:, s], t["gate_t"][c]).then_inc(loaded[s], 16)

        @block.sync
        def _(sp):
            sp.dma_start(back[:], t["k_back"]).then_inc(consts, 16)
            with nc.allow_non_contiguous_dma(reason="skips by channel"):
                sp.dma_start(skip[:], t["hy_bias"][0].rearrange("(m p) -> p m", p=P)).then_inc(consts, 16)
            lead(sp, *stored, unit=16)
            with sp.Fori(0, CT // SLOTS) as i:
                for s in range(SLOTS):
                    c = SLOTS * i + s
                    sp.wait_ge(y_done, nth(c))
                    sp.dma_start(t["yh_t"][c], y[:, s]).then_inc(stored[s], 16)
            for s in range(SLOTS):
                sp.wait_ge(stored[s], nth(CT // SLOTS - 1, 16))

        @block.tensor
        def _(pe):
            lead(pe, y_mm, s_mm)
            pe.wait_ge(consts, 32)
            pe.wait_ge(ones_done, 1)
            with pe.Fori(0, CT // SLOTS) as i:
                for s in range(SLOTS):
                    c = SLOTS * i + s
                    pe.wait_ge(loaded[s], 64 * i + 64)
                    for q in range(4):
                        pe.wait_ge(y_sum, nth(4 * (c - 1) + q))
                        for a in range(4):
                            n2 = 4 * q + a
                            for r in range(2):
                                ins = pe.matmul(y_ps[:, q, a * P:(a + 1) * P], z[:, s, r, n2], back[:, r], start=(r == 0), stop=(r == 1))
                        ins.then_inc(y_mm, 1)
                    pe.wait_ge(sq_done, nth(c))
                    pe.wait_ge(s_done, nth(c - 1))
                    for n in range(NC_LAT):
                        ins = pe.matmul(s_ps[:, n:n + 1], sq[:, n * P:(n + 1) * P], ones[:], start=True, stop=True)
                    ins.then_inc(s_mm, 1)

        @block.scalar
        def _(act):
            lead(act, sq_done)
            with act.Fori(0, CT // SLOTS) as i:
                for s in range(SLOTS):
                    c = SLOTS * i + s
                    act.wait_ge(y_done, nth(c))
                    act.wait_ge(s_mm, nth(c - 1))
                    act.activation(sq[:], y[:, s], ACT.Square).then_inc(sq_done, 1)

        @block.vector
        def _(dve):
            lead(dve, y_sum, y_done, s_done)
            dve.memset(ssh[:], 0.0)
            dve.memset(ones[:], 1.0).then_inc(ones_done, 1)
            dve.wait_ge(consts, 32)
            with dve.Fori(0, CT // SLOTS) as i:
                for s in range(SLOTS):
                    c = SLOTS * i + s
                    dve.tensor_copy(skip_now[:, s:s + 1], skip[:, bass.ds(c, 1)]).then_inc(skip_done, 1)
                    dve.wait_ge(skip_done, c + 1)
                    dve.wait_ge(loaded[s], 64 * i + 64)
                    dve.wait_ge(stored[s], nth(i - 1, 16))
                    dve.wait_ge(sq_done, nth(c - SLOTS))
                    for q in range(4):
                        dve.wait_ge(y_mm, nth(4 * c + q))
                        def tok(a):
                            return a[:, s].rearrange("p (n k) -> p k n", k=RIN)[:, 4 * q:4 * q + 4]
                        dve.scalar_tensor_tensor(tok(y), tok(vv), skip_now[:, s:s + 1], y_ps[:, q].rearrange("p (k n) -> p k n", n=P),
                                                 ALU.mult, ALU.add).then_inc(y_sum, 1)
                    dve.wait_ge(y_sum, nth(4 * c + 3))
                    dve.tensor_tensor(y[:, s], y[:, s], gate[:, s], ALU.mult).then_inc(y_done, 1)
                    dve.wait_ge(s_mm, nth(c))
                    dve.wait_ge(s_done, nth(c - 1))
                    dve.tensor_tensor(ssh[:], ssh[:], s_ps[:, 0:NC_LAT], ALU.add).then_inc(s_done, 1)
ROWS_SHAPE = [NC_LAT, 2, 3, HEADS * CHUNK]
STEPS_LN = 8


def per_head(a, n, side):
    return a[:, bass.ds(n, 1), side * HEADS:(side + 1) * HEADS].rearrange("p a h -> p (a h)").unsqueeze(2).to_broadcast([P, HEADS, HEADDIM])


def by_head(a):
    return a.rearrange("p (h d) -> p h d", h=HEADS)


def ssd_scales(nc, t, keep):
    with ExitStack() as ph:
        def sem(name):
            return nc.alloc_semaphore(name)

        def sb(name, shape, dt=F32):
            return ph.enter_context(nc.sbuf_tensor("q_" + name, shape, dt))

        def psum(name, shape):
            return ph.enter_context(nc.psum_tensor("q_" + name, shape, F32))

        dt, te, cd = keep["dt_raw"], keep["to_end"], keep["chunk_decay"]
        W = 2 * HEADS
        bias = sb("bias", [P, W])
        a_neg = sb("a_neg", [P, W])
        tri = sb("tri", [P, 2, P])
        ones = sb("ones", [P, P])
        e = sb("e", [P, NCH, W])
        s = sb("s", [P, NCH, W])
        q = sb("q", [P, NCH, W])
        pos = sb("pos", [P, NCH, W])
        da = sb("da", [P, NCH, W])
        rows = sb("rows", [HEADS, SEQ])
        parts = sb("parts", [HEADS, 2, 3, SEQ], BF16)
        cum_ps = psum("cum_ps", [P, 2, BANK])
        tot_ps = psum("tot_ps", [P, 2, BANK])
        row_ps = psum("row_ps", [HEADS, 4, BANK])
        consts, v_step, e_in, e_out, log_done, exp_a, da_done, sums, rows_mm, rows_used, expo, stored = (sem("q_" + n) for n in (
            "consts", "v_step", "e_in", "e_out", "log_done", "exp_a", "da_done", "sums", "rows_mm", "rows_used", "expo", "stored"))
        weights, a_ready, parts_done = sem("q_weights"), sem("q_a_ready"), sem("q_parts_done")
        block = ph.enter_context(nc.Block())

        @block.sync
        def _(sp):
            sp.dma_start(bias[:], t["dt_bias"][0].rearrange("s h -> (s h)").partition_broadcast(P)).then_inc(consts, 16)
            sp.dma_start(a_neg[:], t["a_log"][0].rearrange("s h -> (s h)").partition_broadcast(P)).then_inc(consts, 16)
            sp.dma_start(tri[:], t["k_tri"]).then_inc(consts, 16)
            sp.wait_ge(parts_done, 2)
            for side in range(2):
                for k in range(3):
                    sp.dma_start(t["rows"][:, side, k].rearrange("n (h i) -> h n i", h=HEADS),
                                 parts[:, side, k].rearrange("h (n i) -> h n i", n=NC_LAT)).then_inc(stored, 16)
            sp.wait_ge(stored, 96)

        @block.scalar
        def _(act):
            act.wait_ge(consts, 48)
            act.activation(a_neg[:], a_neg[:], ACT.Exp).then_inc(exp_a, 1)
            act.wait_ge(e_in, 1)
            act.activation(e[:], e[:], ACT.Exp).then_inc(e_out, 1)
            act.wait_ge(weights, 1)
            act.activation(te[:], te[:], ACT.Exp).then_inc(expo, 1)
            act.activation(cd[:], cd[:], ACT.Exp).then_inc(expo, 1)

        @block.tensor
        def _(pe):
            pe.wait_ge(da_done, 1)
            for side in range(2):
                cols = slice(side * HEADS, (side + 1) * HEADS)
                w = NCH * HEADS
                pe.matmul(cum_ps[:, side, 0:w], tri[:, side], da[:, :, cols], start=True, stop=True)
                ins = pe.matmul(tot_ps[:, side, 0:w], ones[:], da[:, :, cols], start=True, stop=True)
            ins.then_inc(sums, 1)
            for side in range(2):
                cols = slice(side * HEADS, (side + 1) * HEADS)
                if side:
                    pe.wait_ge(rows_used, 1)
                for n in range(NC_LAT):
                    ins = pe.matmul(row_ps[:, n // 4, (n % 4) * P:(n % 4 + 1) * P], da[:, n, cols], tri[:, side], start=True, stop=True)
                ins.then_inc(rows_mm, 1)

        @block.vector
        def _(dve):
            step = chained(dve, v_step)
            dve.memset(ones[:], 1.0)
            dve.wait_ge(consts, 48)
            step(dve.tensor_tensor(dt[:], dt[:], bias[:].unsqueeze(1).to_broadcast([P, NCH, W]), ALU.add))
            step(dve.tensor_scalar(pos[:], dt[:], 0.0, None, ALU.max))
            step(dve.tensor_scalar(e[:], dt[:], -1.0, None, ALU.mult))
            dve.tensor_tensor(e[:], e[:], dt[:], ALU.min).then_inc(e_in, 1)
            dve.wait_ge(e_out, 1)
            step(dve.tensor_scalar(s[:], e[:], 2.0, None, ALU.add))
            step(dve.reciprocal(s[:], s[:]))
            step(dve.tensor_tensor(s[:], s[:], e[:], ALU.mult))
            step(dve.tensor_tensor(q[:], s[:], s[:], ALU.mult))
            step(dve.tensor_scalar(e[:], q[:], 1.0 / (2 * STEPS_LN + 1), None, ALU.mult))
            for k in range(STEPS_LN - 1, 0, -1):
                step(dve.scalar_tensor_tensor(e[:], e[:], 1.0 / (2 * k + 1), q[:], ALU.add, ALU.mult))
            step(dve.scalar_tensor_tensor(e[:], e[:], 1.0, s[:], ALU.add, ALU.mult))
            step(dve.scalar_tensor_tensor(dt[:], e[:], 2.0, pos[:], ALU.mult, ALU.add))
            dve.wait_ge(exp_a, 1)
            step(dve.tensor_scalar(a_neg[:], a_neg[:], -1.0, None, ALU.mult))
            dve.tensor_tensor(da[:], dt[:], a_neg[:].unsqueeze(1).to_broadcast([P, NCH, W]), ALU.mult).then_inc(da_done, 1)
            dve.wait_ge(sums, 1)
            for side in range(2):
                cols = slice(side * HEADS, (side + 1) * HEADS)

                def chunks(a):
                    return a[:, side, 0:NCH * HEADS].rearrange("p (n h) -> p n h", n=NCH)
                step(dve.tensor_copy(cd[:, :, cols], chunks(tot_ps)))
                ins = dve.tensor_tensor(te[:, :, cols], cd[:, :, cols], chunks(cum_ps), ALU.subtract)
                if side == 0:
                    step(ins)
            ins.then_inc(weights, 1)
            for side in range(2):
                dve.wait_ge(rows_mm, side + 1)
                dve.tensor_copy(rows[:], row_ps[:].rearrange("p a b -> p (a b)")).then_inc(rows_used, 1)
                dve.wait_ge(rows_used, side + 1)
                step(dve.tensor_copy(parts[:, side, 0], rows[:]))
                step(dve.tensor_tensor(rows[:], rows[:], parts[:, side, 0], ALU.subtract))
                step(dve.tensor_copy(parts[:, side, 1], rows[:]))
                step(dve.tensor_tensor(rows[:], rows[:], parts[:, side, 1], ALU.subtract))
                dve.tensor_copy(parts[:, side, 2], rows[:]).then_inc(parts_done, 1)
                dve.wait_ge(parts_done, side + 1)
            dve.wait_ge(expo, 2)
            dve.tensor_tensor(te[:], te[:], dt[:], ALU.mult)


def ssd_backward_states(nc, t, keep):
    with ExitStack() as ph:
        def sem(name):
            return nc.alloc_semaphore(name)

        def sb(name, shape, dt=F32):
            return ph.enter_context(nc.sbuf_tensor("r_" + name, shape, dt))

        te, cd = keep["to_end"], keep["chunk_decay"]
        XB = D + GROUPS * STATE
        xb = sb("xb", [P, 2, XB])
        xw = sb("xw", [P, 2, D])
        h = sb("h", [P, 2, D])
        h_ps = ph.enter_context(nc.psum_tensor("r_h_ps", [P, 2, D], F32))
        loaded = [sem(f"r_loaded{s}") for s in range(2)]
        stored = [sem(f"r_stored{s}") for s in range(2)]
        xw_done, h_mm, h_decayed, h_done, h_zero, sp_passed, pool_passed, dve_passed = (sem("r_" + n) for n in (
            "xw_done", "h_mm", "h_decayed", "h_done", "h_zero", "sp_passed", "pool_passed", "dve_passed"))
        block = ph.enter_context(nc.Block())

        @block.gpsimd
        def _(pool):
            with pool.Fori(0, NCH // 2) as i:
                for s in range(2):
                    m = 2 * i + s
                    pool.wait_ge(h_mm, nth(m - 2))
                    pool.sem_inc(pool_passed, 1)
                    pool.dma_start(xb[:, s], t["xbc"][NCH - 1 - m][:, 0:XB]).then_inc(loaded[s], 16)

        @block.sync
        def _(sp):
            lead(sp, *stored, unit=16)
            with sp.Fori(0, NCH // 2) as i:
                for s in range(2):
                    m = 2 * i + s
                    sp.wait_ge(h_done, nth(m - 1))
                    sp.sem_inc(sp_passed, 1)
                    sp.dma_start(t["h_back"][NCH - 1 - m], h[:, s]).then_inc(stored[s], 16)
            for s in range(2):
                sp.wait_ge(stored[s], nth(NCH // 2 - 1, 16))

        @block.tensor
        def _(pe):
            lead(pe, h_mm)
            with pe.Fori(0, NCH // 2) as i:
                for s in range(2):
                    m = 2 * i + s
                    pe.wait_ge(loaded[s], 16 * i + 16)
                    pe.wait_ge(xw_done, nth(m))
                    pe.wait_ge(h_done, nth(m - 2))
                    for g in range(GROUPS):
                        ins = pe.matmul(h_ps[:, s, g * BANK:(g + 1) * BANK], xb[:, s, D + g * STATE:D + (g + 1) * STATE],
                                        xw[:, s, g * BANK:(g + 1) * BANK], start=True, stop=True)
                    ins.then_inc(h_mm, 1)

        @block.vector
        def _(dve):
            lead(dve, xw_done, h_decayed)
            dve.memset(h[:, 0], 0.0).then_inc(h_zero, 1)
            dve.wait_ge(h_zero, 1)
            lead(dve, h_done)
            with dve.Fori(0, NCH // 2) as i:
                for s in range(2):
                    m = 2 * i + s
                    n = NCH - 1 - m
                    dve.wait_ge(loaded[s], 16 * i + 16)
                    dve.wait_ge(h_mm, nth(m - 2))
                    dve.sem_inc(dve_passed, 1)
                    dve.tensor_tensor(by_head(xw[:, s]), by_head(xb[:, s, 0:D]), per_head(te, n, 1), ALU.mult).then_inc(xw_done, 1)
                    dve.wait_ge(stored[1 - s], nth(i - 1 + s, 16))
                    dve.sem_inc(dve_passed, 1)
                    dve.tensor_tensor(by_head(h[:, 1 - s]), by_head(h[:, s]), per_head(cd, n, 1), ALU.mult).then_inc(h_decayed, 1)
                    dve.wait_ge(h_decayed, nth(m))
                    dve.wait_ge(h_mm, nth(m))
                    dve.tensor_tensor(h[:, 1 - s], h[:, 1 - s], h_ps[:, s], ALU.add).then_inc(h_done, 1)
                    dve.wait_ge(h_done, nth(m))


def ssd_and_out(nc, t, keep):
    with ExitStack() as ph:
        def sem(name):
            return nc.alloc_semaphore(name)

        def sb(name, shape, dt=F32):
            return ph.enter_context(nc.sbuf_tensor("o_" + name, shape, dt))

        def psum(name, shape):
            return ph.enter_context(nc.psum_tensor("o_" + name, shape, F32))

        dt, te, cd, ssh, gate_row = keep["dt_raw"], keep["to_end"], keep["chunk_decay"], keep["ssh"], keep["gate_row"]
        XB = D + GROUPS * STATE
        HALF = BANK
        w_out = sb("w_out", [P, 2 * KT, D])
        gn = sb("gn", [P, 2 * KT])
        fw = sb("fw", [P, D])
        dk = sb("dk", [P, 2, KT])
        tri = sb("tri", [P, 2, P])
        ones = sb("ones", [P, 1])
        ones_b = sb("ones_b", [3, HEADDIM], BF16)
        halves = sb("halves", [P, NC_LAT])
        eps = sb("eps", [P, 1])
        xk = sb("xk", [P, 2, XB])
        bc = sb("bc", [P, 2, 2 * GROUPS, P])
        xt = sb("xt", [P, 2, KT, P])
        zs = sb("zs", [P, 2, KT, P])
        hb = sb("hb", [P, 2, D])
        yh = sb("yh", [P, KT, P])
        xres = sb("xres", [P, D])
        row_i = sb("row_i", [6, 2, HEADS * CHUNK], BF16)
        row_j = sb("row_j", [6, 2, HEADS * CHUNK], BF16)
        cbm = sb("cbm", [P, 2, GROUPS, P])
        es = sb("es", [P, HEADS, P])
        mu = sb("mu", [P, HEADS, P])
        ea = sb("ea", [P, 2, 2, HALF])
        xf = sb("xf", [P, D])
        xbk = sb("xbk", [P, D])
        xw = sb("xw", [P, D])
        h = sb("h", [P, D])
        ys = sb("ys", [P, KT, P])
        tmp = sb("tmp", [P, HALF])
        sq = sb("sq", [P, KT, P])
        rs = sb("rs", [P, 4])
        o = sb("o", [P, D])
        ob = sb("ob", [P, D])
        o_ps = psum("o_ps", [P, 2, BANK])
        d_ps = psum("d_ps", [P, 2, BANK])
        in_ps = psum("in_ps", [P, 2, BANK])
        y_ps = psum("y_ps", [P, BANK])
        m_ps = psum("m_ps", [P, BANK])

        names = ("consts w_in_ w_ready prep h_zero xw_done cb_mm cbm_done s_mm dc_done dm_done e_done ml_done "
                 "r_mm y_read y_done v_step ys_done h_mm h_done sq_done ss_mm ss_done rs_done o_mm oa_done ob_done "
                 "sp_passed o_pre fsq_done frs_done fin_done hn_done p_step rsh_done rows_set xt_done h_dec f_step")
        S = {n: sem("o_" + n) for n in names.split()}
        early = [sem(f"o_early{s}") for s in range(2)]
        ctx_in = [sem(f"o_ctx_in{s}") for s in range(2)]
        rows_in, late_in, stored = sem("o_rows_in"), sem("o_late_in"), sem("o_stored")
        EARLY = 16 * 5
        block = ph.enter_context(nc.Block())
        LAST = NC_LAT - 1

        def pairs(eng, body, head=0, count=NC_LAT // 2 - 1):
            with eng.Fori(0, count) as i:
                for j in range(2):
                    n = head + j
                    body(2 * i + n, i + n // 2, n % 2)
            for n in range(head + 2 * count, NC_LAT):
                body(n, n // 2, n % 2)

        @block.sync
        def _(sp):
            def load_early(n, s):
                sp.wait_ge(S["ys_done"], nth(2 * (n - 2) + 1))
                sp.sem_inc(S["sp_passed"], 1)
                sp.wait_ge(S["h_mm"], nth(n))
                sp.sem_inc(S["sp_passed"], 1)
                sp.dma_start(xk[:, s], t["xbc"][n][:, 0:XB]).then_inc(early[s], 16)
                cols = bass.ds(n * P, P)
                sp.dma_start(bc[:, s], t["xbc_t"][KT:XBC_T][:, :, cols].rearrange("m p t -> p m t")).then_inc(early[s], 16)
                sp.dma_start(xt[:, s], t["xbc_t"][0:KT][:, :, cols].rearrange("m p t -> p m t")).then_inc(early[s], 16)
                sp.dma_start(zs[:, s], t["zs_t"][:, :, cols].rearrange("m p t -> p m t")).then_inc(early[s], 16)
                sp.dma_start(hb[:, s], t["h_back"][n]).then_inc(early[s], 16)

            def load_rows(n):
                sp.wait_ge(S["s_mm"], nth(6 * (n - 1) + 5))
                sp.sem_inc(S["sp_passed"], 1)
                sp.wait_ge(S["rows_set"], 1)
                rows = t["rows"][n].rearrange("s k c -> k s c")
                sp.dma_start(row_i[0:3], rows).then_inc(rows_in, 16)
                sp.dma_start(row_j[3:6], rows).then_inc(rows_in, 16)

            def load_late(n):
                sp.wait_ge(S["o_mm"], nth(4 * (n - 1) + 3))
                sp.sem_inc(S["sp_passed"], 1)
                sp.wait_ge(S["o_pre"], nth(n - 1))
                sp.sem_inc(S["sp_passed"], 1)
                sp.dma_start(yh[:], t["yh_t"][:, :, bass.ds(n * P, P)].rearrange("m p t -> p m t")).then_inc(late_in, 16)
                sp.dma_start(xres[:], t["x"][0][bass.ds(n * P, P)]).then_inc(late_in, 16)

            def store(n):
                sp.wait_ge(S["fin_done"], nth(n))
                sp.sem_inc(S["sp_passed"], 1)
                sp.dma_start(t["out"][0][bass.ds(n * P, P)], ob[:]).then_inc(stored, 16)

            for s in range(2):
                sp.dma_start(xk[:, s], t["xbc"][NC_LAT + s][:, 0:XB]).then_inc(ctx_in[s], 16)
            with nc.allow_non_contiguous_dma(reason="small vectors"):
                sp.dma_start(gn[:], t["gnorm_w"][0].rearrange("(m p) -> p m", p=P)).then_inc(S["consts"], 16)
                sp.dma_start(fw[:], t["final_norm_w"].partition_broadcast(P)).then_inc(S["consts"], 16)
                for side in range(2):
                    for par in range(2):
                        sp.dma_start(dk[64 * par:64 * par + 64, side],
                                     t["d_skip"][0, side].rearrange("(m two) -> two m", two=2)[par].partition_broadcast(HEADDIM)).then_inc(S["consts"], 16)
                sp.dma_start(tri[:], t["k_tri"]).then_inc(S["consts"], 16)
            sp.dma_start(w_out[:], t["w_out"][0].rearrange("(k p) d -> p k d", p=P)).then_inc(S["w_in_"], 16)
            lead(sp, stored, unit=16)
            load_early(0, 0)
            load_rows(0)

            def body(n, i, s):
                load_early(n + 1, 1 - s)
                load_rows(n + 1)
                load_late(n)
                store(n - 1)
            load_early(1, 1)
            load_rows(1)
            load_late(0)
            with sp.Fori(0, LAST // 2) as i:
                for j in range(2):
                    n = 2 * i + 1 + j
                    body(n, None, (1 + j) % 2)
            load_late(LAST)
            store(LAST - 1)
            store(LAST)
            sp.wait_ge(stored, nth(LAST, 16))

        @block.gpsimd
        def _(pool):
            step = chained(pool, S["p_step"])
            pool.memset(halves[:], -0.5)
            pool.memset(eps[:], EPS)
            pool.memset(row_i[:], -1.0)
            step(pool.memset(row_j[:], 1.0))
            pool.sem_inc(S["rows_set"], 1)
            pool.wait_ge(S["consts"], 16 * 7)
            step(pool.tensor_tensor(dk[:, 0], dk[:, 0], dk[:, 1], ALU.add))
            step(pool.tensor_scalar(ssh[:], ssh[:], 1.0 / D, EPS, ALU.mult, ALU.add))
            pool.tensor_tensor(ssh[:], ssh[:], halves[:], ALU.pow).then_inc(S["rsh_done"], 1)
            lead(pool, S["xw_done"], S["rs_done"], S["frs_done"], S["xt_done"])

            def weigh(n, s, m):
                pool.wait_ge(S["h_mm"], nth(m - 1))
                pool.tensor_tensor(by_head(xw[:]), by_head(xk[:, s, 0:D]), per_head(te, n, 0), ALU.mult).then_inc(S["xw_done"], 1)

            for s in range(2):
                pool.wait_ge(ctx_in[s], 16)
                weigh(NC_LAT + s, s, s)

            def chunk(n, i, s):
                pool.wait_ge(early[s], EARLY * i + EARLY)
                pool.wait_ge(S["r_mm"], nth(2 * (n - 1) + 1))
                pool.tensor_tensor(by_head(xf[:]), by_head(xk[:, s, 0:D]), per_head(dt, n, 0), ALU.mult)
                pool.tensor_tensor(by_head(xbk[:]), by_head(xk[:, s, 0:D]), per_head(dt, n, 1), ALU.mult)
                pool.tensor_tensor(xt[:, s], xt[:, s], dk[:, 0].unsqueeze(2).to_broadcast([P, KT, P]), ALU.mult).then_inc(S["xt_done"], 1)
                weigh(n, s, n + 2)

            def powers(n):
                pool.wait_ge(S["ss_done"], nth(n))
                pool.tensor_tensor(rs[:, 0:1], rs[:, 0:1], halves[:, 0:1], ALU.pow).then_inc(S["rs_done"], 1)
                pool.wait_ge(S["fsq_done"], nth(n))
                pool.tensor_tensor(rs[:, 1:2], rs[:, 3:4], eps[:], ALU.add).then_inc(S["f_step"], 1)
                pool.wait_ge(S["f_step"], n + 1)
                pool.tensor_tensor(rs[:, 1:2], rs[:, 1:2], halves[:, 0:1], ALU.pow).then_inc(S["frs_done"], 1)

            chunk(0, 0, 0)

            def body(n, i, s):
                if not (isinstance(n, int) and n == LAST):
                    chunk(n + 1, i + s, 1 - s)
                powers(n)
            pairs(pool, body)

        @block.tensor
        def _(pe):
            lead(pe, S["cb_mm"], S["s_mm"], S["r_mm"], S["h_mm"], S["ss_mm"], S["o_mm"])

            def state(s, m):
                pe.wait_ge(S["xw_done"], nth(m))
                for g in range(GROUPS):
                    ins = pe.matmul(d_ps[:, g], xk[:, s, D + g * STATE:D + (g + 1) * STATE], xw[:, g * BANK:(g + 1) * BANK], start=True, stop=True)
                ins.then_inc(S["h_mm"], 1)

            def cb(n, i, s):
                pe.wait_ge(early[s], EARLY * i + EARLY)
                pe.wait_ge(S["ss_done"], nth(n - 2))
                for g in range(GROUPS):
                    ins = pe.matmul(m_ps[:, g * P:(g + 1) * P], bc[:, s, g], bc[:, s, GROUPS + g], start=True, stop=True)
                ins.then_inc(S["cb_mm"], 1)

            def quad(n, k):
                if k == 0:
                    pe.wait_ge(rows_in, 32 * n + 32)
                    pe.wait_ge(S["h_done"], nth(n + 1))
                pe.wait_ge(S["dc_done"], nth(6 * n + k - 1))
                pe.wait_ge(S["dm_done"], nth(4 * n + min(k, 4) - 1))
                for side in range(2):
                    if k < 4:
                        for a in range(4):
                            cols = slice((4 * k + a) * P, (4 * k + a + 1) * P)
                            ins = pe.matmul(d_ps[:, side, a * P:(a + 1) * P], row_j[:, side, cols], row_i[:, side, cols], start=True, stop=True)
                    else:
                        for par in range(2):
                            src = row_i[0:3, side].rearrange("q (m two i) -> q two m i", two=2, i=P)[:, par, 4 * (k - 4):4 * (k - 4) + 4]
                            ins = pe.matmul(d_ps[64 * par:64 * par + 64, side], ones_b[:], src, start=True, stop=True)
                ins.then_inc(S["s_mm"], 1)

            def rest(n, i, s):
                for f in range(2):
                    pe.wait_ge(S["y_read"], nth(2 * n + f - 1))
                    if f == 0:
                        pe.wait_ge(S["h_done"], nth(n + 1))
                    for a in range(4):
                        m = 4 * f + a
                        c_now = bc[:, s, GROUPS + m // 4]
                        out = slice(a * P, (a + 1) * P)
                        pe.matmul(in_ps[:, 0, out], h[:, m * P:(m + 1) * P], c_now, start=True, stop=True)
                        pe.matmul(in_ps[:, 1, out], hb[:, s, m * P:(m + 1) * P], c_now, start=True, stop=True)
                    pe.wait_ge(S["ml_done"], nth(4 * n + 2 * f + 1))
                    pe.wait_ge(S["xt_done"], nth(n))
                    for a in range(4):
                        for par in range(2):
                            hd = 8 * f + 2 * a + par
                            out = y_ps[64 * par:64 * par + 64, a * P:(a + 1) * P]
                            cols = slice(hd * HEADDIM, (hd + 1) * HEADDIM)
                            pe.matmul(out, xf[:, cols], es[:, hd], start=True, stop=False)
                            ins = pe.matmul(out, xbk[:, cols], mu[:, hd], start=False, stop=True)
                    ins.then_inc(S["r_mm"], 1)
                pe.wait_ge(S["dc_done"], nth(6 * n + 5))
                state(s, n + 2)

            def sum_squares(n):
                pe.wait_ge(S["sq_done"], nth(n))
                if not (isinstance(n, int) and n == LAST):
                    pe.wait_ge(S["cbm_done"], nth(n + 1))
                for k in range(KT):
                    ins = pe.matmul(m_ps[:, 0:1], sq[:, k], ones[:], start=(k == 0), stop=(k == KT - 1))
                ins.then_inc(S["ss_mm"], 1)

            def quarter(n, k):
                half, part = k // 2, k % 2
                if k == 0:
                    pe.wait_ge(S["w_ready"], 1)
                    pe.wait_ge(late_in, 32 * n + 32)
                pe.wait_ge(S[("oa_done", "ob_done")[part]], nth(2 * n + half - 1))
                for a in range(KT):
                    src = ys[:, a] if part == 0 else yh[:, a]
                    ins = pe.matmul(o_ps[:, part], src, w_out[:, part * KT + a, half * BANK:(half + 1) * BANK], start=(a == 0), stop=(a == KT - 1))
                ins.then_inc(S["o_mm"], 1)

            pe.wait_ge(S["prep"], 1)
            for s in range(2):
                if s:
                    pe.wait_ge(S["h_done"], nth(0))
                state(s, s)
            cb(0, 0, 0)
            for k in range(6):
                quad(0, k)

            def body(n, i, s):
                last = isinstance(n, int) and n == LAST
                rest(n, i, s)
                if not last:
                    cb(n + 1, i + s, 1 - s)
                    quad(n + 1, 0)
                sum_squares(n)
                quarter(n, 0)
                for k in range(1, 4):
                    if not last:
                        quad(n + 1, k)
                    quarter(n, k)
                if not last:
                    quad(n + 1, 4)
                    quad(n + 1, 5)
            pairs(pe, body)

        @block.scalar
        def _(act):
            lead(act, S["dc_done"], S["e_done"], S["sq_done"], S["oa_done"], S["fsq_done"])

            def copy(n, k):
                act.wait_ge(S["s_mm"], nth(6 * n + k))
                if k == 0:
                    act.wait_ge(S["r_mm"], nth(2 * (n - 1) + 1))
                act.activation(es[:, 4 * k:4 * k + 4].rearrange("p h i -> p (h i)"), d_ps[:, 0], ACT.Copy).then_inc(S["dc_done"], 1)

            def exp(n, k):
                act.wait_ge(S["dm_done"], nth(4 * n + k))
                cols = es[:, 4 * k:4 * k + 4]
                act.activation(cols, cols, ACT.Exp).then_inc(S["e_done"], 1)

            def exp_sums(n, k):
                act.wait_ge(S["s_mm"], nth(6 * n + k))
                act.wait_ge(S["ys_done"], nth(2 * (n - 1) + 1))
                act.activation(ea[:, k - 4], d_ps[:], ACT.Exp).then_inc(S["dc_done"], 1)

            def out_part(n, half):
                act.wait_ge(S["o_mm"], nth(4 * n + 2 * half))
                if half == 0:
                    act.wait_ge(S["rs_done"], nth(n))
                    act.wait_ge(S["fin_done"], nth(n - 1))
                act.activation(o[:, half * BANK:(half + 1) * BANK], o_ps[:, 0], ACT.Identity, scale=rs[:, 0:1]).then_inc(S["oa_done"], 1)

            def head(n, with_out):
                copy(n, 0)
                exp(n, 0)
                if with_out:
                    out_part(n - 1, 0)
                copy(n, 1)
                exp(n, 1)
                copy(n, 2)
                exp(n, 2)
                if with_out:
                    out_part(n - 1, 1)
                copy(n, 3)
                exp(n, 3)
                exp_sums(n, 4)
                exp_sums(n, 5)

            def body(n, i, s):
                act.wait_ge(S["ys_done"], nth(2 * n + 1))
                act.wait_ge(S["ss_mm"], nth(n - 1))
                act.activation(sq[:], ys[:], ACT.Square).then_inc(S["sq_done"], 1)
                if isinstance(n, int) and n == LAST:
                    out_part(n, 0)
                    out_part(n, 1)
                else:
                    head(n + 1, True)
                act.wait_ge(S["o_pre"], nth(n))
                act.activation(ob[:], o[:], ACT.Square, scale=D ** -0.5, accum_out=rs[:, 3:4]).then_inc(S["fsq_done"], 1)
            head(0, False)
            pairs(act, body)

        @block.vector
        def _(dve):
            dve.memset(h[:], 0.0)
            dve.memset(ones_b[:], 1.0)
            dve.memset(ones[:], 1.0).then_inc(S["prep"], 1)
            lead(dve, *(S[n] for n in "cbm_done dm_done ml_done y_read ys_done h_done ss_done ob_done o_pre fin_done h_dec hn_done".split()))
            dve.wait_ge(S["prep"], 1)

            def decay(n, m):
                if not isinstance(m, int) or m >= 2:
                    dve.wait_ge(S["r_mm"], nth(2 * n + 1))
                dve.tensor_tensor(by_head(h[:]), by_head(h[:]), per_head(cd, n, 0), ALU.mult).then_inc(S["h_dec"], 1)

            def add_state(m):
                dve.wait_ge(S["h_dec"], nth(m))
                dve.wait_ge(S["h_mm"], nth(m))
                dve.tensor_tensor(h[:], h[:], d_ps[:].rearrange("p a b -> p (a b)"), ALU.add).then_inc(S["h_done"], 1)
                dve.wait_ge(S["h_done"], nth(m))

            for s in range(2):
                decay(NC_LAT + s, s)
                add_state(s)

            def masks(n):
                dve.wait_ge(S["cb_mm"], nth(n))
                dve.wait_ge(S["consts"], 16 * 7)
                for u in range(2):
                    ins = dve.tensor_tensor(cbm[:, u], m_ps[:, 0:GROUPS * P].rearrange("p (g i) -> p g i", g=GROUPS),
                                            tri[:, u].unsqueeze(1).to_broadcast([P, GROUPS, P]), ALU.mult)
                ins.then_inc(S["cbm_done"], 1)

            def least(n, k):
                dve.wait_ge(S["dc_done"], nth(6 * n + k))
                cols = es[:, 4 * k:4 * k + 4].rearrange("p h i -> p (h i)")
                dve.tensor_tensor(cols, cols, d_ps[:, 1], ALU.min).then_inc(S["dm_done"], 1)

            def weigh(n, k):
                dve.wait_ge(S["cbm_done"], nth(n))
                dve.wait_ge(S["e_done"], nth(4 * n + k))
                if k == 0:
                    dve.wait_ge(S["r_mm"], nth(2 * (n - 1) + 1))
                heads = slice(4 * k, 4 * k + 4)
                g = k // 2
                dve.tensor_tensor(mu[:, heads], es[:, heads], cbm[:, 1, g].unsqueeze(1).to_broadcast([P, 4, P]), ALU.mult)
                dve.tensor_tensor(es[:, heads], es[:, heads], cbm[:, 0, g].unsqueeze(1).to_broadcast([P, 4, P]), ALU.mult).then_inc(S["ml_done"], 1)

            def sum_done(n):
                dve.wait_ge(S["ss_mm"], nth(n))
                dve.wait_ge(S["rs_done"], nth(n - 1))
                dve.wait_ge(S["oa_done"], nth(2 * n - 1))
                dve.tensor_scalar(rs[:, 0:1], m_ps[:, 0:1], 1.0 / D, EPS, ALU.mult, ALU.add).then_inc(S["ss_done"], 1)
                dve.wait_ge(S["rsh_done"], 1)
                dve.tensor_copy(rs[:, 2:3], ssh[:, bass.ds(n, 1)]).then_inc(S["hn_done"], 1)

            def out_part(n, half):
                cols = slice(half * BANK, (half + 1) * BANK)
                dve.wait_ge(S["hn_done"], nth(n))
                dve.wait_ge(S["oa_done"], nth(2 * n + half))
                dve.wait_ge(S["o_mm"], nth(4 * n + 2 * half + 1))
                dve.scalar_tensor_tensor(o[:, cols], o_ps[:, 1], rs[:, 2:3], o[:, cols], ALU.mult, ALU.add).then_inc(S["ob_done"], 1)

            def residual(n):
                dve.wait_ge(S["ob_done"], nth(2 * n + 1))
                v = S["v_step"]
                dve.tensor_tensor(o[:], o[:], gate_row[:], ALU.mult).then_inc(v, 1)
                dve.wait_ge(v, n + 1)
                dve.wait_ge(late_in, 32 * n + 32)
                dve.wait_ge(stored, nth(n - 1, 16))
                dve.tensor_tensor(o[:], o[:], xres[:], ALU.add).then_inc(S["o_pre"], 1)

            def finish(n):
                dve.wait_ge(S["frs_done"], nth(n))
                dve.scalar_tensor_tensor(ob[:], o[:], rs[:, 1:2], fw[:], ALU.mult, ALU.mult).then_inc(S["fin_done"], 1)

            def outputs(n, s, i):
                for f in range(2):
                    q = slice(4 * f, 4 * f + 4)
                    base = 10 * n + 5 * f
                    out = ys[:, q].rearrange("p m i -> p (m i)")

                    def flat(a):
                        return a[:, s, q].rearrange("p m i -> p (m i)")
                    step = chained(dve, S["y_done"], base)
                    dve.wait_ge(S["r_mm"], nth(2 * n + f))
                    if f == 0:
                        dve.wait_ge(S["dc_done"], nth(6 * n + 5))
                        dve.wait_ge(S["xt_done"], nth(n))
                        dve.wait_ge(S["o_mm"], nth(4 * (n - 1) + 3))
                        dve.wait_ge(S["sq_done"], nth(n - 1))
                        dve.wait_ge(early[s], EARLY * i + EARLY)
                    step(dve.tensor_tensor(out, in_ps[:, 0], ea[:, f, 0], ALU.mult))
                    step(dve.tensor_tensor(tmp[:], in_ps[:, 1], ea[:, f, 1], ALU.mult))
                    step(dve.tensor_tensor(out, out, tmp[:], ALU.add))
                    step(dve.tensor_tensor(out, out, y_ps[:], ALU.add))
                    dve.sem_inc(S["y_read"], 1)
                    step(dve.tensor_tensor(out, out, flat(xt), ALU.add))
                    dve.tensor_tensor(out, out, flat(zs), ALU.mult).then_inc(S["ys_done"], 1)

            def head(n, with_out):
                masks(n)
                least(n, 0)
                weigh(n, 0)
                if with_out:
                    sum_done(n - 1)
                least(n, 1)
                weigh(n, 1)
                if with_out:
                    out_part(n - 1, 0)
                least(n, 2)
                weigh(n, 2)
                least(n, 3)
                weigh(n, 3)
                if with_out:
                    out_part(n - 1, 1)
                    residual(n - 1)

            head(0, False)
            dve.wait_ge(S["w_in_"], 16)
            for k in range(2 * KT):
                ins = dve.tensor_scalar(w_out[:, k], w_out[:, k], gn[:, k:k + 1], None, ALU.mult)
            ins.then_inc(S["w_ready"], 1)

            def body(n, i, s):
                outputs(n, s, i)
                decay(n, n + 2)
                add_state(n + 2)
                if isinstance(n, int) and n == LAST:
                    sum_done(n)
                    out_part(n, 0)
                    out_part(n, 1)
                    residual(n)
                    finish(n)
                else:
                    head(n + 1, True)
                    finish(n)
            pairs(dve, body)
INPUTS = ["x", "c", "ctx", "c_ctx", "norm_w", "ada_w", "ada_b", "w_in", "ssd_conv_w", "ssd_conv_b", "dt_bias", "a_log",
          "d_skip", "hy_conv_w", "hy_conv_b", "filt_w1", "filt_b1", "filt_w2", "filt_b2", "filt_w3", "filt_b3", "filt_w4",
          "filt_freq", "hy_bias", "gnorm_w", "w_out", "final_norm_w"]


def program(nc, t):
    with ExitStack() as ctx:
        def kept(name, shape, dt=F32):
            return ctx.enter_context(nc.sbuf_tensor(name, shape, dt))
        keep = {"eye": kept("eye", [P, P]), "gate_row": kept("gate_row", [P, D]), "to_end": kept("to_end", [P, NCH, 2 * HEADS]), "chunk_decay": kept("chunk_decay", [P, NCH, 2 * HEADS]), "ssh": kept("ssh", [P, NC_LAT]), "dt_raw": kept("dt_raw", [P, NCH, 2 * HEADS])}

        def phase(build):
            with nc.cleanup_on_exit():
                build(nc, t, keep)
        with nc.sbuf_tensor("xnT", [P, KT, TOK], F32) as xnT:
            keep["xnT"] = xnT
            with nc.sbuf_tensor("hT", [FW, SEQ + RIN], F32) as hT:
                keep["hT"] = hT
                phase(prepare)
                phase(filter_first_stage)
            phase(project_hyena)
            phase(project_ssd)
        phase(spectra)
        phase(hyena_back)
        phase(ssd_scales)
        phase(ssd_backward_states)
        phase(ssd_and_out)


SCRATCH = {
    "f_spec": [RIN, 2, P, D],
    "u_spec": [RIN, 2, P, D],
    "v_spec": [RIN, 2, P, D],
    "vv_t": [KT, P, SEQ],
    "gate_t": [KT, P, SEQ],
    "yh_t": [KT, P, SEQ],
    "zs_t": [KT, P, SEQ],
    "xbc_t": [XBC_T, P, TOK],
    "xbc": [NCH, P, XBC_T * P],
    "h_back": [NCH, P, D],
}


def kernel(**inputs):
    import concourse.bacc as _bacc
    from concourse.bass_utils import run_bass_kernel_spmd as _run

    nc = _bacc.Bacc("TRN2", target_bir_lowering=False, num_devices=1)
    arrays = {n: np.ascontiguousarray(inputs[n]) for n in INPUTS}
    arrays.update(shape_constants())
    t = {}
    for name, a in arrays.items():
        t[name] = nc.dram_tensor("in_" + name, a.shape, mybir.dt.from_np(a.dtype), kind="ExternalInput").ap()
    for name, shape in SCRATCH.items():
        t[name] = nc.dram_tensor("scratch_" + name, shape, F32, kind="Internal").ap()
    t["rows"] = nc.dram_tensor("scratch_rows", ROWS_SHAPE, BF16, kind="Internal").ap()
    t["out"] = nc.dram_tensor("out_0", [1, SEQ, D], F32, kind="ExternalOutput").ap()
    program(nc, t)
    r = _run(nc, [{"in_" + n: a for n, a in arrays.items()}], core_ids=[0])
    return r.results[0]["out_0"]
```

```python
from contextlib import ExitStack

import numpy as np
import concourse.bass as bass
from concourse import mybir

F32 = mybir.dt.float32
BF16 = mybir.dt.bfloat16
F32R = mybir.dt.float32r
ALU = mybir.AluOpType
ACT = mybir.ActivationFunctionType

P = 128
BANK = 512
D = 1024
KT = D // P
SEQ, CTX = 2048, 256
TOK = SEQ + CTX
CHUNK = 128
NC_LAT, NC_CTX = SEQ // CHUNK, CTX // CHUNK
NCH = NC_LAT + NC_CTX
GRID_W = 64
HEADS, HEADDIM, GROUPS, STATE = 16, 64, 2, 128
HPG = HEADS // GROUPS
XBC_T = (D + 2 * GROUPS * STATE) // P
COL_ZS = 0
COL_XBC = COL_ZS + D
COL_DT = COL_XBC + XBC_T * P
COL_ZH = COL_DT + 2 * HEADS
COL_HY = COL_ZH + D
EPS = 1e-6
FW = 64
EMB = 33
N_FFT = 2 * SEQ
RIN, ROUT = 16, 256
FG = 4
NG = P // FG
PI = 3.1415925
TWO_PI = 2.0 * np.pi
ROUNDER = 1.5 * 2.0 ** 23
PI_A = 6.28125
PI_B = float(np.float32(np.floor((TWO_PI - PI_A) * 2 ** 20) / 2 ** 20))
PI_C = float(np.float32(TWO_PI - PI_A - PI_B))


def chained(eng, sem, start=0):
    count = [0]

    def step(ins):
        count[0] += 1
        ins.then_inc(sem, 1)
        eng.wait_ge(sem, start + count[0])
    return step


LEAD = 20


def lead(eng, *sems, unit=1):
    for s in sems:
        eng.sem_inc(s, LEAD * unit)


def nth(n, unit=1):
    return (n + LEAD + 1) * unit


def product(pe, out, w, x, at, width, contraction):
    pairs = ((0, 0), (0, 1), (1, 0))
    for k in range(contraction):
        for n, (a, b) in enumerate(pairs):
            ins = pe.matmul(out, w[a](k), x[b][:, k, at:at + width], start=(k == 0 and n == 0), stop=(k == contraction - 1 and n == 2))
    return ins


def dft_tables():
    f32 = np.float32
    q, k1 = np.arange(P), np.arange(P)

    def first(rows):
        ang = 2 * np.pi * ((rows[:, None] * k1) % ROUT) / ROUT
        re, im = np.cos(ang), -np.sin(ang)
        im[:, 0] = (-1.0) ** rows
        return np.stack([re, im], 1)
    fwd = np.stack([first(q), first(ROUT - 1 - q)], 1)
    n2, j = np.arange(RIN), np.arange(RIN)
    mats = np.zeros((NG, 5, 2, FG, RIN, 2, FG, RIN))
    S, A, B, G1, G2 = (mats[:, m] for m in range(5))
    for g in range(NG):
        for l in range(FG):
            k = FG * g + l
            low = j < RIN // 2
            bins = k + ROUT * j if k else np.where(low, ROUT * j, P + ROUT * (j - RIN // 2))
            ang = 2 * np.pi * ((n2[:, None] * bins) % N_FFT) / N_FFT
            c, s = np.cos(ang), np.sin(ang)
            if k:
                S[g, 0, l, :, 0, l], S[g, 1, l, :, 0, l] = c, s
                S[g, 0, l, :, 1, l], S[g, 1, l, :, 1, l] = -s, c
            else:
                for r, m in ((0, low), (1, ~low)):
                    S[g, r, l, :, 0, l], S[g, r, l, :, 1, l] = c * m, -s * m
                S[g, :, l, :, 1, l, 0] = 0
                S[g, 0, l, :, 1, l, 0] = (-1.0) ** n2
            for r in range(2):
                A[g, :, l, :, r, l] = S[g, :, l, :, 0, l]
                B[g, :, l, :, r, l] = S[g, :, l, :, 1, l]
            if k:
                yre, yim = np.stack([c.T, s.T], 1), np.stack([-s.T, c.T], 1)
            else:
                A[g, :, l, :, 1, l, 0] = S[g, :, l, :, 1, l, 0]
                B[g, :, l, :, :, l, 0] = 0
                yre, yim = np.zeros((RIN, 2, RIN)), np.zeros((RIN, 2, RIN))
                for r, m in ((0, low), (1, ~low)):
                    yre[m, r], yim[m, r] = 2 * c.T[m], -2 * s.T[m]
                yre[0, 0], yim[0, 0], yim[0, 1] = 1, (-1.0) ** n2, 0
            G1[g, 0, l, :, :, l], G1[g, 1, l, :, :, l] = yre, yim
            G2[g, 1, l, :, :, l], G2[g, 0, l, :, :, l] = -yre, yim
            if not k:
                G2[g, :, l, 0] = 0
    mats = mats.reshape(NG, 5, P, P).transpose(0, 2, 1, 3)
    ang = 2 * np.pi * ((k1[:, None] * q) % ROUT) / ROUT
    er, ei = 2 * np.cos(ang) / N_FFT, -2 * np.sin(ang) / N_FFT
    er[0], ei[0] = 1 / N_FFT, (-1.0) ** q / N_FFT
    return fwd.astype(f32), np.ascontiguousarray(mats, dtype=f32), np.stack([er, ei], 1).astype(f32)


def shape_constants():
    f32 = np.float32
    fwd, mats, back = dft_tables()
    t = np.linspace(0.0, 1.0, SEQ, dtype=f32)[:, None]
    w = (f32(2.0 * np.pi / SEQ) * np.arange(SEQ, dtype=f32))[:, None]
    f = np.linspace(1e-4, (EMB - 1) // 2 - 1, (EMB - 1) // 2, dtype=f32)[None, :]
    feats = np.concatenate([t, np.cos(f * w), -np.sin(f * w)], axis=1)
    lo, hi = np.log(1e-2) / 1.5, np.log(1e-2) / 0.3
    deltas = np.abs(np.linspace(lo, hi, D, dtype=f32))
    q, n2 = np.arange(P)[:, None], np.arange(RIN)[None, :]
    mt = np.stack([-(RIN * q + n2), -(RIN * q + RIN - n2)], 2) / (SEQ - 1)
    i = np.arange(P)
    upto, since = (i[:, None] <= i[None, :]), (i[:, None] >= i[None, :])
    tri = np.stack([upto, since], 1)
    return {
        "k_fwd": fwd, "k_mats": mats, "k_back": back,
        "k_feats": np.ascontiguousarray(feats.T, dtype=f32), "k_deltas": deltas[None, :],
        "k_mt": mt.astype(f32), "k_eye": np.eye(P, dtype=f32), "k_tri": tri.astype(f32),
    }
def prepare(nc, t, keep):
    with ExitStack() as ph:
        def sem(name):
            return nc.alloc_semaphore(name)

        def sb(name, shape, dt=F32):
            return ph.enter_context(nc.sbuf_tensor("p_" + name, shape, dt))

        def psum(name, shape):
            return ph.enter_context(nc.psum_tensor("p_" + name, shape, F32))

        hT, eye, gate_row = keep["hT"], keep["eye"], keep["gate_row"]
        parts = [(keep["x_hi"], keep["x_lo"]), (keep["c_hi"], keep["c_lo"])]
        RING = 5
        early = keep["early"]
        at = [0]

        def place(rows, *dims):
            n = int(np.prod(dims))
            at[0] += n
            return early[0:rows, at[0] - n:at[0]]
        ada = place(P, RING, 3 * D).rearrange("p (r n) -> p r n", r=RING)
        s_wide = place(P, KT, P).rearrange("p (k n) -> p k n", k=KT)
        ada_b_gate = place(P, D)
        feats = place(EMB, SEQ)
        assert at[0] <= 2 * KT * SEQ
        at[0] = 2 * KT * SEQ
        turns = place(FW, SEQ)
        squares = place(P, D)
        c_col = sb("c_col", [P, KT, 2])
        s_col = sb("s_col", [P, KT, 2])
        ada_b_col = sb("ada_b_col", [P, 2 * KT])
        norm_w = sb("norm_w", [P, KT])
        mod = sb("mod", [P, 2, 2, KT])
        xg = sb("xg", [P, 2, 4, D])
        ss = sb("ss", [P, NCH])
        rstd = sb("rstd", [P, NCH])
        halves = sb("halves", [P, NCH])
        xn = sb("xn", [P, 2, BANK])
        w1 = sb("w1", [EMB, FW])
        w23 = sb("w23", [FW, 2, FW])
        fb = sb("fb", [FW, 3])
        freq = sb("freq", [FW, 1])
        ang = sb("ang", [FW, SEQ])
        mod_ps = psum("mod_ps", [P, 2 * KT, 2])
        gate_ps = psum("gate_ps", [P, D])
        net_ps = psum("net_ps", [FW, 2, BANK])
        tr = psum("tr", [P, 2, BANK])

        c_in, net_in, small_in, silu_done, wide_done = (sem(n) for n in ("c_in", "net_in", "small_in", "silu_done", "wide_done"))
        ada_in = [sem(f"ada_in{i}") for i in range(RING)]
        x_in = [sem(f"x_in{i}") for i in range(2)]
        ada_used, mod_done, mod_ready, v_step = (sem(n) for n in ("ada_used", "mod_done", "mod_ready", "p_v_step"))
        net_mm, net_out, net_ang, sin_done = (sem(n) for n in ("net_mm", "net_out", "net_ang", "sin_done"))
        sq_done, rstd_done, x_scaled, tr_done, tr_used, pool_step, hi_done, lo_done = (
            sem(n) for n in ("sq_done", "rstd_done", "x_scaled", "tr_done", "tr_used", "pool_step", "hi_done", "lo_done"))
        tiles = [4, 4, 4, 4, NC_CTX]
        x_dram = [t["x"][0].rearrange("(g a p) d -> g p a d", a=4, p=P)[g] for g in range(4)]
        x_dram.append(t["ctx"][0].rearrange("(a p) d -> p a d", p=P))
        block = ph.enter_context(nc.Block())

        @block.sync
        def _(sp):
            with nc.allow_non_contiguous_dma(reason="small vectors by column"):
                sp.dma_start(c_col[:, :, 0], t["c"][0].rearrange("(k p) -> p k", p=P)).then_inc(c_in, 16)
                sp.dma_start(c_col[:, :, 1], t["c_ctx"].rearrange("(k p) -> p k", p=P)).then_inc(c_in, 16)
            ada_k = t["ada_w"][0].rearrange("(k p) n -> k p n", p=P)
            for k in range(KT):
                if k >= RING:
                    sp.wait_ge(ada_used, k - RING + 1)
                sp.dma_start(ada[:, k % RING], ada_k[k]).then_inc(ada_in[k % RING], 16)
                if k == RING - 1:
                    for g in range(2):
                        sp.dma_start(xg[:, g], x_dram[g]).then_inc(x_in[g], 16)
            for g in range(2, 5):
                sp.wait_ge(tr_done, KT * (g - 1))
                sp.dma_start(xg[:, g % 2, 0:tiles[g]], x_dram[g]).then_inc(x_in[g % 2], 16)

        @block.gpsimd
        def _(pool):
            with nc.allow_non_contiguous_dma(reason="small vectors by column"):
                pool.dma_start(feats, t["k_feats"]).then_inc(net_in, 16)
                pool.dma_start(w1[:], t["filt_w1"][0]).then_inc(net_in, 16)
                pool.dma_start(w23[:, 0], t["filt_w2"][0]).then_inc(net_in, 16)
                pool.dma_start(w23[:, 1], t["filt_w3"][0]).then_inc(net_in, 16)
                for n in range(3):
                    pool.dma_start(fb[:, n:n + 1], t[f"filt_b{n + 1}"].rearrange("a c -> c a")).then_inc(net_in, 16)
                pool.dma_start(freq[:], t["filt_freq"].rearrange("a c -> c a")).then_inc(net_in, 16)
                pool.dma_start(eye[:], t["k_eye"]).then_inc(small_in, 16)
                pool.dma_start(norm_w[:], t["norm_w"][0].rearrange("(k p) -> p k", p=P)).then_inc(small_in, 16)
                pool.dma_start(ada_b_col[:], t["ada_b"][0, 0:2 * D].rearrange("(k p) -> p k", p=P)).then_inc(small_in, 16)
                pool.dma_start(ada_b_gate, t["ada_b"][0, 2 * D:3 * D].partition_broadcast(P)).then_inc(small_in, 16)
            step = chained(pool, pool_step)
            step(pool.memset(halves[:], -0.5))
            for g in range(5):
                a = slice(4 * g, 4 * g + tiles[g])
                pool.wait_ge(sq_done, 4 * g + tiles[g])
                step(pool.tensor_scalar(rstd[:, a], ss[:, a], 1.0 / D, EPS, ALU.mult, ALU.add))
                pool.tensor_tensor(rstd[:, a], rstd[:, a], halves[:, a], ALU.pow).then_inc(rstd_done, 1)

        @block.scalar
        def _(act):
            def squares_of(g):
                act.wait_ge(x_in[g % 2], 16 * (g // 2 + 1))
                for a in range(tiles[g]):
                    n = 4 * g + a
                    act.activation(squares, xg[:, g % 2, a], ACT.Square, accum_out=ss[:, n:n + 1]).then_inc(sq_done, 1)
                    act.wait_ge(sq_done, n + 1)

            def sines(layer):
                act.wait_ge(net_ang, layer + 1)
                act.activation(hT[:, 0:SEQ], ang[:], ACT.Sin).then_inc(sin_done, 1)

            def modulate(g):
                r = 0 if g < 4 else 1
                for k in range(KT):
                    w = P * tiles[g]
                    act.wait_ge(tr_done, KT * g + k + 1)
                    n = KT * g + k
                    if n >= 2:
                        act.wait_ge(lo_done, n - 1)
                    act.activation(xn[:, k % 2, 0:w], tr[:, k % 2, 0:w], ACT.Identity,
                                   bias=mod[:, 0, r, k:k + 1], scale=mod[:, 1, r, k:k + 1]).then_inc(tr_used, 1)

            act.wait_ge(c_in, 32)
            act.activation(s_col[:], c_col[:], ACT.Silu).then_inc(silu_done, 1)
            sines(0)
            squares_of(0)
            squares_of(1)
            sines(1)
            act.wait_ge(mod_ready, 1)
            modulate(0)
            squares_of(2)
            modulate(1)
            squares_of(3)
            sines(2)
            modulate(2)
            squares_of(4)
            modulate(3)
            modulate(4)

        @block.tensor
        def _(pe):
            def net(layer):
                w = w1[:] if layer == 0 else w23[:, layer - 1]
                if layer:
                    pe.wait_ge(sin_done, layer)
                for c in range(4):
                    n = 4 * layer + c
                    if n >= 2:
                        pe.wait_ge(net_out, n - 1)
                    src = feats if layer == 0 else hT[:]
                    pe.matmul(net_ps[:, n % 2], w, src[:, c * BANK:(c + 1) * BANK], start=True, stop=True).then_inc(net_mm, 1)

            def transposes(g):
                pe.wait_ge(x_scaled, g + 1)
                for k in range(KT):
                    n = KT * g + k
                    if n >= 2:
                        pe.wait_ge(tr_used, n - 1)
                    for a in range(tiles[g]):
                        ins = pe.transpose(tr[:, n % 2, a * P:(a + 1) * P], xg[:, g % 2, a, k * P:(k + 1) * P], eye[:])
                    ins.then_inc(tr_done, 1)

            pe.wait_ge(net_in, 16 * 8)
            net(0)
            pe.wait_ge(wide_done, 1)
            for k in range(KT):
                pe.wait_ge(ada_in[k % RING], 16 * (k // RING + 1))
                for m in range(2 * KT):
                    pe.matmul(mod_ps[:, m], ada[:, k % RING, m * P:(m + 1) * P], s_col[:, k],
                              start=(k == 0 and m == 0), stop=(k == KT - 1 and m == 2 * KT - 1), skip_group_check=True)
                for h in range(2):
                    ins = pe.matmul(gate_ps[:, h * BANK:(h + 1) * BANK], s_wide[:, k],
                                    ada[:, k % RING, 2 * D + h * BANK:2 * D + (h + 1) * BANK], start=(k == 0), stop=(k == KT - 1))
                ins.then_inc(ada_used, 1)
            net(1)
            pe.wait_ge(small_in, 64)
            transposes(0)
            transposes(1)
            net(2)
            for g in range(2, 5):
                transposes(g)

        @block.vector
        def _(dve):
            step = chained(dve, v_step)

            def angles(layer):
                for c in range(4):
                    n = 4 * layer + c
                    dve.wait_ge(net_mm, n + 1)
                    dve.tensor_scalar(ang[:, c * BANK:(c + 1) * BANK], net_ps[:, n % 2], fb[:, layer:layer + 1], freq[:, 0:1],
                                      ALU.add, ALU.mult).then_inc(net_out, 1)
                dve.wait_ge(net_out, 4 * layer + 4)
                step(dve.tensor_scalar(turns, ang[:], 1.0 / TWO_PI, ROUNDER, ALU.mult, ALU.add))
                step(dve.tensor_scalar(turns, turns, -ROUNDER, None, ALU.add))
                for part in (PI_A, PI_B, PI_C):
                    step(dve.scalar_tensor_tensor(ang[:], turns, -part, ang[:], ALU.mult, ALU.add))
                dve.tensor_scalar(ang[:], ang[:], PI, -PI, ALU.min, ALU.max).then_inc(net_ang, 1)

            def scale_tokens(g):
                dve.wait_ge(rstd_done, g + 1)
                for a in range(tiles[g]):
                    n = 4 * g + a
                    ins = dve.tensor_scalar(xg[:, g % 2, a], xg[:, g % 2, a], rstd[:, n:n + 1], None, ALU.mult)
                ins.then_inc(x_scaled, 1)

            def split(g):
                hi, lo = parts[g // 4]
                at = BANK * (g % 4)
                for k in range(KT):
                    n, w = KT * g + k, P * tiles[g]
                    cols = slice(at, at + w)
                    dve.wait_ge(tr_used, n + 1)
                    dve.tensor_copy(hi[:, k, cols], xn[:, k % 2, 0:w]).then_inc(hi_done, 1)
                    dve.wait_ge(hi_done, n + 1)
                    dve.tensor_tensor(lo[:, k, cols], xn[:, k % 2, 0:w], hi[:, k, cols].bitcast(F32), ALU.subtract).then_inc(lo_done, 1)

            dve.memset(hT[:, SEQ:SEQ + 1], 0.0)
            dve.wait_ge(silu_done, 1)
            dve.tensor_copy(s_wide, s_col[:, :, 0:1].to_broadcast([P, KT, P])).then_inc(wide_done, 1)
            dve.wait_ge(net_in, 16 * 8)
            angles(0)
            dve.wait_ge(ada_used, KT)
            dve.wait_ge(small_in, 64)
            for r in range(2):
                step(dve.tensor_tensor(mod[:, 0, r], mod_ps[:, 0:KT, r], ada_b_col[:, 0:KT], ALU.add))
                step(dve.tensor_tensor(mod[:, 1, r], mod_ps[:, KT:2 * KT, r], ada_b_col[:, KT:2 * KT], ALU.add))
                step(dve.scalar_tensor_tensor(mod[:, 1, r], mod[:, 1, r], 1.0, norm_w[:], ALU.add, ALU.mult))
            dve.tensor_tensor(gate_row[:], gate_ps[:], ada_b_gate, ALU.add).then_inc(mod_ready, 1)
            angles(1)
            scale_tokens(0)
            scale_tokens(1)
            split(0)
            split(1)
            angles(2)
            scale_tokens(2)
            scale_tokens(3)
            split(2)
            scale_tokens(4)
            split(3)
            split(4)


def filter_first_stage(nc, t, keep):
    with ExitStack() as ph:
        def sem(name):
            return nc.alloc_semaphore(name)

        def sb(name, shape, dt=F32):
            return ph.enter_context(nc.sbuf_tensor("f_" + name, shape, dt))

        def psum(name, shape):
            return ph.enter_context(nc.psum_tensor("f_" + name, shape, F32))

        hT = keep["hT"]
        w4 = sb("w4", [FW, 2, D])
        fwd = sb("fwd", [P, 2, 2, P])
        deltas = sb("deltas", [P, D])
        mt = sb("mt", [P, RIN, 2])
        mt_now = sb("mt_now", [P, 2])
        h_now = sb("h_now", [FW, 2, P])
        window = sb("window", [P, 2, 2, BANK])
        taps = sb("taps", [P, 2, 2, BANK])
        out = sb("out", [P, 2, 2, BANK])
        h_ps = psum("h_ps", [P, 2, 2, BANK])
        f_ps = psum("f_ps", [P, 2, 2, BANK])
        w_in_, net_now, mt_done, h_mm, win_done, taps_done, f_mm = (
            sem(n) for n in ("f_consts", "f_net_now", "f_mt_done", "f_h_mm", "f_win_done", "f_taps_done", "f_mm"))
        out_re, out_im = sem("f_out_re"), sem("f_out_im")
        stored = [sem(f"f_stored{h}") for h in range(2)]
        block = ph.enter_context(nc.Block())

        @block.sync
        def _(sp):
            sp.dma_start(w4[:], t["filt_w4"][0].rearrange("p (s d) -> p s d", s=2)).then_inc(w_in_, 16)
            sp.dma_start(fwd[:], t["k_fwd"]).then_inc(w_in_, 16)
            sp.dma_start(deltas[:], t["k_deltas"][0].partition_broadcast(P)).then_inc(w_in_, 16)
            sp.dma_start(mt[:], t["k_mt"]).then_inc(w_in_, 16)
            lead(sp, *stored, unit=16)
            with sp.Fori(0, RIN) as n2:
                for h in range(2):
                    sp.wait_ge(out_re, nth(2 * n2 + h))
                    sp.wait_ge(out_im, nth(2 * n2 + h))
                    sp.dma_start(t["f_spec"][n2][:, :, h * BANK:(h + 1) * BANK].rearrange("r k c -> k r c"),
                                 out[:, h]).then_inc(stored[h], 16)
            for h in range(2):
                sp.wait_ge(stored[h], nth(RIN - 1, 16))

        @block.tensor
        def _(pe):
            lead(pe, h_mm, f_mm)
            pe.wait_ge(w_in_, 64)
            with pe.Fori(0, RIN) as n2:
                pe.wait_ge(net_now, n2 + 1)
                for h in range(2):
                    for s in range(2):
                        ins = pe.matmul(h_ps[:, h, s], h_now[:, s], w4[:, s, h * BANK:(h + 1) * BANK], start=True, stop=True)
                    ins.then_inc(h_mm, 1)
                for h in range(2):
                    n = 2 * n2 + h
                    pe.wait_ge(taps_done, nth(n))
                    pe.wait_ge(out_re, nth(n - 2))
                    pe.wait_ge(out_im, nth(n - 2))
                    for r in range(2):
                        for s in range(2):
                            ins = pe.matmul(f_ps[:, h, r], fwd[:, s, r], taps[:, h, s], start=(s == 0), stop=(s == 1))
                    ins.then_inc(f_mm, 1)

        @block.scalar
        def _(act):
            lead(act, win_done, out_re)
            act.wait_ge(w_in_, 64)
            with act.Fori(0, RIN) as n2:
                act.wait_ge(mt_done, n2 + 1)
                for h in range(2):
                    act.wait_ge(taps_done, nth(2 * n2 + h - 2))
                    for s in range(2):
                        ins = act.activation(window[:, h, s], deltas[:, h * BANK:(h + 1) * BANK], ACT.Exp, scale=mt_now[:, s:s + 1])
                    ins.then_inc(win_done, 1)
                for h in range(2):
                    n = 2 * n2 + h
                    act.wait_ge(f_mm, nth(n))
                    act.wait_ge(stored[h], nth(n2 - 1, 16))
                    act.activation(out[:, h, 0], f_ps[:, h, 0], ACT.Copy).then_inc(out_re, 1)

        @block.vector
        def _(dve):
            lead(dve, taps_done, out_im)
            dve.wait_ge(w_in_, 64)
            with dve.Fori(0, RIN) as n2:
                dve.wait_ge(h_mm, nth(2 * n2 - 1))
                dve.tensor_copy(h_now[:, 0], hT[:, bass.ds(n2, P, step=RIN)])
                dve.tensor_copy(h_now[:, 1], hT[:, bass.ds(RIN - n2, P, step=RIN)]).then_inc(net_now, 1)
                dve.wait_ge(win_done, nth(2 * n2 - 1))
                dve.tensor_copy(mt_now[:], mt[:, bass.ds(n2, 1)].rearrange("p a s -> p (a s)")).then_inc(mt_done, 1)
                for h in range(2):
                    n = 2 * n2 + h
                    dve.wait_ge(h_mm, nth(n))
                    dve.wait_ge(win_done, nth(n))
                    dve.wait_ge(f_mm, nth(n - 2))
                    for s in range(2):
                        ins = dve.tensor_tensor(taps[:, h, s], h_ps[:, h, s], window[:, h, s], ALU.mult)
                    ins.then_inc(taps_done, 1)
                for h in range(2):
                    n = 2 * n2 + h
                    dve.wait_ge(f_mm, nth(n))
                    dve.wait_ge(stored[h], nth(n2 - 1, 16))
                    dve.tensor_copy(out[:, h, 1], f_ps[:, h, 1]).then_inc(out_im, 1)
def conv_taps(dve, step, tile, ps, taps, rows, width):
    a = tile.rearrange("p (r w) -> p r w", w=width)
    b = ps.rearrange("p (r w) -> p r w", w=width)
    step(dve.scalar_tensor_tensor(a[:, :, 1:width], b[:, :, 0:width - 1], taps[:, 0:1], a[:, :, 1:width], ALU.mult, ALU.add))
    return dve.scalar_tensor_tensor(a[:, :, 0:width - 1], b[:, :, 1:width], taps[:, 2:3], a[:, :, 0:width - 1], ALU.mult, ALU.add)


def split_weights(eng, parts, raw, hi_done, count):
    eng.tensor_copy(parts[:, 0], raw).then_inc(hi_done, 1)
    eng.wait_ge(hi_done, count)
    return eng.tensor_tensor(parts[:, 1], raw, parts[:, 0].bitcast(F32), ALU.subtract)


def project_hyena(nc, t, keep):
    with ExitStack() as ph:
        def sem(name):
            return nc.alloc_semaphore(name)

        def sb(name, shape, dt=F32):
            return ph.enter_context(nc.sbuf_tensor("h_" + name, shape, dt))

        def psum(name, shape):
            return ph.enter_context(nc.psum_tensor("h_" + name, shape, F32))

        x, eye = (keep["x_hi"], keep["x_lo"]), keep["eye"]
        HY_T = D // P
        KINDS = (COL_HY + D, COL_HY + 2 * D, COL_HY, COL_ZH)
        CONV_AT = (1, 2, 0)
        w_raw = sb("w_raw", [P, KT, P])
        w = sb("w", [P, 2, 2, KT, P], F32R)
        taps = sb("taps", [P, 3, HY_T, 4])
        taps_now = sb("taps_now", [P, 3, 4])
        fwd = sb("fwd", [P, 2, P])
        part = sb("part", [P, 4, SEQ])
        vv, gate = part[:, 0], part[:, 2]
        u = sb("u", [P, RIN, P])
        spec = sb("spec", [P, 2, 2, 4 * P])
        pj = psum("pj", [P, 4, BANK])
        tr = psum("tr", [P, 2, BANK])
        st = psum("st", [P, 2, BANK])
        w_in_ = [sem(f"h_w_in{j}") for j in range(2)]
        w_hi_done, w_split, passed = sem("h_w_hi_done"), sem("h_w_split"), sem("h_passed")
        consts, taps_ready, pj_mm, cv_mid, cv_side, cv_done, z_done, vv_done, gate_done = (sem("h_" + n) for n in (
            "consts", "taps_ready", "pj_mm", "cv_mid", "cv_side", "cv_done", "z_done", "vv_done", "gate_done"))
        tr_mm, u_done, st_mm, re_done, im_done, vv_out, gate_out = (sem("h_" + n) for n in (
            "tr_mm", "u_done", "st_mm", "re_done", "im_done", "vv_out", "gate_out"))
        spec_out = [sem(f"h_spec_out{s}") for s in range(2)]
        w_cols = t["w_in"][0].rearrange("(k p) n -> p k n", p=P)
        block = ph.enter_context(nc.Block())

        @block.gpsimd
        def _(pool):
            def load(c, j):
                pool.dma_start(w_raw[:], w_cols[:, :, bass.ds(KINDS[j] + c * P, P)]).then_inc(w_in_[j % 2], 16)

            def split(c, j):
                pool.wait_ge(w_in_[j % 2], 16 * (2 * c + j // 2) + 16)
                pool.wait_ge(pj_mm, nth(16 * c + 4 * (j - 2) + 3))
                pool.sem_inc(passed, 1)
                split_weights(pool, w[:, j % 2], w_raw[:], w_hi_done, 4 * c + j + 1).then_inc(w_split, 1)
                pool.wait_ge(w_split, 4 * c + j + 1)

            load(0, 0)
            with pool.Fori(0, HY_T - 1) as c:
                for j in range(4):
                    split(c, j)
                    load(c + (j + 1) // 4, (j + 1) % 4)
            for j in range(4):
                split(HY_T - 1, j)
                if j < 3:
                    load(HY_T - 1, j + 1)

        @block.sync
        def _(sp):
            with nc.allow_non_contiguous_dma(reason="taps by channel"):
                for a in range(3):
                    cols = slice(a * D, (a + 1) * D)
                    for k in range(3):
                        sp.dma_start(taps[:, a, :, k], t["hy_conv_w"][0, k, cols].rearrange("(m p) -> p m", p=P)).then_inc(consts, 16)
                    sp.dma_start(taps[:, a, :, 3], t["hy_conv_b"][0, cols].rearrange("(m p) -> p m", p=P)).then_inc(consts, 16)
                sp.dma_start(fwd[:], t["k_fwd"][:, 0]).then_inc(consts, 16)
            lead(sp, vv_out, gate_out, unit=16)
            lead(sp, *spec_out, unit=64)
            with sp.Fori(0, HY_T) as c:
                sp.wait_ge(vv_done, nth(c))
                sp.dma_start(t["vv_t"][c], vv).then_inc(vv_out, 16)
                sp.wait_ge(gate_done, nth(c))
                sp.dma_start(t["gate_t"][c], gate).then_inc(gate_out, 16)
                for n in range(4):
                    sp.wait_ge(re_done, nth(4 * c + n))
                    sp.wait_ge(im_done, nth(4 * c + n))
                    for r in range(2):
                        sp.dma_start(t["u_spec"][4 * n:4 * n + 4, r, :, bass.ds(c * P, P)].rearrange("n k c -> k n c"),
                                     spec[:, n % 2, r].rearrange("k (n c) -> k n c", n=4)).then_inc(spec_out[n % 2], 16)
            sp.wait_ge(vv_out, nth(HY_T - 1, 16))
            sp.wait_ge(gate_out, nth(HY_T - 1, 16))
            for s in range(2):
                sp.wait_ge(spec_out[s], nth(HY_T - 1, 64))

        @block.tensor
        def _(pe):
            lead(pe, pj_mm, tr_mm, st_mm)
            pe.wait_ge(consts, 16 * 13)
            with pe.Fori(0, HY_T) as c:
                for j in range(4):
                    pe.wait_ge(w_split, 4 * c + j + 1)
                    for q in range(4):
                        if j == 0:
                            pe.wait_ge(z_done, nth(4 * (c - 1) + q))
                        else:
                            pe.wait_ge(cv_done, nth(12 * c + 4 * (j - 1) + q))
                        weights = [lambda k, j=j, a=a: w[:, j % 2, a, k] for a in range(2)]
                        product(pe, pj[:, q], weights, x, q * BANK, BANK, KT).then_inc(pj_mm, 1)
                    if j == 2:
                        pe.wait_ge(vv_done, nth(c))
                        for n in range(4):
                            pe.wait_ge(u_done, nth(4 * c + n - 2))
                            for a in range(4):
                                ins = pe.transpose(tr[:, n % 2, a * P:(a + 1) * P], vv[:, 4 * n + a::RIN], eye[:])
                            ins.then_inc(tr_mm, 1)
                for n in range(4):
                    pe.wait_ge(u_done, nth(4 * c + n))
                    pe.wait_ge(re_done, nth(4 * c + n - 1))
                    pe.wait_ge(im_done, nth(4 * c + n - 1))
                    for r in range(2):
                        ins = pe.matmul(st[:, r], fwd[:, r], u[:, 4 * n:4 * n + 4].rearrange("p a c -> p (a c)"), start=True, stop=True)
                    ins.then_inc(st_mm, 1)

        @block.scalar
        def _(act):
            lead(act, z_done, u_done, re_done, cv_mid)
            act.wait_ge(consts, 16 * 13)
            with act.Fori(0, HY_T) as c:
                act.wait_ge(taps_ready, c + 1)
                for j in range(4):
                    if j == 0:
                        act.wait_ge(tr_mm, nth(4 * (c - 1) + 3))
                        act.wait_ge(vv_out, nth(c - 1, 16))
                    elif j == 1:
                        act.wait_ge(vv_done, nth(c - 1))
                    elif j == 2:
                        act.wait_ge(gate_out, nth(c - 1, 16))
                    else:
                        act.wait_ge(gate_done, nth(c - 1))
                    for q in range(4):
                        act.wait_ge(pj_mm, nth(16 * c + 4 * j + q))
                        cols = part[:, j, q * BANK:(q + 1) * BANK]
                        if j == 3:
                            act.activation(cols, pj[:, q], ACT.Silu).then_inc(z_done, 1)
                        else:
                            act.activation(cols, pj[:, q], ACT.Identity, bias=taps_now[:, j, 3:4], scale=taps_now[:, j, 1:2]).then_inc(cv_mid, 1)
                    if j == 2:
                        act.wait_ge(st_mm, nth(4 * (c - 1) + 3))
                        for n in range(4):
                            act.wait_ge(tr_mm, nth(4 * c + n))
                            act.activation(u[:, 4 * n:4 * n + 4].rearrange("p a c -> p (a c)"), tr[:, n % 2], ACT.Copy).then_inc(u_done, 1)
                for n in range(4):
                    act.wait_ge(spec_out[n % 2], nth(c - 1, 64) + 32 * (n // 2))
                    act.wait_ge(st_mm, nth(4 * c + n))
                    act.activation(spec[:, n % 2, 0], st[:, 0], ACT.Copy).then_inc(re_done, 1)

        @block.vector
        def _(dve):
            lead(dve, cv_done, im_done, vv_done, gate_done)
            dve.wait_ge(consts, 16 * 13)
            with dve.Fori(0, HY_T) as c:
                dve.wait_ge(cv_mid, nth(12 * c - 1))
                dve.wait_ge(cv_done, nth(12 * c - 1))
                for j in range(3):
                    ins = dve.tensor_copy(taps_now[:, j], taps[:, CONV_AT[j], bass.ds(c, 1)].rearrange("p a k -> p (a k)"))
                ins.then_inc(taps_ready, 1)
                step = chained(dve, cv_side, 12 * c)
                dve.wait_ge(taps_ready, c + 1)
                for j in range(3):
                    for q in range(4):
                        n = 12 * c + 4 * j + q
                        dve.wait_ge(cv_mid, nth(n))
                        conv_taps(dve, step, part[:, j, q * BANK:(q + 1) * BANK], pj[:, q], taps_now[:, j], BANK // GRID_W, GRID_W).then_inc(cv_done, 1)
                    if j == 1:
                        dve.wait_ge(cv_done, nth(12 * c + 7))
                        dve.tensor_tensor(vv, part[:, 0], part[:, 1], ALU.mult).then_inc(vv_done, 1)
                dve.wait_ge(cv_done, nth(12 * c + 11))
                dve.wait_ge(z_done, nth(4 * c + 3))
                dve.tensor_tensor(gate, part[:, 2], part[:, 3], ALU.mult).then_inc(gate_done, 1)
                for n in range(4):
                    dve.wait_ge(spec_out[n % 2], nth(c - 1, 64) + 32 * (n // 2))
                    dve.wait_ge(st_mm, nth(4 * c + n))
                    dve.tensor_copy(spec[:, n % 2, 1], st[:, 1]).then_inc(im_done, 1)


def project_ssd(nc, t, keep):
    project_xbc(nc, t, keep, "s", 0, D // P, True)
    project_xbc(nc, t, keep, "b", D // P, XBC_T - D // P, False)


def project_xbc(nc, t, keep, pre, first, tiles, with_z):
    with ExitStack() as ph:
        def sem(name):
            return nc.alloc_semaphore(name)

        def sb(name, shape, dt=F32):
            return ph.enter_context(nc.sbuf_tensor(f"{pre}_{name}", shape, dt))

        def psum(name, shape):
            return ph.enter_context(nc.psum_tensor(f"{pre}_{name}", shape, F32))

        x, cx, eye, dt_raw = (keep["x_hi"], keep["x_lo"]), (keep["c_hi"], keep["c_lo"]), keep["eye"], keep["dt_raw"]
        MM = 9 if with_z else 5
        CONSTS = 16 * (4 if with_z else 5)
        QUADS = (NCH + 3) // 4
        KINDS = 2 if with_z else 1
        w_raw = sb("w_raw", [P, KT, P])
        w = sb("w", [P, 2, 2, KT, P], F32R)
        taps = sb("taps", [P, tiles, 4])
        taps_now = sb("taps_now", [P, 4])
        conv = sb("conv", [P, TOK])
        xt = sb("xt", [P, TOK])
        zt = sb("zt", [P, SEQ]) if with_z else None
        xk = sb("xk", [P, NCH, P])
        if not with_z:
            w_dt = sb("w_dt", [P, KT, 2 * HEADS])
            w_dt_parts = sb("w_dt_parts", [P, 2, KT, 2 * HEADS], F32R)
        dtT = conv[0:2 * HEADS]
        pj = psum("pj", [P, 4, BANK])
        pc = psum("pc", [P, BANK])
        tr = psum("tr", [P, 2, BANK])
        w_in_ = [sem(f"{pre}_w_in{s}") for s in range(2)]
        w_hi_done, w_split, w_dt_hi, w_dt_split, passed = (sem(f"{pre}_{n}") for n in (
            "w_hi_done", "w_split", "w_dt_hi", "w_dt_split", "passed"))
        consts, taps_ready, mm, cv_mid, cv_side, cv_done, x_done, z_done = (sem(f"{pre}_{n}") for n in (
            "consts", "taps_ready", "mm", "cv_mid", "cv_side", "cv_done", "x_done", "z_done"))
        tr_mm, xk_done, xt_out, xk_out, z_out, dt_done, dt_tr, dt_copied = (sem(f"{pre}_{n}") for n in (
            "tr_mm", "xk_done", "xt_out", "xk_out", "z_out", "dt_done", "dt_tr", "dt_copied"))
        w_cols = t["w_in"][0].rearrange("(k p) n -> p k n", p=P)
        block = ph.enter_context(nc.Block())
        chunks = [(q, q * BANK, BANK) for q in range(4)] + [(4, SEQ, CTX)]

        def bank(q):
            return pj[:, q] if q < 4 else pc[:, 0:CTX]

        @block.gpsimd
        def _(pool):
            def column(c, s):
                return (COL_XBC, COL_ZS)[s] + c * P if with_z else COL_XBC + (first + 2 * c + s) * P

            def load(c, s):
                pool.dma_start(w_raw[:], w_cols[:, :, bass.ds(column(c, s), P)]).then_inc(w_in_[s], 16)

            def split(c, s):
                pool.wait_ge(w_in_[s], 16 * c + 16)
                pool.wait_ge(mm, nth(MM * (c - 1) + (4, 8)[s]) if with_z else nth(5 * (2 * c + s - 2) + 4))
                pool.sem_inc(passed, 1)
                split_weights(pool, w[:, s], w_raw[:], w_hi_done, 2 * c + s + 1).then_inc(w_split, 1)
                pool.wait_ge(w_split, 2 * c + s + 1)

            ROUNDS = tiles if with_z else tiles // 2
            load(0, 0)
            if not with_z:
                pool.wait_ge(consts, CONSTS)
                split_weights(pool, w_dt_parts, w_dt[:], w_dt_hi, 1).then_inc(w_dt_split, 1)
            with pool.Fori(0, ROUNDS - 1) as c:
                for s in range(2):
                    split(c, s)
                    load(c + s, 1 - s)
            split(ROUNDS - 1, 0)
            load(ROUNDS - 1, 1)
            split(ROUNDS - 1, 1)

        @block.sync
        def _(sp):
            with nc.allow_non_contiguous_dma(reason="taps by channel"):
                cols = slice(first * P, (first + tiles) * P)
                for k in range(3):
                    sp.dma_start(taps[:, :, k], t["ssd_conv_w"][0, k, cols].rearrange("(m p) -> p m", p=P)).then_inc(consts, 16)
                sp.dma_start(taps[:, :, 3], t["ssd_conv_b"][0, cols].rearrange("(m p) -> p m", p=P)).then_inc(consts, 16)
                if not with_z:
                    sp.dma_start(w_dt[:], w_cols[:, :, COL_DT:COL_DT + 2 * HEADS]).then_inc(consts, 16)
            lead(sp, xt_out, xk_out, z_out, unit=16)
            with sp.Fori(0, tiles) as c:
                sp.wait_ge(x_done, nth(c))
                sp.dma_start(t["xbc_t"][first + c], xt[:]).then_inc(xt_out, 16)
                if with_z:
                    sp.wait_ge(z_done, nth(4 * c + 3))
                    sp.dma_start(t["zs_t"][c], zt[:]).then_inc(z_out, 16)
                sp.wait_ge(xk_done, nth(QUADS * c + QUADS - 1))
                sp.dma_start(t["xbc"][:, :, bass.ds((first + c) * P, P)].rearrange("n p c -> p n c"), xk[:]).then_inc(xk_out, 16)
            sp.wait_ge(xt_out, nth(tiles - 1, 16))
            sp.wait_ge(xk_out, nth(tiles - 1, 16))
            if with_z:
                sp.wait_ge(z_out, nth(tiles - 1, 16))

        @block.tensor
        def _(pe):
            lead(pe, mm, tr_mm)
            pe.wait_ge(consts, CONSTS)

            def tile(c, s, before):
                pe.wait_ge(w_split, 2 * c + 1 if with_z else c + 1)
                weights = [lambda k, a=a: w[:, s, a, k] for a in range(2)]
                for q, at, width in chunks:
                    if q < 4 and with_z:
                        pe.wait_ge(z_done, nth(4 * (c - 1) + q))
                    else:
                        pe.wait_ge(cv_done, nth(5 * (c - 1) + q))
                    src = x if q < 4 else cx
                    product(pe, bank(q), weights, src, at if q < 4 else 0, width, KT).then_inc(mm, 1)
                if before:
                    transposes(c - 1)
                if with_z:
                    pe.wait_ge(w_split, 2 * c + 2)
                    weights = [lambda k, a=a: w[:, 1, a, k] for a in range(2)]
                    for q in range(4):
                        pe.wait_ge(cv_done, nth(5 * c + q))
                        product(pe, pj[:, q], weights, x, q * BANK, BANK, KT).then_inc(mm, 1)

            def transposes(c):
                pe.wait_ge(x_done, nth(c))
                for n in range(QUADS):
                    pe.wait_ge(xk_done, nth(QUADS * c + (n - 2 if n > 1 else -1)))
                    for a in range(min(4, NCH - 4 * n)):
                        m = 4 * n + a
                        ins = pe.transpose(tr[:, n % 2, a * P:(a + 1) * P], xt[:, m * P:(m + 1) * P], eye[:])
                    ins.then_inc(tr_mm, 1)

            tile(0, 0, False)
            if with_z:
                with pe.Fori(1, tiles) as c:
                    tile(c, 0, True)
            else:
                for c in range(1, tiles):
                    tile(c, c % 2, True)
            transposes(tiles - 1)
            if not with_z:
                for q, at, width in chunks:
                    pe.wait_ge(cv_done, nth(5 * tiles - 5 + q))
                    if q == 0:
                        pe.wait_ge(w_dt_split, 1)
                    weights = [lambda k, a=a: w_dt_parts[:, a, k] for a in range(2)]
                    product(pe, bank(q)[0:2 * HEADS], weights, x if q < 4 else cx, at if q < 4 else 0, width, KT).then_inc(mm, 1)
                pe.wait_ge(dt_done, 5)
                pe.wait_ge(xk_done, nth(QUADS * tiles - 1))
                for n in range(NCH):
                    ins = pe.transpose(tr[:, n // 16, 32 * (n % 16):32 * (n % 16) + 32], dtT[:, n * P:(n + 1) * P], eye[0:32, 0:32])
                ins.then_inc(dt_tr, 1)

        @block.scalar
        def _(act):
            lead(act, z_done, x_done, cv_mid)
            act.wait_ge(consts, CONSTS)
            with act.Fori(0, tiles) as c:
                act.wait_ge(taps_ready, c + 1)
                act.wait_ge(x_done, nth(c - 1))
                for q, at, width in chunks:
                    act.wait_ge(mm, nth(MM * c + q))
                    act.activation(conv[:, at:at + width], bank(q), ACT.Identity, bias=taps_now[:, 3:4], scale=taps_now[:, 1:2]).then_inc(cv_mid, 1)
                act.wait_ge(cv_done, nth(5 * c + 4))
                act.wait_ge(tr_mm, nth(QUADS * c - 1))
                act.wait_ge(xt_out, nth(c - 1, 16))
                act.activation(xt[:], conv[:], ACT.Silu).then_inc(x_done, 1)
                if with_z:
                    act.wait_ge(z_out, nth(c - 1, 16))
                    for q in range(4):
                        act.wait_ge(mm, nth(MM * c + 5 + q))
                        act.activation(zt[:, q * BANK:(q + 1) * BANK], pj[:, q], ACT.Silu).then_inc(z_done, 1)
            if not with_z:
                for q, at, width in chunks:
                    act.wait_ge(mm, nth(MM * tiles + q))
                    act.wait_ge(x_done, nth(tiles - 1))
                    act.activation(dtT[:, at:at + width], bank(q)[0:2 * HEADS], ACT.Copy).then_inc(dt_done, 1)

        @block.vector
        def _(dve):
            lead(dve, cv_done, xk_done)
            dve.wait_ge(consts, CONSTS)

            def convolve(c):
                dve.wait_ge(cv_mid, nth(5 * c - 1))
                dve.wait_ge(cv_done, nth(5 * c - 1))
                dve.tensor_copy(taps_now[:], taps[:, bass.ds(c, 1)].rearrange("p a k -> p (a k)")).then_inc(taps_ready, 1)
                dve.wait_ge(taps_ready, c + 1)
                step = chained(dve, cv_side, 5 * c)
                for q, at, width in chunks:
                    dve.wait_ge(cv_mid, nth(5 * c + q))
                    row = GRID_W if q < 4 else CTX
                    conv_taps(dve, step, conv[:, at:at + width], bank(q), taps_now, width // row, row).then_inc(cv_done, 1)

            def copies(c):
                dve.wait_ge(xk_out, nth(c - 1, 16))
                for n in range(QUADS):
                    m = min(4, NCH - 4 * n)
                    dve.wait_ge(tr_mm, nth(QUADS * c + n))
                    dve.tensor_copy(xk[:, 4 * n:4 * n + m].rearrange("p a c -> p (a c)"), tr[:, n % 2, 0:m * P]).then_inc(xk_done, 1)
            convolve(0)
            with dve.Fori(1, tiles) as c:
                convolve(c)
                copies(c - 1)
            copies(tiles - 1)
            if not with_z:
                dve.wait_ge(dt_tr, 1)
                dve.tensor_copy(dt_raw[:].rearrange("p n h -> p (n h)")[:, 0:BANK], tr[:, 0])
                dve.tensor_copy(dt_raw[:].rearrange("p n h -> p (n h)")[:, BANK:32 * NCH], tr[:, 1, 0:32 * NCH - BANK]).then_inc(dt_copied, 1)
                dve.wait_ge(dt_copied, 1)
def spectra(nc, t, keep):
    with ExitStack() as ph:
        def sem(name):
            return nc.alloc_semaphore(name)

        def sb(name, shape, dt=F32):
            return ph.enter_context(nc.sbuf_tensor("g_" + name, shape, dt))

        def psum(name, shape):
            return ph.enter_context(nc.psum_tensor("g_" + name, shape, F32))

        SLOTS = 2
        sig = sb("sig", [P, SLOTS, D])
        fil = sb("fil", [P, SLOTS, D])
        mats = sb("mats", [P, SLOTS, 5, P])
        ab = sb("ab", [P, 2, 2, BANK])
        prod = sb("prod", [P, 2, 2, BANK])
        back = sb("back", [P, SLOTS, 2, BANK])
        xab = psum("xab", [P, 2, 3, BANK])
        v_ps = psum("v_ps", [P, 2, BANK])
        loaded = [sem(f"g_loaded{s}") for s in range(SLOTS)]
        stored = [sem(f"g_stored{s}") for s in range(SLOTS)]
        x_mm, ab_done, prod_done, v_mm, v_done = (sem("g_" + n) for n in ("x_mm", "ab_done", "prod_done", "v_mm", "v_done"))
        block = ph.enter_context(nc.Block())

        def rows(name, g, r):
            return t[name][:, r, bass.ds(g * FG, FG), :].rearrange("n k c -> k n c")

        @block.gpsimd
        def _(pool):
            with pool.Fori(0, NG // SLOTS) as i:
                for s in range(SLOTS):
                    g = SLOTS * i + s
                    pool.wait_ge(v_mm, nth(2 * (g - SLOTS) + 1))
                    for r in range(2):
                        pool.dma_start(sig[64 * r:64 * r + 64, s], rows("u_spec", g, r)).then_inc(loaded[s], 16)
                        pool.dma_start(fil[64 * r:64 * r + 64, s], rows("f_spec", g, r)).then_inc(loaded[s], 16)
                    pool.dma_start(mats[:, s], t["k_mats"][g]).then_inc(loaded[s], 16)

        @block.sync
        def _(sp):
            lead(sp, *stored, unit=32)
            with sp.Fori(0, NG // SLOTS) as i:
                for s in range(SLOTS):
                    g = SLOTS * i + s
                    sp.wait_ge(v_done, nth(2 * g + 1))
                    for r in range(2):
                        sp.dma_start(rows("v_spec", g, r), back[64 * r:64 * r + 64, s].rearrange("p h c -> p (h c)")).then_inc(stored[s], 32 // 2)
            for s in range(SLOTS):
                sp.wait_ge(stored[s], nth(NG // SLOTS - 1, 32))

        @block.tensor
        def _(pe):
            lead(pe, x_mm, v_mm)

            def forward(g, s, h):
                cols = slice(h * BANK, (h + 1) * BANK)
                pe.matmul(xab[:, h, 0], mats[:, s, 0], sig[:, s, cols], start=True, stop=True)
                for m in (1, 2):
                    ins = pe.matmul(xab[:, h, m], mats[:, s, m], fil[:, s, cols], start=True, stop=True)
                ins.then_inc(x_mm, 1)

            def backward(g, s, h):
                n = 2 * g + h
                pe.wait_ge(prod_done, nth(n))
                pe.wait_ge(v_done, nth(n - 2))
                for m in range(2):
                    ins = pe.matmul(v_ps[:, h], mats[:, s, 3 + m], prod[:, h, m], start=(m == 0), stop=(m == 1))
                ins.then_inc(v_mm, 1)

            with pe.Fori(0, NG // SLOTS) as i:
                g = SLOTS * i
                pe.wait_ge(loaded[0], 80 * i + 80)
                forward(g, 0, 0)
                forward(g, 0, 1)
                backward(g, 0, 0)
                pe.wait_ge(loaded[1], 80 * i + 80)
                forward(g + 1, 1, 0)
                backward(g, 0, 1)
                forward(g + 1, 1, 1)
                backward(g + 1, 1, 0)
                backward(g + 1, 1, 1)

        @block.scalar
        def _(act):
            lead(act, ab_done, v_done)

            def filter_parts(n, h):
                act.wait_ge(x_mm, nth(n))
                act.wait_ge(prod_done, nth(n - 2))
                act.activation(ab[:, h], xab[:, h, 1:3], ACT.Copy).then_inc(ab_done, 1)

            def keep_back(n, i, s, h):
                act.wait_ge(v_mm, nth(n))
                act.wait_ge(stored[s], nth(i - 1, 32))
                act.activation(back[:, s, h], v_ps[:, h], ACT.Copy).then_inc(v_done, 1)

            with act.Fori(0, NG // SLOTS) as i:
                n = 2 * SLOTS * i
                filter_parts(n, 0)
                filter_parts(n + 1, 1)
                filter_parts(n + 2, 0)
                keep_back(n, i, 0, 0)
                filter_parts(n + 3, 1)
                keep_back(n + 1, i, 0, 1)
                keep_back(n + 2, i, 1, 0)
                keep_back(n + 3, i, 1, 1)

        @block.vector
        def _(dve):
            lead(dve, prod_done)
            with dve.Fori(0, NG // SLOTS) as i:
                for s in range(SLOTS):
                    for h in range(2):
                        n = 2 * SLOTS * i + 2 * s + h
                        dve.wait_ge(ab_done, nth(n))
                        dve.wait_ge(v_mm, nth(n - 2))
                        dve.tensor_tensor(prod[:, h, 0], xab[:, h, 0], ab[:, h, 0], ALU.mult)
                        dve.tensor_tensor(prod[:, h, 1], xab[:, h, 0], ab[:, h, 1], ALU.mult).then_inc(prod_done, 1)


def hyena_back(nc, t, keep):
    with ExitStack() as ph:
        def sem(name):
            return nc.alloc_semaphore(name)

        def sb(name, shape, dt=F32):
            return ph.enter_context(nc.sbuf_tensor("c_" + name, shape, dt))

        def psum(name, shape):
            return ph.enter_context(nc.psum_tensor("c_" + name, shape, F32))

        ssh = keep["ssh"]
        CT, SLOTS = D // P, 2
        back = sb("back", [P, 2, P])
        skip = sb("skip", [P, CT])
        skip_now = sb("skip_now", [P, SLOTS])
        z = sb("z", [P, SLOTS, 2, RIN, P])
        vv = sb("vv", [P, SLOTS, SEQ])
        gate = sb("gate", [P, SLOTS, SEQ])
        y = sb("y", [P, SLOTS, SEQ])
        sq = sb("sq", [P, SEQ])
        ones = sb("ones", [P, 1])
        y_ps = psum("y_ps", [P, 4, BANK])
        s_ps = psum("s_ps", [P, BANK])
        loaded = [sem(f"c_loaded{s}") for s in range(SLOTS)]
        stored = [sem(f"c_stored{s}") for s in range(SLOTS)]
        consts, y_mm, y_sum, y_done, sq_done, s_mm, s_done, skip_done, ones_done = (sem("c_" + n) for n in (
            "consts", "y_mm", "y_sum", "y_done", "sq_done", "s_mm", "s_done", "skip_done", "ones_done"))
        block = ph.enter_context(nc.Block())

        @block.gpsimd
        def _(pool):
            with pool.Fori(0, CT // SLOTS) as i:
                for s in range(SLOTS):
                    c = SLOTS * i + s
                    pool.wait_ge(y_done, nth(c - SLOTS))
                    for r in range(2):
                        pool.dma_start(z[:, s, r], t["v_spec"][:, r, :, bass.ds(c * P, P)].rearrange("n k c -> k n c")).then_inc(loaded[s], 16)
                    pool.dma_start(vv[:, s], t["vv_t"][c]).then_inc(loaded[s], 16)
                    pool.dma_start(gate[:, s], t["gate_t"][c]).then_inc(loaded[s], 16)

        @block.sync
        def _(sp):
            sp.dma_start(back[:], t["k_back"]).then_inc(consts, 16)
            with nc.allow_non_contiguous_dma(reason="skips by channel"):
                sp.dma_start(skip[:], t["hy_bias"][0].rearrange("(m p) -> p m", p=P)).then_inc(consts, 16)
            lead(sp, *stored, unit=16)
            with sp.Fori(0, CT // SLOTS) as i:
                for s in range(SLOTS):
                    c = SLOTS * i + s
                    sp.wait_ge(y_done, nth(c))
                    sp.dma_start(t["yh_t"][c], y[:, s]).then_inc(stored[s], 16)
            for s in range(SLOTS):
                sp.wait_ge(stored[s], nth(CT // SLOTS - 1, 16))

        @block.tensor
        def _(pe):
            lead(pe, y_mm, s_mm)
            pe.wait_ge(consts, 32)
            pe.wait_ge(ones_done, 1)
            with pe.Fori(0, CT // SLOTS) as i:
                for s in range(SLOTS):
                    c = SLOTS * i + s
                    pe.wait_ge(loaded[s], 64 * i + 64)
                    for q in range(4):
                        pe.wait_ge(y_sum, nth(4 * (c - 1) + q))
                        for a in range(4):
                            n2 = 4 * q + a
                            for r in range(2):
                                ins = pe.matmul(y_ps[:, q, a * P:(a + 1) * P], z[:, s, r, n2], back[:, r], start=(r == 0), stop=(r == 1))
                        ins.then_inc(y_mm, 1)
                    pe.wait_ge(sq_done, nth(c))
                    pe.wait_ge(s_done, nth(c - 1))
                    for n in range(NC_LAT):
                        ins = pe.matmul(s_ps[:, n:n + 1], sq[:, n * P:(n + 1) * P], ones[:], start=True, stop=True)
                    ins.then_inc(s_mm, 1)

        @block.scalar
        def _(act):
            lead(act, sq_done)
            with act.Fori(0, CT // SLOTS) as i:
                for s in range(SLOTS):
                    c = SLOTS * i + s
                    act.wait_ge(y_done, nth(c))
                    act.wait_ge(s_mm, nth(c - 1))
                    act.activation(sq[:], y[:, s], ACT.Square).then_inc(sq_done, 1)

        @block.vector
        def _(dve):
            lead(dve, y_sum, y_done, s_done)
            dve.memset(ssh[:], 0.0)
            dve.memset(ones[:], 1.0).then_inc(ones_done, 1)
            dve.wait_ge(consts, 32)
            with dve.Fori(0, CT // SLOTS) as i:
                for s in range(SLOTS):
                    c = SLOTS * i + s
                    dve.tensor_copy(skip_now[:, s:s + 1], skip[:, bass.ds(c, 1)]).then_inc(skip_done, 1)
                    dve.wait_ge(skip_done, c + 1)
                    dve.wait_ge(loaded[s], 64 * i + 64)
                    dve.wait_ge(stored[s], nth(i - 1, 16))
                    dve.wait_ge(sq_done, nth(c - SLOTS))
                    for q in range(4):
                        dve.wait_ge(y_mm, nth(4 * c + q))
                        def tok(a):
                            return a[:, s].rearrange("p (n k) -> p k n", k=RIN)[:, 4 * q:4 * q + 4]
                        dve.scalar_tensor_tensor(tok(y), tok(vv), skip_now[:, s:s + 1], y_ps[:, q].rearrange("p (k n) -> p k n", n=P),
                                                 ALU.mult, ALU.add).then_inc(y_sum, 1)
                    dve.wait_ge(y_sum, nth(4 * c + 3))
                    dve.tensor_tensor(y[:, s], y[:, s], gate[:, s], ALU.mult).then_inc(y_done, 1)
                    dve.wait_ge(s_mm, nth(c))
                    dve.wait_ge(s_done, nth(c - 1))
                    dve.tensor_tensor(ssh[:], ssh[:], s_ps[:, 0:NC_LAT], ALU.add).then_inc(s_done, 1)
ROWS_SHAPE = [NC_LAT, 2, 3, HEADS * CHUNK]
STEPS_LN = 8


def per_head(a, n, side):
    return a[:, bass.ds(n, 1), side * HEADS:(side + 1) * HEADS].rearrange("p a h -> p (a h)").unsqueeze(2).to_broadcast([P, HEADS, HEADDIM])


def by_head(a):
    return a.rearrange("p (h d) -> p h d", h=HEADS)


def ssd_scales(nc, t, keep):
    with ExitStack() as ph:
        def sem(name):
            return nc.alloc_semaphore(name)

        def sb(name, shape, dt=F32):
            return ph.enter_context(nc.sbuf_tensor("q_" + name, shape, dt))

        def psum(name, shape):
            return ph.enter_context(nc.psum_tensor("q_" + name, shape, F32))

        dt, te, cd = keep["dt_raw"], keep["to_end"], keep["chunk_decay"]
        W = 2 * HEADS
        bias = sb("bias", [P, W])
        a_neg = sb("a_neg", [P, W])
        tri = sb("tri", [P, 2, P])
        ones = sb("ones", [P, P])
        e = sb("e", [P, NCH, W])
        s = sb("s", [P, NCH, W])
        q = sb("q", [P, NCH, W])
        pos = sb("pos", [P, NCH, W])
        da = sb("da", [P, NCH, W])
        rows = sb("rows", [HEADS, SEQ])
        parts = sb("parts", [HEADS, 2, 3, SEQ], BF16)
        cum_ps = psum("cum_ps", [P, 2, BANK])
        tot_ps = psum("tot_ps", [P, 2, BANK])
        row_ps = psum("row_ps", [HEADS, 4, BANK])
        consts, v_step, e_in, e_out, log_done, exp_a, da_done, sums, rows_mm, rows_used, expo, stored = (sem("q_" + n) for n in (
            "consts", "v_step", "e_in", "e_out", "log_done", "exp_a", "da_done", "sums", "rows_mm", "rows_used", "expo", "stored"))
        weights, a_ready, parts_done = sem("q_weights"), sem("q_a_ready"), sem("q_parts_done")
        block = ph.enter_context(nc.Block())

        @block.sync
        def _(sp):
            sp.dma_start(bias[:], t["dt_bias"][0].rearrange("s h -> (s h)").partition_broadcast(P)).then_inc(consts, 16)
            sp.dma_start(a_neg[:], t["a_log"][0].rearrange("s h -> (s h)").partition_broadcast(P)).then_inc(consts, 16)
            sp.dma_start(tri[:], t["k_tri"]).then_inc(consts, 16)
            sp.wait_ge(parts_done, 2)
            for side in range(2):
                for k in range(3):
                    sp.dma_start(t["rows"][:, side, k].rearrange("n (h i) -> h n i", h=HEADS),
                                 parts[:, side, k].rearrange("h (n i) -> h n i", n=NC_LAT)).then_inc(stored, 16)
            sp.wait_ge(stored, 96)

        @block.scalar
        def _(act):
            act.wait_ge(consts, 48)
            act.activation(a_neg[:], a_neg[:], ACT.Exp).then_inc(exp_a, 1)
            act.wait_ge(e_in, 1)
            act.activation(e[:], e[:], ACT.Exp).then_inc(e_out, 1)
            act.wait_ge(weights, 1)
            act.activation(te[:], te[:], ACT.Exp).then_inc(expo, 1)
            act.activation(cd[:], cd[:], ACT.Exp).then_inc(expo, 1)

        @block.tensor
        def _(pe):
            pe.wait_ge(da_done, 1)
            for side in range(2):
                cols = slice(side * HEADS, (side + 1) * HEADS)
                w = NCH * HEADS
                pe.matmul(cum_ps[:, side, 0:w], tri[:, side], da[:, :, cols], start=True, stop=True)
                ins = pe.matmul(tot_ps[:, side, 0:w], ones[:], da[:, :, cols], start=True, stop=True)
            ins.then_inc(sums, 1)
            for side in range(2):
                cols = slice(side * HEADS, (side + 1) * HEADS)
                if side:
                    pe.wait_ge(rows_used, 1)
                for n in range(NC_LAT):
                    ins = pe.matmul(row_ps[:, n // 4, (n % 4) * P:(n % 4 + 1) * P], da[:, n, cols], tri[:, side], start=True, stop=True)
                ins.then_inc(rows_mm, 1)

        @block.vector
        def _(dve):
            step = chained(dve, v_step)
            dve.memset(ones[:], 1.0)
            dve.wait_ge(consts, 48)
            step(dve.tensor_tensor(dt[:], dt[:], bias[:].unsqueeze(1).to_broadcast([P, NCH, W]), ALU.add))
            step(dve.tensor_scalar(pos[:], dt[:], 0.0, None, ALU.max))
            step(dve.tensor_scalar(e[:], dt[:], -1.0, None, ALU.mult))
            dve.tensor_tensor(e[:], e[:], dt[:], ALU.min).then_inc(e_in, 1)
            dve.wait_ge(e_out, 1)
            step(dve.tensor_scalar(s[:], e[:], 2.0, None, ALU.add))
            step(dve.reciprocal(s[:], s[:]))
            step(dve.tensor_tensor(s[:], s[:], e[:], ALU.mult))
            step(dve.tensor_tensor(q[:], s[:], s[:], ALU.mult))
            step(dve.tensor_scalar(e[:], q[:], 1.0 / (2 * STEPS_LN + 1), None, ALU.mult))
            for k in range(STEPS_LN - 1, 0, -1):
                step(dve.scalar_tensor_tensor(e[:], e[:], 1.0 / (2 * k + 1), q[:], ALU.add, ALU.mult))
            step(dve.scalar_tensor_tensor(e[:], e[:], 1.0, s[:], ALU.add, ALU.mult))
            step(dve.scalar_tensor_tensor(dt[:], e[:], 2.0, pos[:], ALU.mult, ALU.add))
            dve.wait_ge(exp_a, 1)
            step(dve.tensor_scalar(a_neg[:], a_neg[:], -1.0, None, ALU.mult))
            dve.tensor_tensor(da[:], dt[:], a_neg[:].unsqueeze(1).to_broadcast([P, NCH, W]), ALU.mult).then_inc(da_done, 1)
            dve.wait_ge(sums, 1)
            for side in range(2):
                cols = slice(side * HEADS, (side + 1) * HEADS)

                def chunks(a):
                    return a[:, side, 0:NCH * HEADS].rearrange("p (n h) -> p n h", n=NCH)
                step(dve.tensor_copy(cd[:, :, cols], chunks(tot_ps)))
                ins = dve.tensor_tensor(te[:, :, cols], cd[:, :, cols], chunks(cum_ps), ALU.subtract)
                if side == 0:
                    step(ins)
            ins.then_inc(weights, 1)
            for side in range(2):
                dve.wait_ge(rows_mm, side + 1)
                dve.tensor_copy(rows[:], row_ps[:].rearrange("p a b -> p (a b)")).then_inc(rows_used, 1)
                dve.wait_ge(rows_used, side + 1)
                step(dve.tensor_copy(parts[:, side, 0], rows[:]))
                step(dve.tensor_tensor(rows[:], rows[:], parts[:, side, 0], ALU.subtract))
                step(dve.tensor_copy(parts[:, side, 1], rows[:]))
                step(dve.tensor_tensor(rows[:], rows[:], parts[:, side, 1], ALU.subtract))
                dve.tensor_copy(parts[:, side, 2], rows[:]).then_inc(parts_done, 1)
                dve.wait_ge(parts_done, side + 1)
            dve.wait_ge(expo, 2)
            dve.tensor_tensor(te[:], te[:], dt[:], ALU.mult)


def ssd_backward_states(nc, t, keep):
    with ExitStack() as ph:
        def sem(name):
            return nc.alloc_semaphore(name)

        def sb(name, shape, dt=F32):
            return ph.enter_context(nc.sbuf_tensor("r_" + name, shape, dt))

        te, cd = keep["to_end"], keep["chunk_decay"]
        XB = D + GROUPS * STATE
        xb = sb("xb", [P, 2, XB])
        xw = sb("xw", [P, 2, D])
        h = sb("h", [P, 2, D])
        h_ps = ph.enter_context(nc.psum_tensor("r_h_ps", [P, 2, D], F32))
        loaded = [sem(f"r_loaded{s}") for s in range(2)]
        stored = [sem(f"r_stored{s}") for s in range(2)]
        xw_done, h_mm, h_decayed, h_done, h_zero, sp_passed, pool_passed, dve_passed = (sem("r_" + n) for n in (
            "xw_done", "h_mm", "h_decayed", "h_done", "h_zero", "sp_passed", "pool_passed", "dve_passed"))
        block = ph.enter_context(nc.Block())

        @block.gpsimd
        def _(pool):
            with pool.Fori(0, NCH // 2) as i:
                for s in range(2):
                    m = 2 * i + s
                    pool.wait_ge(h_mm, nth(m - 2))
                    pool.sem_inc(pool_passed, 1)
                    pool.dma_start(xb[:, s], t["xbc"][NCH - 1 - m][:, 0:XB]).then_inc(loaded[s], 16)

        @block.sync
        def _(sp):
            lead(sp, *stored, unit=16)
            with sp.Fori(0, NCH // 2) as i:
                for s in range(2):
                    m = 2 * i + s
                    sp.wait_ge(h_done, nth(m - 1))
                    sp.sem_inc(sp_passed, 1)
                    sp.dma_start(t["h_back"][NCH - 1 - m], h[:, s]).then_inc(stored[s], 16)
            for s in range(2):
                sp.wait_ge(stored[s], nth(NCH // 2 - 1, 16))

        @block.tensor
        def _(pe):
            lead(pe, h_mm)
            with pe.Fori(0, NCH // 2) as i:
                for s in range(2):
                    m = 2 * i + s
                    pe.wait_ge(loaded[s], 16 * i + 16)
                    pe.wait_ge(xw_done, nth(m))
                    pe.wait_ge(h_done, nth(m - 2))
                    for g in range(GROUPS):
                        ins = pe.matmul(h_ps[:, s, g * BANK:(g + 1) * BANK], xb[:, s, D + g * STATE:D + (g + 1) * STATE],
                                        xw[:, s, g * BANK:(g + 1) * BANK], start=True, stop=True)
                    ins.then_inc(h_mm, 1)

        @block.vector
        def _(dve):
            lead(dve, xw_done, h_decayed)
            dve.memset(h[:, 0], 0.0).then_inc(h_zero, 1)
            dve.wait_ge(h_zero, 1)
            lead(dve, h_done)
            with dve.Fori(0, NCH // 2) as i:
                for s in range(2):
                    m = 2 * i + s
                    n = NCH - 1 - m
                    dve.wait_ge(loaded[s], 16 * i + 16)
                    dve.wait_ge(h_mm, nth(m - 2))
                    dve.sem_inc(dve_passed, 1)
                    dve.tensor_tensor(by_head(xw[:, s]), by_head(xb[:, s, 0:D]), per_head(te, n, 1), ALU.mult).then_inc(xw_done, 1)
                    dve.wait_ge(stored[1 - s], nth(i - 1 + s, 16))
                    dve.sem_inc(dve_passed, 1)
                    dve.tensor_tensor(by_head(h[:, 1 - s]), by_head(h[:, s]), per_head(cd, n, 1), ALU.mult).then_inc(h_decayed, 1)
                    dve.wait_ge(h_decayed, nth(m))
                    dve.wait_ge(h_mm, nth(m))
                    dve.tensor_tensor(h[:, 1 - s], h[:, 1 - s], h_ps[:, s], ALU.add).then_inc(h_done, 1)
                    dve.wait_ge(h_done, nth(m))


def ssd_and_out(nc, t, keep):
    with ExitStack() as ph:
        def sem(name):
            return nc.alloc_semaphore(name)

        def sb(name, shape, dt=F32):
            return ph.enter_context(nc.sbuf_tensor("o_" + name, shape, dt))

        def psum(name, shape):
            return ph.enter_context(nc.psum_tensor("o_" + name, shape, F32))

        dt, te, cd, ssh, gate_row = keep["dt_raw"], keep["to_end"], keep["chunk_decay"], keep["ssh"], keep["gate_row"]
        XB = D + GROUPS * STATE
        HALF = BANK
        w_out = sb("w_out", [P, 2 * KT, D])
        gn = sb("gn", [P, 2 * KT])
        fw = sb("fw", [P, D])
        dk = sb("dk", [P, 2, KT])
        tri = sb("tri", [P, 2, P])
        ones = sb("ones", [P, 1])
        ones_b = sb("ones_b", [3, HEADDIM], BF16)
        halves = sb("halves", [P, NC_LAT])
        eps = sb("eps", [P, 1])
        xk = sb("xk", [P, 2, XB])
        bc = sb("bc", [P, 2, 2 * GROUPS, P])
        xt = sb("xt", [P, 2, KT, P])
        zs = sb("zs", [P, 2, KT, P])
        hb = sb("hb", [P, 2, D])
        yh = sb("yh", [P, KT, P])
        xres = sb("xres", [P, D])
        row_i = sb("row_i", [6, 2, HEADS * CHUNK], BF16)
        row_j = sb("row_j", [6, 2, HEADS * CHUNK], BF16)
        cbm = sb("cbm", [P, 2, GROUPS, P])
        es = sb("es", [P, HEADS, P])
        mu = sb("mu", [P, HEADS, P])
        ea = sb("ea", [P, 2, 2, HALF])
        xf = sb("xf", [P, D])
        xbk = sb("xbk", [P, D])
        xw = sb("xw", [P, D])
        h = sb("h", [P, D])
        ys = sb("ys", [P, KT, P])
        tmp = sb("tmp", [P, 2, BANK])
        sq = sb("sq", [P, KT, P])
        rs = sb("rs", [P, 4])
        o = sb("o", [P, D])
        ob = sb("ob", [P, D])
        o_ps = psum("o_ps", [P, 2, BANK])
        d_ps = psum("d_ps", [P, 2, BANK])
        in_ps = psum("in_ps", [P, 2, BANK])
        y_ps = psum("y_ps", [P, BANK])
        m_ps = psum("m_ps", [P, BANK])

        names = ("consts w_in_ w_ready prep h_zero xw_done cb_mm cbm_done s_mm dc_done dm_done e_done ml_done "
                 "r_mm y_read y_done v_step ys_done h_mm h_done sq_step sq_done sq_sum ss_mm ss_done rs_done o_mm oa_done ob_done "
                 "sp_passed o_pre fsq_done frs_done fin_done hn_done p_step rsh_done rows_set xt_done h_dec f_step")
        S = {n: sem("o_" + n) for n in names.split()}
        early = [sem(f"o_early{s}") for s in range(2)]
        ctx_in = [sem(f"o_ctx_in{s}") for s in range(2)]
        rows_in, late_in, stored = sem("o_rows_in"), sem("o_late_in"), sem("o_stored")
        EARLY = 16 * 5
        block = ph.enter_context(nc.Block())
        LAST = NC_LAT - 1

        def pairs(eng, body, head=0, count=NC_LAT // 2 - 1):
            with eng.Fori(0, count) as i:
                for j in range(2):
                    n = head + j
                    body(2 * i + n, i + n // 2, n % 2)
            for n in range(head + 2 * count, NC_LAT):
                body(n, n // 2, n % 2)

        @block.sync
        def _(sp):
            def load_early(n, s):
                sp.wait_ge(S["ys_done"], nth(2 * (n - 2) + 1))
                sp.sem_inc(S["sp_passed"], 1)
                sp.wait_ge(S["h_mm"], nth(n))
                sp.sem_inc(S["sp_passed"], 1)
                sp.dma_start(xk[:, s], t["xbc"][n][:, 0:XB]).then_inc(early[s], 16)
                cols = bass.ds(n * P, P)
                sp.dma_start(bc[:, s], t["xbc_t"][KT:XBC_T][:, :, cols].rearrange("m p t -> p m t")).then_inc(early[s], 16)
                sp.dma_start(xt[:, s], t["xbc_t"][0:KT][:, :, cols].rearrange("m p t -> p m t")).then_inc(early[s], 16)
                sp.dma_start(zs[:, s], t["zs_t"][:, :, cols].rearrange("m p t -> p m t")).then_inc(early[s], 16)
                sp.dma_start(hb[:, s], t["h_back"][n]).then_inc(early[s], 16)

            def load_rows(n):
                sp.wait_ge(S["s_mm"], nth(6 * (n - 1) + 5))
                sp.sem_inc(S["sp_passed"], 1)
                sp.wait_ge(S["rows_set"], 1)
                rows = t["rows"][n].rearrange("s k c -> k s c")
                sp.dma_start(row_i[0:3], rows).then_inc(rows_in, 16)
                sp.dma_start(row_j[3:6], rows).then_inc(rows_in, 16)

            def load_late(n):
                sp.wait_ge(S["o_mm"], nth(4 * (n - 1) + 2))
                sp.sem_inc(S["sp_passed"], 1)
                sp.wait_ge(S["o_pre"], nth(n - 1))
                sp.sem_inc(S["sp_passed"], 1)
                sp.dma_start(yh[:], t["yh_t"][:, :, bass.ds(n * P, P)].rearrange("m p t -> p m t")).then_inc(late_in, 16)
                sp.dma_start(xres[:], t["x"][0][bass.ds(n * P, P)]).then_inc(late_in, 16)

            def store(n):
                sp.wait_ge(S["fin_done"], nth(n))
                sp.sem_inc(S["sp_passed"], 1)
                sp.dma_start(t["out"][0][bass.ds(n * P, P)], ob[:]).then_inc(stored, 16)

            for s in range(2):
                sp.dma_start(xk[:, s], t["xbc"][NC_LAT + s][:, 0:XB]).then_inc(ctx_in[s], 16)
            with nc.allow_non_contiguous_dma(reason="small vectors"):
                sp.dma_start(gn[:], t["gnorm_w"][0].rearrange("(m p) -> p m", p=P)).then_inc(S["consts"], 16)
                sp.dma_start(fw[:], t["final_norm_w"].partition_broadcast(P)).then_inc(S["consts"], 16)
                for side in range(2):
                    for par in range(2):
                        sp.dma_start(dk[64 * par:64 * par + 64, side],
                                     t["d_skip"][0, side].rearrange("(m two) -> two m", two=2)[par].partition_broadcast(HEADDIM)).then_inc(S["consts"], 16)
                sp.dma_start(tri[:], t["k_tri"]).then_inc(S["consts"], 16)
            sp.dma_start(w_out[:], t["w_out"][0].rearrange("(k p) d -> p k d", p=P)).then_inc(S["w_in_"], 16)
            lead(sp, stored, unit=16)
            load_early(0, 0)
            load_rows(0)

            def body(n, i, s):
                load_early(n + 1, 1 - s)
                load_rows(n + 1)
                load_late(n)
                store(n - 1)
            load_early(1, 1)
            load_rows(1)
            load_late(0)
            with sp.Fori(0, LAST // 2) as i:
                for j in range(2):
                    n = 2 * i + 1 + j
                    body(n, None, (1 + j) % 2)
            load_late(LAST)
            store(LAST - 1)
            store(LAST)
            sp.wait_ge(stored, nth(LAST, 16))

        @block.gpsimd
        def _(pool):
            step = chained(pool, S["p_step"])
            pool.memset(halves[:], -0.5)
            pool.memset(eps[:], EPS)
            pool.memset(row_i[:], -1.0)
            step(pool.memset(row_j[:], 1.0))
            pool.sem_inc(S["rows_set"], 1)
            pool.wait_ge(S["consts"], 16 * 7)
            step(pool.tensor_tensor(dk[:, 0], dk[:, 0], dk[:, 1], ALU.add))
            step(pool.tensor_scalar(ssh[:], ssh[:], 1.0 / D, EPS, ALU.mult, ALU.add))
            pool.tensor_tensor(ssh[:], ssh[:], halves[:], ALU.pow).then_inc(S["rsh_done"], 1)
            lead(pool, S["xw_done"], S["rs_done"], S["frs_done"], S["xt_done"], S["ys_done"], S["sq_sum"])

            def weigh(n, s, m):
                pool.wait_ge(S["h_mm"], nth(m - 1))
                pool.tensor_tensor(by_head(xw[:]), by_head(xk[:, s, 0:D]), per_head(te, n, 0), ALU.mult).then_inc(S["xw_done"], 1)

            for s in range(2):
                pool.wait_ge(ctx_in[s], 16)
                weigh(NC_LAT + s, s, s)

            def chunk(n, i, s):
                pool.wait_ge(early[s], EARLY * i + EARLY)
                pool.wait_ge(S["r_mm"], nth(2 * (n - 1) + 1))
                pool.tensor_tensor(by_head(xf[:]), by_head(xk[:, s, 0:D]), per_head(dt, n, 0), ALU.mult)
                pool.tensor_tensor(by_head(xbk[:]), by_head(xk[:, s, 0:D]), per_head(dt, n, 1), ALU.mult)
                pool.tensor_tensor(xt[:, s], xt[:, s], dk[:, 0].unsqueeze(2).to_broadcast([P, KT, P]), ALU.mult).then_inc(S["xt_done"], 1)
                weigh(n, s, n + 2)

            def gather(n, s, f):
                q = slice(4 * f, 4 * f + 4)
                out = ys[:, q].rearrange("p m i -> p (m i)")
                pool.wait_ge(S["y_read"], nth(2 * n + f))
                step = chained(pool, S["y_done"], 4 * n + 2 * f)
                step(pool.tensor_tensor(out, out, tmp[:, f], ALU.add))
                step(pool.tensor_tensor(out, out, xt[:, s, q].rearrange("p m i -> p (m i)"), ALU.add))
                pool.tensor_tensor(out, out, zs[:, s, q].rearrange("p m i -> p (m i)"), ALU.mult).then_inc(S["ys_done"], 1)

            def sum_tiles(n):
                pool.wait_ge(S["sq_done"], nth(n))
                step = chained(pool, S["sq_step"], 2 * n)
                step(pool.tensor_tensor(sq[:, 0:4], sq[:, 0:4], sq[:, 4:8], ALU.add))
                step(pool.tensor_tensor(sq[:, 0:2], sq[:, 0:2], sq[:, 2:4], ALU.add))
                pool.tensor_tensor(sq[:, 0], sq[:, 0], sq[:, 1], ALU.add).then_inc(S["sq_sum"], 1)

            def ssd_power(n):
                pool.wait_ge(S["ss_done"], nth(n))
                pool.tensor_tensor(rs[:, 0:1], rs[:, 0:1], halves[:, 0:1], ALU.pow).then_inc(S["rs_done"], 1)

            def final_power(n):
                pool.wait_ge(S["fsq_done"], nth(n))
                pool.tensor_tensor(rs[:, 1:2], rs[:, 3:4], eps[:], ALU.add).then_inc(S["f_step"], 1)
                pool.wait_ge(S["f_step"], n + 1)
                pool.tensor_tensor(rs[:, 1:2], rs[:, 1:2], halves[:, 0:1], ALU.pow).then_inc(S["frs_done"], 1)

            chunk(0, 0, 0)

            def body(n, i, s):
                gather(n, s, 0)
                gather(n, s, 1)
                if not isinstance(n, int) or n > 0:
                    final_power(n - 1)
                sum_tiles(n)
                if not (isinstance(n, int) and n == LAST):
                    chunk(n + 1, i + s, 1 - s)
                ssd_power(n)
            body(0, 0, 0)
            pairs(pool, body, head=1)
            final_power(LAST)

        @block.tensor
        def _(pe):
            lead(pe, S["cb_mm"], S["s_mm"], S["r_mm"], S["h_mm"], S["ss_mm"], S["o_mm"])

            def state(s, m):
                pe.wait_ge(S["xw_done"], nth(m))
                for g in range(GROUPS):
                    ins = pe.matmul(in_ps[:, g], xk[:, s, D + g * STATE:D + (g + 1) * STATE], xw[:, g * BANK:(g + 1) * BANK], start=True, stop=True)
                ins.then_inc(S["h_mm"], 1)

            def cb(n, i, s):
                pe.wait_ge(early[s], EARLY * i + EARLY)
                pe.wait_ge(S["ss_done"], nth(n - 2))
                for g in range(GROUPS):
                    ins = pe.matmul(m_ps[:, g * P:(g + 1) * P], bc[:, s, g], bc[:, s, GROUPS + g], start=True, stop=True)
                ins.then_inc(S["cb_mm"], 1)

            def quad(n, k):
                if k == 0:
                    pe.wait_ge(rows_in, 32 * n + 32)
                pe.wait_ge(S["dc_done"], nth(6 * n + k - 1))
                pe.wait_ge(S["dm_done"], nth(4 * n + min(k, 4) - 1))
                for side in range(2):
                    if k < 4:
                        for a in range(4):
                            cols = slice((4 * k + a) * P, (4 * k + a + 1) * P)
                            ins = pe.matmul(d_ps[:, side, a * P:(a + 1) * P], row_j[:, side, cols], row_i[:, side, cols], start=True, stop=True)
                    else:
                        for par in range(2):
                            src = row_i[0:3, side].rearrange("q (m two i) -> q two m i", two=2, i=P)[:, par, 4 * (k - 4):4 * (k - 4) + 4]
                            ins = pe.matmul(d_ps[64 * par:64 * par + 64, side], ones_b[:], src, start=True, stop=True)
                ins.then_inc(S["s_mm"], 1)

            def rest(n, i, s):
                for f in range(2):
                    pe.wait_ge(S["y_read"], nth(2 * n + f - 1))
                    if f == 0:
                        pe.wait_ge(S["h_done"], nth(n + 1))
                    for a in range(4):
                        m = 4 * f + a
                        c_now = bc[:, s, GROUPS + m // 4]
                        out = slice(a * P, (a + 1) * P)
                        pe.matmul(in_ps[:, 0, out], h[:, m * P:(m + 1) * P], c_now, start=True, stop=True)
                        pe.matmul(in_ps[:, 1, out], hb[:, s, m * P:(m + 1) * P], c_now, start=True, stop=True)
                    pe.wait_ge(S["ml_done"], nth(4 * n + 2 * f + 1))
                    pe.wait_ge(S["xt_done"], nth(n))
                    for a in range(4):
                        for par in range(2):
                            hd = 8 * f + 2 * a + par
                            out = y_ps[64 * par:64 * par + 64, a * P:(a + 1) * P]
                            cols = slice(hd * HEADDIM, (hd + 1) * HEADDIM)
                            pe.matmul(out, xf[:, cols], es[:, hd], start=True, stop=False)
                            ins = pe.matmul(out, xbk[:, cols], mu[:, hd], start=False, stop=True)
                    ins.then_inc(S["r_mm"], 1)

            def sum_squares(n):
                pe.wait_ge(S["sq_sum"], nth(n))
                if not (isinstance(n, int) and n == LAST):
                    pe.wait_ge(S["cbm_done"], nth(n + 1))
                pe.matmul(m_ps[:, 0:1], sq[:, 0], ones[:], start=True, stop=True).then_inc(S["ss_mm"], 1)

            def quarter(n, k):
                half, part = k // 2, k % 2
                if k == 0:
                    pe.wait_ge(S["w_ready"], 1)
                    pe.wait_ge(late_in, 32 * n + 32)
                if k == 1:
                    pe.wait_ge(S["ys_done"], nth(2 * n + 1))
                pe.wait_ge(S[("oa_done", "ob_done")[part]], nth(2 * n + half - 1))
                for a in range(KT):
                    src = yh[:, a] if part == 0 else ys[:, a]
                    ins = pe.matmul(o_ps[:, part], src, w_out[:, (1 - part) * KT + a, half * BANK:(half + 1) * BANK], start=(a == 0), stop=(a == KT - 1))
                ins.then_inc(S["o_mm"], 1)

            pe.wait_ge(S["prep"], 1)
            for s in range(2):
                if s:
                    pe.wait_ge(S["h_done"], nth(0))
                state(s, s)
            cb(0, 0, 0)
            for k in range(6):
                quad(0, k)

            def body(n, i, s):
                last = isinstance(n, int) and n == LAST
                rest(n, i, s)
                if not last:
                    cb(n + 1, i + s, 1 - s)
                    quad(n + 1, 0)
                pe.wait_ge(S["y_read"], nth(2 * n + 1))
                state(s, n + 2)
                quarter(n, 0)
                for k in range(1, 4):
                    if not last:
                        quad(n + 1, k)
                    if k == 1:
                        sum_squares(n)
                    quarter(n, k)
                if not last:
                    quad(n + 1, 4)
                    quad(n + 1, 5)
            pairs(pe, body)

        @block.scalar
        def _(act):
            lead(act, S["dc_done"], S["e_done"], S["sq_done"], S["oa_done"], S["fsq_done"])

            def copy(n, k):
                act.wait_ge(S["s_mm"], nth(6 * n + k))
                if k == 0:
                    act.wait_ge(S["r_mm"], nth(2 * (n - 1) + 1))
                act.activation(es[:, 4 * k:4 * k + 4].rearrange("p h i -> p (h i)"), d_ps[:, 0], ACT.Copy).then_inc(S["dc_done"], 1)

            def exp(n, k):
                act.wait_ge(S["dm_done"], nth(4 * n + k))
                cols = es[:, 4 * k:4 * k + 4]
                act.activation(cols, cols, ACT.Exp).then_inc(S["e_done"], 1)

            def exp_sums(n, k):
                act.wait_ge(S["s_mm"], nth(6 * n + k))
                act.wait_ge(S["ys_done"], nth(2 * (n - 1) + 1))
                act.activation(ea[:, k - 4], d_ps[:], ACT.Exp).then_inc(S["dc_done"], 1)

            def out_part(n, half):
                act.wait_ge(S["o_mm"], nth(4 * n + 2 * half))
                if half == 0:
                    act.wait_ge(S["hn_done"], nth(n))
                    act.wait_ge(S["fin_done"], nth(n - 1))
                act.activation(o[:, half * BANK:(half + 1) * BANK], o_ps[:, 0], ACT.Identity, scale=rs[:, 2:3]).then_inc(S["oa_done"], 1)

            def head(n, with_out):
                copy(n, 0)
                exp(n, 0)
                if with_out:
                    out_part(n - 1, 0)
                copy(n, 1)
                exp(n, 1)
                copy(n, 2)
                exp(n, 2)
                if with_out:
                    out_part(n - 1, 1)
                copy(n, 3)
                exp(n, 3)
                exp_sums(n, 4)
                exp_sums(n, 5)

            def body(n, i, s):
                act.wait_ge(S["ys_done"], nth(2 * n + 1))
                act.wait_ge(S["ss_mm"], nth(n - 1))
                act.activation(sq[:], ys[:], ACT.Square).then_inc(S["sq_done"], 1)
                if isinstance(n, int) and n == LAST:
                    out_part(n, 0)
                    out_part(n, 1)
                else:
                    head(n + 1, True)
                act.wait_ge(S["o_pre"], nth(n))
                act.activation(ob[:], o[:], ACT.Square, scale=D ** -0.5, accum_out=rs[:, 3:4]).then_inc(S["fsq_done"], 1)
            head(0, False)
            pairs(act, body)

        @block.vector
        def _(dve):
            dve.memset(h[:], 0.0)
            dve.memset(ones_b[:], 1.0)
            dve.memset(ones[:], 1.0).then_inc(S["prep"], 1)
            lead(dve, *(S[n] for n in "cbm_done dm_done ml_done y_read h_done ss_done ob_done o_pre fin_done h_dec hn_done".split()))
            dve.wait_ge(S["prep"], 1)

            def decay(n, m):
                if not isinstance(m, int) or m >= 2:
                    dve.wait_ge(S["r_mm"], nth(2 * n + 1))
                dve.tensor_tensor(by_head(h[:]), by_head(h[:]), per_head(cd, n, 0), ALU.mult).then_inc(S["h_dec"], 1)

            def add_state(m):
                dve.wait_ge(S["h_dec"], nth(m))
                dve.wait_ge(S["h_mm"], nth(m))
                dve.tensor_tensor(h[:], h[:], in_ps[:].rearrange("p a b -> p (a b)"), ALU.add).then_inc(S["h_done"], 1)
                dve.wait_ge(S["h_done"], nth(m))

            for s in range(2):
                decay(NC_LAT + s, s)
                add_state(s)

            def masks(n):
                dve.wait_ge(S["cb_mm"], nth(n))
                dve.wait_ge(S["consts"], 16 * 7)
                for u in range(2):
                    ins = dve.tensor_tensor(cbm[:, u], m_ps[:, 0:GROUPS * P].rearrange("p (g i) -> p g i", g=GROUPS),
                                            tri[:, u].unsqueeze(1).to_broadcast([P, GROUPS, P]), ALU.mult)
                ins.then_inc(S["cbm_done"], 1)

            def least(n, k):
                dve.wait_ge(S["dc_done"], nth(6 * n + k))
                cols = es[:, 4 * k:4 * k + 4].rearrange("p h i -> p (h i)")
                dve.tensor_tensor(cols, cols, d_ps[:, 1], ALU.min).then_inc(S["dm_done"], 1)

            def weigh(n, k):
                dve.wait_ge(S["cbm_done"], nth(n))
                dve.wait_ge(S["e_done"], nth(4 * n + k))
                if k == 0:
                    dve.wait_ge(S["r_mm"], nth(2 * (n - 1) + 1))
                heads = slice(4 * k, 4 * k + 4)
                g = k // 2
                dve.tensor_tensor(mu[:, heads], es[:, heads], cbm[:, 1, g].unsqueeze(1).to_broadcast([P, 4, P]), ALU.mult)
                dve.tensor_tensor(es[:, heads], es[:, heads], cbm[:, 0, g].unsqueeze(1).to_broadcast([P, 4, P]), ALU.mult).then_inc(S["ml_done"], 1)

            def hyena_norm(n):
                dve.tensor_copy(rs[:, 2:3], ssh[:, bass.ds(n, 1)]).then_inc(S["hn_done"], 1)

            def sum_done(n):
                dve.wait_ge(S["ss_mm"], nth(n))
                dve.wait_ge(S["ob_done"], nth(2 * n - 1))
                dve.tensor_scalar(rs[:, 0:1], m_ps[:, 0:1], 1.0 / D, EPS, ALU.mult, ALU.add).then_inc(S["ss_done"], 1)

            def out_part(n, half):
                cols = slice(half * BANK, (half + 1) * BANK)
                dve.wait_ge(S["rs_done"], nth(n))
                dve.wait_ge(S["oa_done"], nth(2 * n + half))
                dve.wait_ge(S["o_mm"], nth(4 * n + 2 * half + 1))
                dve.scalar_tensor_tensor(o[:, cols], o_ps[:, 1], rs[:, 0:1], o[:, cols], ALU.mult, ALU.add).then_inc(S["ob_done"], 1)

            def residual(n):
                last = isinstance(n, int) and n == LAST
                if not last:
                    hyena_norm(n + 1)
                dve.wait_ge(S["ob_done"], nth(2 * n + 1))
                v = S["v_step"]
                dve.tensor_tensor(o[:], o[:], gate_row[:], ALU.mult).then_inc(v, 1)
                dve.wait_ge(v, n + 1)
                dve.wait_ge(late_in, 32 * n + 32)
                dve.wait_ge(stored, nth(n - 1, 16))
                dve.tensor_tensor(o[:], o[:], xres[:], ALU.add).then_inc(S["o_pre"], 1)

            def finish(n):
                dve.wait_ge(S["frs_done"], nth(n))
                dve.scalar_tensor_tensor(ob[:], o[:], rs[:, 1:2], fw[:], ALU.mult, ALU.mult).then_inc(S["fin_done"], 1)

            def terms(n, s, i):
                for f in range(2):
                    q = slice(4 * f, 4 * f + 4)
                    dve.wait_ge(S["r_mm"], nth(2 * n + f))
                    if f == 0:
                        dve.wait_ge(S["dc_done"], nth(6 * n + 5))
                        dve.wait_ge(S["xt_done"], nth(n))
                        dve.wait_ge(S["o_mm"], nth(4 * (n - 1) + 3))
                        dve.wait_ge(S["sq_done"], nth(n - 1))
                        dve.wait_ge(early[s], EARLY * i + EARLY)
                    dve.wait_ge(S["ys_done"], nth(2 * (n - 1) + f))
                    dve.tensor_tensor(ys[:, q].rearrange("p m i -> p (m i)"), in_ps[:, 0], ea[:, f, 0], ALU.mult)
                    dve.tensor_tensor(tmp[:, f], in_ps[:, 1], ea[:, f, 1], ALU.mult)
                    skip = xt[:, s, q].rearrange("p m i -> p (m i)")
                    dve.tensor_tensor(skip, y_ps[:], skip, ALU.add).then_inc(S["y_read"], 1)

            def head(n, with_out):
                if not with_out:
                    masks(n)
                least(n, 0)
                weigh(n, 0)
                if with_out:
                    sum_done(n - 1)
                least(n, 1)
                weigh(n, 1)
                if with_out:
                    out_part(n - 1, 0)
                least(n, 2)
                weigh(n, 2)
                least(n, 3)
                weigh(n, 3)
                if with_out:
                    out_part(n - 1, 1)
                    residual(n - 1)

            dve.wait_ge(S["rsh_done"], 1)
            hyena_norm(0)
            head(0, False)
            dve.wait_ge(S["w_in_"], 16)
            for k in range(2 * KT):
                ins = dve.tensor_scalar(w_out[:, k], w_out[:, k], gn[:, k:k + 1], None, ALU.mult)
            ins.then_inc(S["w_ready"], 1)

            def body(n, i, s):
                last = isinstance(n, int) and n == LAST
                terms(n, s, i)
                if not last:
                    masks(n + 1)
                decay(n, n + 2)
                add_state(n + 2)
                if not isinstance(n, int) or n > 0:
                    finish(n - 1)
                if last:
                    sum_done(n)
                    out_part(n, 0)
                    out_part(n, 1)
                    residual(n)
                    finish(n)
                else:
                    head(n + 1, True)
            body(0, 0, 0)
            pairs(dve, body, head=1)
INPUTS = ["x", "c", "ctx", "c_ctx", "norm_w", "ada_w", "ada_b", "w_in", "ssd_conv_w", "ssd_conv_b", "dt_bias", "a_log",
          "d_skip", "hy_conv_w", "hy_conv_b", "filt_w1", "filt_b1", "filt_w2", "filt_b2", "filt_w3", "filt_b3", "filt_w4",
          "filt_freq", "hy_bias", "gnorm_w", "w_out", "final_norm_w"]


def program(nc, t):
    with ExitStack() as ctx:
        def kept(name, shape, dt=F32):
            return ctx.enter_context(nc.sbuf_tensor(name, shape, dt))
        keep = {"eye": kept("eye", [P, P]), "gate_row": kept("gate_row", [P, D]), "ssh": kept("ssh", [P, NC_LAT]),
                "dt_raw": kept("dt_raw", [P, NCH, 2 * HEADS])}

        def phase(build):
            with nc.cleanup_on_exit():
                build(nc, t, keep)

        with nc.sbuf_tensor("early", [P, 2 * KT * TOK], F32) as keep["early"]:
            pass
        with nc.sbuf_tensor("x_hi", [P, KT, SEQ], F32R) as keep["x_hi"], nc.sbuf_tensor("x_lo", [P, KT, SEQ], F32R) as keep["x_lo"]:
            with nc.sbuf_tensor("c_hi", [P, KT, CTX], F32R) as keep["c_hi"], nc.sbuf_tensor("c_lo", [P, KT, CTX], F32R) as keep["c_lo"]:
                with nc.sbuf_tensor("hT", [FW, SEQ + RIN], F32) as keep["hT"]:
                    phase(prepare)
                    phase(filter_first_stage)
                phase(project_ssd)
            phase(project_hyena)
        phase(spectra)
        phase(hyena_back)
        keep["to_end"], keep["chunk_decay"] = kept("to_end", [P, NCH, 2 * HEADS]), kept("chunk_decay", [P, NCH, 2 * HEADS])
        phase(ssd_scales)
        phase(ssd_backward_states)
        phase(ssd_and_out)


SCRATCH = {
    "f_spec": [RIN, 2, P, D],
    "u_spec": [RIN, 2, P, D],
    "v_spec": [RIN, 2, P, D],
    "vv_t": [KT, P, SEQ],
    "gate_t": [KT, P, SEQ],
    "yh_t": [KT, P, SEQ],
    "zs_t": [KT, P, SEQ],
    "xbc_t": [XBC_T, P, TOK],
    "xbc": [NCH, P, XBC_T * P],
    "h_back": [NCH, P, D],
}


def kernel(**inputs):
    import concourse.bacc as _bacc
    from concourse.bass_utils import run_bass_kernel_spmd as _run

    nc = _bacc.Bacc("TRN2", target_bir_lowering=False, num_devices=1)
    arrays = {n: np.ascontiguousarray(inputs[n]) for n in INPUTS}
    arrays.update(shape_constants())
    t = {}
    for name, a in arrays.items():
        t[name] = nc.dram_tensor("in_" + name, a.shape, mybir.dt.from_np(a.dtype), kind="ExternalInput").ap()
    for name, shape in SCRATCH.items():
        t[name] = nc.dram_tensor("scratch_" + name, shape, F32, kind="Internal").ap()
    t["rows"] = nc.dram_tensor("scratch_rows", ROWS_SHAPE, BF16, kind="Internal").ap()
    t["out"] = nc.dram_tensor("out_0", [1, SEQ, D], F32, kind="ExternalOutput").ap()
    program(nc, t)
    r = _run(nc, [{"in_" + n: a for n, a in arrays.items()}], core_ids=[0])
    return r.results[0]["out_0"]
```

```python
from contextlib import ExitStack

import numpy as np
import concourse.bass as bass
from concourse import mybir

F32 = mybir.dt.float32
BF16 = mybir.dt.bfloat16
F32R = mybir.dt.float32r
ALU = mybir.AluOpType
ACT = mybir.ActivationFunctionType

P = 128
BANK = 512
D = 1024
KT = D // P
SEQ, CTX = 2048, 256
TOK = SEQ + CTX
CHUNK = 128
NC_LAT, NC_CTX = SEQ // CHUNK, CTX // CHUNK
NCH = NC_LAT + NC_CTX
GRID_W = 64
HEADS, HEADDIM, GROUPS, STATE = 16, 64, 2, 128
HPG = HEADS // GROUPS
XBC_T = (D + 2 * GROUPS * STATE) // P
COL_ZS = 0
COL_XBC = COL_ZS + D
COL_DT = COL_XBC + XBC_T * P
COL_ZH = COL_DT + 2 * HEADS
COL_HY = COL_ZH + D
EPS = 1e-6
FW = 64
EMB = 33
N_FFT = 2 * SEQ
RIN, ROUT = 16, 256
FG = 4
NG = P // FG
PI = 3.1415925
TWO_PI = 2.0 * np.pi
ROUNDER = 1.5 * 2.0 ** 23
PI_A = 6.28125
PI_B = float(np.float32(np.floor((TWO_PI - PI_A) * 2 ** 20) / 2 ** 20))
PI_C = float(np.float32(TWO_PI - PI_A - PI_B))


def chained(eng, sem, start=0):
    count = [0]

    def step(ins):
        count[0] += 1
        ins.then_inc(sem, 1)
        eng.wait_ge(sem, start + count[0])
    return step


LEAD = 20


def lead(eng, *sems, unit=1):
    for s in sems:
        eng.sem_inc(s, LEAD * unit)


def nth(n, unit=1):
    return (n + LEAD + 1) * unit


def product(pe, out, w, x, at, width, contraction):
    pairs = ((0, 0), (0, 1), (1, 0))
    for k in range(contraction):
        for n, (a, b) in enumerate(pairs):
            ins = pe.matmul(out, w[a](k), x[b][:, k, at:at + width], start=(k == 0 and n == 0), stop=(k == contraction - 1 and n == 2))
    return ins


def dft_tables():
    f32 = np.float32
    q, k1 = np.arange(P), np.arange(P)

    def first(rows):
        ang = 2 * np.pi * ((rows[:, None] * k1) % ROUT) / ROUT
        re, im = np.cos(ang), -np.sin(ang)
        im[:, 0] = (-1.0) ** rows
        return np.stack([re, im], 1)
    fwd = np.stack([first(q), first(ROUT - 1 - q)], 1)
    n2, j = np.arange(RIN), np.arange(RIN)
    mats = np.zeros((NG, 5, 2, FG, RIN, 2, FG, RIN))
    S, A, B, G1, G2 = (mats[:, m] for m in range(5))
    for g in range(NG):
        for l in range(FG):
            k = FG * g + l
            low = j < RIN // 2
            bins = k + ROUT * j if k else np.where(low, ROUT * j, P + ROUT * (j - RIN // 2))
            ang = 2 * np.pi * ((n2[:, None] * bins) % N_FFT) / N_FFT
            c, s = np.cos(ang), np.sin(ang)
            if k:
                S[g, 0, l, :, 0, l], S[g, 1, l, :, 0, l] = c, s
                S[g, 0, l, :, 1, l], S[g, 1, l, :, 1, l] = -s, c
            else:
                for r, m in ((0, low), (1, ~low)):
                    S[g, r, l, :, 0, l], S[g, r, l, :, 1, l] = c * m, -s * m
                S[g, :, l, :, 1, l, 0] = 0
                S[g, 0, l, :, 1, l, 0] = (-1.0) ** n2
            for r in range(2):
                A[g, :, l, :, r, l] = S[g, :, l, :, 0, l]
                B[g, :, l, :, r, l] = S[g, :, l, :, 1, l]
            if k:
                yre, yim = np.stack([c.T, s.T], 1), np.stack([-s.T, c.T], 1)
            else:
                A[g, :, l, :, 1, l, 0] = S[g, :, l, :, 1, l, 0]
                B[g, :, l, :, :, l, 0] = 0
                yre, yim = np.zeros((RIN, 2, RIN)), np.zeros((RIN, 2, RIN))
                for r, m in ((0, low), (1, ~low)):
                    yre[m, r], yim[m, r] = 2 * c.T[m], -2 * s.T[m]
                yre[0, 0], yim[0, 0], yim[0, 1] = 1, (-1.0) ** n2, 0
            G1[g, 0, l, :, :, l], G1[g, 1, l, :, :, l] = yre, yim
            G2[g, 1, l, :, :, l], G2[g, 0, l, :, :, l] = -yre, yim
            if not k:
                G2[g, :, l, 0] = 0
    mats = mats.reshape(NG, 5, P, P).transpose(0, 2, 1, 3)
    ang = 2 * np.pi * ((k1[:, None] * q) % ROUT) / ROUT
    er, ei = 2 * np.cos(ang) / N_FFT, -2 * np.sin(ang) / N_FFT
    er[0], ei[0] = 1 / N_FFT, (-1.0) ** q / N_FFT
    return fwd.astype(f32), np.ascontiguousarray(mats, dtype=f32), np.stack([er, ei], 1).astype(f32)


def shape_constants():
    f32 = np.float32
    fwd, mats, back = dft_tables()
    t = np.linspace(0.0, 1.0, SEQ, dtype=f32)[:, None]
    w = (f32(2.0 * np.pi / SEQ) * np.arange(SEQ, dtype=f32))[:, None]
    f = np.linspace(1e-4, (EMB - 1) // 2 - 1, (EMB - 1) // 2, dtype=f32)[None, :]
    feats = np.concatenate([t, np.cos(f * w), -np.sin(f * w)], axis=1)
    lo, hi = np.log(1e-2) / 1.5, np.log(1e-2) / 0.3
    deltas = np.abs(np.linspace(lo, hi, D, dtype=f32))
    q, n2 = np.arange(P)[:, None], np.arange(RIN)[None, :]
    mt = np.stack([-(RIN * q + n2), -(RIN * q + RIN - n2)], 2) / (SEQ - 1)
    i = np.arange(P)
    upto, since = (i[:, None] <= i[None, :]), (i[:, None] >= i[None, :])
    tri = np.stack([upto, since], 1)
    return {
        "k_fwd": fwd, "k_mats": mats, "k_back": back,
        "k_feats": np.ascontiguousarray(feats.T, dtype=f32), "k_deltas": deltas[None, :],
        "k_mt": mt.astype(f32), "k_eye": np.eye(P, dtype=f32), "k_tri": tri.astype(f32),
    }
EARLY_FREE = KT * 3 * D


def places(early, at):
    now = [at]

    def place(rows, *dims):
        n = int(np.prod(dims))
        now[0] += n
        assert now[0] <= 2 * KT * TOK
        return early[0:rows, now[0] - n:now[0]]
    return place


def filter_network(nc, t, keep):
    with ExitStack() as ph:
        def sem(name):
            return nc.alloc_semaphore(name)

        def sb(name, shape, dt=F32):
            return ph.enter_context(nc.sbuf_tensor("n_" + name, shape, dt))

        hT = keep["hT"]
        place = places(keep["early"], EARLY_FREE)
        feats, ang, turns = place(EMB, SEQ), place(FW, SEQ), place(FW, SEQ)
        w1 = sb("w1", [EMB, FW])
        w23 = sb("w23", [FW, 2, FW])
        fb = sb("fb", [FW, 3])
        freq = sb("freq", [FW, 1])
        net_ps = ph.enter_context(nc.psum_tensor("n_net_ps", [FW, 2, BANK], F32))
        net_in, v_step, net_mm, net_out, net_ang, sin_done = (sem("n_" + n) for n in (
            "net_in", "v_step", "net_mm", "net_out", "net_ang", "sin_done"))
        block = ph.enter_context(nc.Block())

        @block.gpsimd
        def _(pool):
            with nc.allow_non_contiguous_dma(reason="small vectors by column"):
                pool.dma_start(feats, t["k_feats"]).then_inc(net_in, 16)
                pool.dma_start(w1[:], t["filt_w1"][0]).then_inc(net_in, 16)
                pool.dma_start(w23[:, 0], t["filt_w2"][0]).then_inc(net_in, 16)
                pool.dma_start(w23[:, 1], t["filt_w3"][0]).then_inc(net_in, 16)
                for n in range(3):
                    pool.dma_start(fb[:, n:n + 1], t[f"filt_b{n + 1}"].rearrange("a c -> c a")).then_inc(net_in, 16)
                pool.dma_start(freq[:], t["filt_freq"].rearrange("a c -> c a")).then_inc(net_in, 16)

        @block.scalar
        def _(act):
            for layer in range(3):
                act.wait_ge(net_ang, layer + 1)
                act.activation(hT[:, 0:SEQ], ang, ACT.Sin).then_inc(sin_done, 1)

        @block.tensor
        def _(pe):
            pe.wait_ge(net_in, 16 * 8)
            for layer in range(3):
                w = w1[:] if layer == 0 else w23[:, layer - 1]
                if layer:
                    pe.wait_ge(sin_done, layer)
                for c in range(4):
                    n = 4 * layer + c
                    if n >= 2:
                        pe.wait_ge(net_out, n - 1)
                    src = feats if layer == 0 else hT[:]
                    pe.matmul(net_ps[:, n % 2], w, src[:, c * BANK:(c + 1) * BANK], start=True, stop=True).then_inc(net_mm, 1)

        @block.vector
        def _(dve):
            step = chained(dve, v_step)
            dve.memset(hT[:, SEQ:SEQ + 1], 0.0)
            dve.wait_ge(net_in, 16 * 8)
            for layer in range(3):
                for c in range(4):
                    n = 4 * layer + c
                    dve.wait_ge(net_mm, n + 1)
                    if layer and c == 0:
                        dve.wait_ge(sin_done, layer)
                    dve.tensor_scalar(ang[:, c * BANK:(c + 1) * BANK], net_ps[:, n % 2], fb[:, layer:layer + 1], freq[:, 0:1],
                                      ALU.add, ALU.mult).then_inc(net_out, 1)
                dve.wait_ge(net_out, 4 * layer + 4)
                step(dve.tensor_scalar(turns, ang, 1.0 / TWO_PI, ROUNDER, ALU.mult, ALU.add))
                step(dve.tensor_scalar(turns, turns, -ROUNDER, None, ALU.add))
                for part in (PI_A, PI_B, PI_C):
                    step(dve.scalar_tensor_tensor(ang, turns, -part, ang, ALU.mult, ALU.add))
                dve.tensor_scalar(ang, ang, PI, -PI, ALU.min, ALU.max).then_inc(net_ang, 1)


def prepare(nc, t, keep):
    with ExitStack() as ph:
        def sem(name):
            return nc.alloc_semaphore(name)

        def sb(name, shape, dt=F32):
            return ph.enter_context(nc.sbuf_tensor("p_" + name, shape, dt))

        def psum(name, shape):
            return ph.enter_context(nc.psum_tensor("p_" + name, shape, F32))

        eye, gate_row, xg, x_in = keep["eye"], keep["gate_row"], keep["xg"], keep["x_in"]
        parts = [(keep["x_hi"], keep["x_lo"]), (keep["c_hi"], keep["c_lo"])]
        ada = keep["early"][:, 0:EARLY_FREE].rearrange("p (k n) -> p k n", k=KT)
        place = places(keep["early"], EARLY_FREE)
        ada_b = place(2, 3 * D)
        row = place(2, 3 * D)
        squares = places(keep["early"], 2 * KT * SEQ)(P, D)
        c_col = sb("c_col", [P, KT, 2])
        s_col = sb("s_col", [P, KT, 2])
        ones = sb("ones", [1, P])
        norm_w = sb("norm_w", [P, KT])
        mod = sb("mod", [P, 2, 2, KT])
        ss = sb("ss", [P, NCH])
        rstd = sb("rstd", [P, NCH])
        halves = sb("halves", [P, NCH])
        RING = 4
        xn = sb("xn", [P, RING, BANK])
        ps = psum("ps", [P, 3 * D // BANK, BANK])
        col_ps = psum("col_ps", [P, 2 * KT, 2])
        tr, gate_ps = ps[:, 0:RING], ps[:, RING:RING + 2]

        c_in, small_in, silu_done = (sem(n) for n in ("c_in", "small_in", "silu_done"))
        mods_mm, mod_ready, v_step, row_done, cols_mm = (sem(n) for n in (
            "mods_mm", "mod_ready", "p_v_step", "row_done", "cols_mm"))
        x_late = [sem(f"x_late{i}") for i in range(2)]
        sq_done, rstd_done, x_scaled, tr_done, tr_used, pool_step, hi_done, lo_done = (
            sem(n) for n in ("sq_done", "rstd_done", "x_scaled", "tr_done", "tr_used", "pool_step", "hi_done", "lo_done"))
        tiles = [4, 4, 4, 4, NC_CTX]
        x_dram = [t["x"][0].rearrange("(g a p) d -> g p a d", a=4, p=P)[g] for g in range(4)]
        x_dram.append(t["ctx"][0].rearrange("(a p) d -> p a d", p=P))
        block = ph.enter_context(nc.Block())

        @block.sync
        def _(sp):
            with nc.allow_non_contiguous_dma(reason="small vectors by column"):
                sp.dma_start(c_col[:, :, 0], t["c"][0].rearrange("(k p) -> p k", p=P)).then_inc(c_in, 16)
                sp.dma_start(c_col[:, :, 1], t["c_ctx"].rearrange("(k p) -> p k", p=P)).then_inc(c_in, 16)
            for g in range(2, 5):
                sp.wait_ge(tr_done, KT * (g - 1))
                sp.dma_start(xg[:, g % 2, 0:tiles[g]], x_dram[g]).then_inc(x_late[g % 2], 16)

        @block.gpsimd
        def _(pool):
            with nc.allow_non_contiguous_dma(reason="small vectors by column"):
                pool.dma_start(eye[:], t["k_eye"]).then_inc(small_in, 16)
                pool.dma_start(norm_w[:], t["norm_w"][0].rearrange("(k p) -> p k", p=P)).then_inc(small_in, 16)
                pool.dma_start(ada_b, t["ada_b"][0].partition_broadcast(2)).then_inc(small_in, 16)
            step = chained(pool, pool_step)
            step(pool.memset(halves[:], -0.5))
            for g in range(5):
                a = slice(4 * g, 4 * g + tiles[g])
                pool.wait_ge(sq_done, 4 * g + tiles[g])
                step(pool.tensor_scalar(rstd[:, a], ss[:, a], 1.0 / D, EPS, ALU.mult, ALU.add))
                pool.tensor_tensor(rstd[:, a], rstd[:, a], halves[:, a], ALU.pow).then_inc(rstd_done, 1)

        @block.scalar
        def _(act):
            def squares_of(g):
                if g < 2:
                    act.wait_ge(x_in[g], 16)
                else:
                    act.wait_ge(x_late[g % 2], 16 * (g // 2))
                for a in range(tiles[g]):
                    n = 4 * g + a
                    act.activation(squares, xg[:, g % 2, a], ACT.Square, accum_out=ss[:, n:n + 1]).then_inc(sq_done, 1)
                    act.wait_ge(sq_done, n + 1)

            def modulate(g):
                r = 0 if g < 4 else 1
                for k in range(KT):
                    w = P * tiles[g]
                    act.wait_ge(tr_done, KT * g + k + 1)
                    n = KT * g + k
                    if n >= RING:
                        act.wait_ge(lo_done, n - RING + 1)
                    act.activation(xn[:, k % RING, 0:w], tr[:, k % RING, 0:w], ACT.Identity,
                                   bias=mod[:, 0, r, k:k + 1], scale=mod[:, 1, r, k:k + 1]).then_inc(tr_used, 1)

            act.wait_ge(c_in, 32)
            act.activation(s_col[:], c_col[:], ACT.Silu).then_inc(silu_done, 1)
            squares_of(0)
            squares_of(1)
            act.wait_ge(mod_ready, 1)
            modulate(0)
            for g in range(2, 5):
                squares_of(g)
                modulate(g - 1)
            modulate(4)

        @block.tensor
        def _(pe):
            def transposes(g):
                pe.wait_ge(x_scaled, g + 1)
                for k in range(KT):
                    n = KT * g + k
                    if n >= RING:
                        pe.wait_ge(tr_used, n - RING + 1)
                    for a in range(tiles[g]):
                        ins = pe.transpose(tr[:, n % RING, a * P:(a + 1) * P], xg[:, g % 2, a, k * P:(k + 1) * P], eye[:])
                    ins.then_inc(tr_done, 1)

            pe.wait_ge(silu_done, 1)
            pe.wait_ge(keep["ada_in"], 16 * KT)
            for k in range(KT):
                for b in range(3 * D // BANK):
                    ins = pe.matmul(ps[0:2, b], s_col[:, k], ada[:, k, b * BANK:(b + 1) * BANK], start=(k == 0), stop=(k == KT - 1))
            ins.then_inc(mods_mm, 1)
            pe.wait_ge(small_in, 48)
            pe.wait_ge(row_done, 1)
            for m in range(2 * KT):
                pe.transpose(col_ps[:, m], row[:, m * P:(m + 1) * P], eye[0:2, 0:2])
            for h in range(2):
                ins = pe.matmul(gate_ps[:, h], ones[:], row[0:1, 2 * D + h * BANK:2 * D + (h + 1) * BANK], start=True, stop=True)
            ins.then_inc(cols_mm, 1)
            for g in range(5):
                transposes(g)

        @block.vector
        def _(dve):
            step = chained(dve, v_step)

            def scale_tokens(g):
                dve.wait_ge(rstd_done, g + 1)
                for a in range(tiles[g]):
                    n = 4 * g + a
                    ins = dve.tensor_scalar(xg[:, g % 2, a], xg[:, g % 2, a], rstd[:, n:n + 1], None, ALU.mult)
                ins.then_inc(x_scaled, 1)

            def split(g):
                hi, lo = parts[g // 4]
                at = BANK * (g % 4)
                for k in range(KT):
                    n, w = KT * g + k, P * tiles[g]
                    cols = slice(at, at + w)
                    dve.wait_ge(tr_used, n + 1)
                    dve.tensor_copy(hi[:, k, cols], xn[:, k % RING, 0:w]).then_inc(hi_done, 1)
                    dve.wait_ge(hi_done, n + 1)
                    dve.tensor_tensor(lo[:, k, cols], xn[:, k % RING, 0:w], hi[:, k, cols].bitcast(F32), ALU.subtract).then_inc(lo_done, 1)

            step(dve.memset(ones[:], 1.0))
            scale_tokens(0)
            scale_tokens(1)
            dve.wait_ge(mods_mm, 1)
            dve.wait_ge(small_in, 48)
            dve.tensor_tensor(row, ps[0:2].rearrange("p b n -> p (b n)"), ada_b, ALU.add).then_inc(row_done, 1)
            dve.wait_ge(cols_mm, 1)
            for r in range(2):
                step(dve.tensor_copy(mod[:, 0, r], col_ps[:, 0:KT, r]))
                step(dve.scalar_tensor_tensor(mod[:, 1, r], col_ps[:, KT:2 * KT, r], 1.0, norm_w[:], ALU.add, ALU.mult))
            dve.tensor_copy(gate_row[:], gate_ps.rearrange("p h n -> p (h n)")).then_inc(mod_ready, 1)
            for g in range(5):
                split(g)
                if g < 3:
                    scale_tokens(g + 2)


def filter_first_stage(nc, t, keep):
    with ExitStack() as ph:
        def sem(name):
            return nc.alloc_semaphore(name)

        def sb(name, shape, dt=F32):
            return ph.enter_context(nc.sbuf_tensor("f_" + name, shape, dt))

        def psum(name, shape):
            return ph.enter_context(nc.psum_tensor("f_" + name, shape, F32))

        hT = keep["hT"]
        place = places(keep["early"], EARLY_FREE)
        w4 = place(FW, 2, D).rearrange("p (s d) -> p s d", s=2)
        fwd = place(P, 2, 2, P).rearrange("p (s r k) -> p s r k", s=2, r=2)
        deltas = place(P, D)
        window, taps, out = (place(P, 2, 2, BANK).rearrange("p (h s c) -> p h s c", h=2, s=2) for _ in range(3))
        skip = sb("skip", [1, D])
        mt = sb("mt", [P, RIN, 2])
        mt_now = sb("mt_now", [P, 2])
        h_now = sb("h_now", [FW, 2, P])
        h_ps = psum("h_ps", [P, 2, 2, BANK])
        f_ps = psum("f_ps", [P, 2, 2, BANK])
        w_in_, net_now, mt_done, h_mm, win_done, taps_done, f_mm = (
            sem(n) for n in ("f_consts", "f_net_now", "f_mt_done", "f_h_mm", "f_win_done", "f_taps_done", "f_mm"))
        out_re, out_im, tap_0 = sem("f_out_re"), sem("f_out_im"), sem("f_tap_0")
        stored = [sem(f"f_stored{h}") for h in range(2)]
        block = ph.enter_context(nc.Block())

        @block.gpsimd
        def _(pool):
            ada = keep["early"][:, 0:EARLY_FREE].rearrange("p (k n) -> p k n", k=KT)
            for k in range(KT):
                pool.dma_start(ada[:, k], t["ada_w"][0].rearrange("(k p) n -> k p n", p=P)[k]).then_inc(keep["ada_in"], 16)
            for g in range(2):
                pool.dma_start(keep["xg"][:, g], t["x"][0].rearrange("(g a p) d -> g p a d", a=4, p=P)[g]).then_inc(keep["x_in"][g], 16)

        @block.sync
        def _(sp):
            sp.dma_start(w4, t["filt_w4"][0].rearrange("p (s d) -> p s d", s=2)).then_inc(w_in_, 16)
            sp.dma_start(fwd, t["k_fwd"]).then_inc(w_in_, 16)
            sp.dma_start(deltas, t["k_deltas"][0].partition_broadcast(P)).then_inc(w_in_, 16)
            sp.dma_start(mt[:], t["k_mt"]).then_inc(w_in_, 16)
            sp.dma_start(skip[:], t["hy_bias"]).then_inc(w_in_, 16)
            lead(sp, *stored, unit=16)
            with sp.Fori(0, RIN) as n2:
                for h in range(2):
                    sp.wait_ge(out_re, nth(2 * n2 + h))
                    sp.wait_ge(out_im, nth(2 * n2 + h))
                    sp.dma_start(t["f_spec"][n2][:, :, h * BANK:(h + 1) * BANK].rearrange("r k c -> k r c"),
                                 out[:, h]).then_inc(stored[h], 16)
            for h in range(2):
                sp.wait_ge(stored[h], nth(RIN - 1, 16))

        @block.tensor
        def _(pe):
            lead(pe, h_mm, f_mm)
            pe.wait_ge(w_in_, 80)

            def net_out(n2, h):
                if h == 0:
                    pe.wait_ge(net_now, n2 + 1)
                for s in range(2):
                    ins = pe.matmul(h_ps[:, h, s], h_now[:, s], w4[:, s, h * BANK:(h + 1) * BANK], start=True, stop=True)
                ins.then_inc(h_mm, 1)

            def stage(n2, h):
                n = 2 * n2 + h
                pe.wait_ge(out_re, nth(n - 2))
                pe.wait_ge(out_im, nth(n - 2))
                for r in range(2):
                    for s in range(2):
                        ins = pe.matmul(f_ps[:, h, r], fwd[:, s, r], taps[:, h, s], start=(s == 0), stop=(s == 1))
                ins.then_inc(f_mm, 1)

            net_out(0, 0)
            net_out(0, 1)
            with pe.Fori(0, RIN - 1) as n2:
                for h in range(2):
                    pe.wait_ge(taps_done, nth(2 * n2 + h))
                    net_out(n2 + 1, h)
                    stage(n2, h)
            for h in range(2):
                pe.wait_ge(taps_done, nth(2 * RIN - 2 + h))
                stage(RIN - 1, h)

        @block.scalar
        def _(act):
            lead(act, win_done, out_re)
            act.wait_ge(w_in_, 80)

            def windows(n2):
                act.wait_ge(mt_done, n2 + 1)
                for h in range(2):
                    act.wait_ge(taps_done, nth(2 * n2 + h - 2))
                    for s in range(2):
                        ins = act.activation(window[:, h, s], deltas[:, h * BANK:(h + 1) * BANK], ACT.Exp, scale=mt_now[:, s:s + 1])
                    ins.then_inc(win_done, 1)

            def real_parts(n2):
                for h in range(2):
                    n = 2 * n2 + h
                    act.wait_ge(f_mm, nth(n))
                    act.wait_ge(stored[h], nth(n2 - 1, 16))
                    act.activation(out[:, h, 0], f_ps[:, h, 0], ACT.Copy).then_inc(out_re, 1)

            windows(0)
            with act.Fori(0, RIN - 1) as n2:
                windows(n2 + 1)
                real_parts(n2)
            real_parts(RIN - 1)

        @block.vector
        def _(dve):
            lead(dve, taps_done, out_im)
            dve.wait_ge(w_in_, 80)

            def columns(n2):
                dve.wait_ge(h_mm, nth(2 * n2 - 1))
                dve.tensor_copy(h_now[:, 0], hT[:, bass.ds(n2, P, step=RIN)])
                dve.tensor_copy(h_now[:, 1], hT[:, bass.ds(RIN - n2, P, step=RIN)]).then_inc(net_now, 1)
                dve.wait_ge(win_done, nth(2 * n2 - 1))
                dve.tensor_copy(mt_now[:], mt[:, bass.ds(n2, 1)].rearrange("p a s -> p (a s)")).then_inc(mt_done, 1)

            def windowed(n2, h, first=False):
                n = 2 * n2 + h
                dve.wait_ge(h_mm, nth(n))
                dve.wait_ge(win_done, nth(n))
                dve.wait_ge(f_mm, nth(n - 2))
                for s in range(2):
                    ins = dve.tensor_tensor(taps[:, h, s], h_ps[:, h, s], window[:, h, s], ALU.mult)
                if first:
                    ins.then_inc(tap_0, 1)
                    dve.wait_ge(tap_0, h + 1)
                    ins = dve.tensor_tensor(taps[0:1, h, 0], taps[0:1, h, 0], skip[:, h * BANK:(h + 1) * BANK], ALU.add)
                ins.then_inc(taps_done, 1)

            def imaginary_part(n2, h):
                dve.wait_ge(f_mm, nth(2 * n2 + h))
                dve.wait_ge(stored[h], nth(n2 - 1, 16))
                dve.tensor_copy(out[:, h, 1], f_ps[:, h, 1]).then_inc(out_im, 1)

            columns(0)
            windowed(0, 0, True)
            columns(1)
            windowed(0, 1, True)
            with dve.Fori(1, RIN - 1) as n2:
                imaginary_part(n2 - 1, 0)
                windowed(n2, 0)
                columns(n2 + 1)
                windowed(n2, 1)
                imaginary_part(n2 - 1, 1)
            imaginary_part(RIN - 2, 0)
            windowed(RIN - 1, 0)
            windowed(RIN - 1, 1)
            imaginary_part(RIN - 2, 1)
            imaginary_part(RIN - 1, 0)
            imaginary_part(RIN - 1, 1)
def conv_taps(dve, step, tile, ps, taps, rows, width):
    a = tile.rearrange("p (r w) -> p r w", w=width)
    b = ps.rearrange("p (r w) -> p r w", w=width)
    step(dve.scalar_tensor_tensor(a[:, :, 1:width], b[:, :, 0:width - 1], taps[:, 0:1], a[:, :, 1:width], ALU.mult, ALU.add))
    return dve.scalar_tensor_tensor(a[:, :, 0:width - 1], b[:, :, 1:width], taps[:, 2:3], a[:, :, 0:width - 1], ALU.mult, ALU.add)


def split_weights(eng, parts, raw, hi_done, count):
    eng.tensor_copy(parts[:, 0], raw).then_inc(hi_done, 1)
    eng.wait_ge(hi_done, count)
    return eng.tensor_tensor(parts[:, 1], raw, parts[:, 0].bitcast(F32), ALU.subtract)


def project_hyena(nc, t, keep):
    with ExitStack() as ph:
        def sem(name):
            return nc.alloc_semaphore(name)

        def sb(name, shape, dt=F32):
            return ph.enter_context(nc.sbuf_tensor("h_" + name, shape, dt))

        def psum(name, shape):
            return ph.enter_context(nc.psum_tensor("h_" + name, shape, F32))

        x, eye = (keep["x_hi"], keep["x_lo"]), keep["eye"]
        HY_T = D // P
        KINDS = (COL_HY + D, COL_HY + 2 * D, COL_HY, COL_ZH)
        CONV_AT = (1, 2, 0)
        w_raw = sb("w_raw", [P, KT, P])
        w = sb("w", [P, 2, 2, KT, P], F32R)
        taps = sb("taps", [P, 3, HY_T, 4])
        taps_now = sb("taps_now", [P, 3, 4])
        fwd = sb("fwd", [P, 2, P])
        part = sb("part", [P, 4, SEQ])
        vv, gate = part[:, 0], part[:, 2]
        u = sb("u", [P, RIN, P])
        spec = sb("spec", [P, 2, 2, 4 * P])
        pj = psum("pj", [P, 4, BANK])
        tr = psum("tr", [P, 2, BANK])
        st = psum("st", [P, 2, BANK])
        stage = (st, tr)
        w_in_ = [sem(f"h_w_in{j}") for j in range(2)]
        w_hi_done, w_split, passed = sem("h_w_hi_done"), sem("h_w_split"), sem("h_passed")
        consts, taps_ready, pj_mm, cv_mid, cv_side, cv_done, z_done, vv_done, gate_done = (sem("h_" + n) for n in (
            "consts", "taps_ready", "pj_mm", "cv_mid", "cv_side", "cv_done", "z_done", "vv_done", "gate_done"))
        tr_mm, u_done, st_mm, re_done, im_done, gate_out = (sem("h_" + n) for n in (
            "tr_mm", "u_done", "st_mm", "re_done", "im_done", "gate_out"))
        spec_out = [sem(f"h_spec_out{s}") for s in range(2)]
        w_cols = t["w_in"][0].rearrange("(k p) n -> p k n", p=P)
        block = ph.enter_context(nc.Block())

        @block.gpsimd
        def _(pool):
            def load(c, j):
                pool.dma_start(w_raw[:], w_cols[:, :, bass.ds(KINDS[j] + c * P, P)]).then_inc(w_in_[j % 2], 16)

            def split(c, j):
                pool.wait_ge(w_in_[j % 2], 16 * (2 * c + j // 2) + 16)
                pool.wait_ge(pj_mm, nth(16 * c + 4 * (j - 2) + 3))
                pool.sem_inc(passed, 1)
                split_weights(pool, w[:, j % 2], w_raw[:], w_hi_done, 4 * c + j + 1).then_inc(w_split, 1)
                pool.wait_ge(w_split, 4 * c + j + 1)

            load(0, 0)
            with pool.Fori(0, HY_T - 1) as c:
                for j in range(4):
                    split(c, j)
                    load(c + (j + 1) // 4, (j + 1) % 4)
            for j in range(4):
                split(HY_T - 1, j)
                if j < 3:
                    load(HY_T - 1, j + 1)

        @block.sync
        def _(sp):
            with nc.allow_non_contiguous_dma(reason="taps by channel"):
                for a in range(3):
                    cols = slice(a * D, (a + 1) * D)
                    for k in range(3):
                        sp.dma_start(taps[:, a, :, k], t["hy_conv_w"][0, k, cols].rearrange("(m p) -> p m", p=P)).then_inc(consts, 16)
                    sp.dma_start(taps[:, a, :, 3], t["hy_conv_b"][0, cols].rearrange("(m p) -> p m", p=P)).then_inc(consts, 16)
                sp.dma_start(fwd[:], t["k_fwd"][:, 0]).then_inc(consts, 16)
            lead(sp, gate_out, unit=16)
            lead(sp, *spec_out, unit=64)
            with sp.Fori(0, HY_T) as c:
                sp.wait_ge(gate_done, nth(c))
                sp.dma_start(t["gate_t"][c], gate).then_inc(gate_out, 16)
                for n in range(4):
                    sp.wait_ge(re_done, nth(4 * c + n))
                    sp.wait_ge(im_done, nth(4 * c + n))
                    for r in range(2):
                        sp.dma_start(t["u_spec"][4 * n:4 * n + 4, r, :, bass.ds(c * P, P)].rearrange("n k c -> k n c"),
                                     spec[:, n % 2, r].rearrange("k (n c) -> k n c", n=4)).then_inc(spec_out[n % 2], 16)
            sp.wait_ge(gate_out, nth(HY_T - 1, 16))
            for s in range(2):
                sp.wait_ge(spec_out[s], nth(HY_T - 1, 64))

        @block.tensor
        def _(pe):
            lead(pe, pj_mm, tr_mm, st_mm)
            with pe.Fori(0, HY_T) as c:
                for j in range(4):
                    pe.wait_ge(w_split, 4 * c + j + 1)
                    for q in range(4):
                        if j == 0:
                            pe.wait_ge(z_done, nth(4 * (c - 1) + q))
                        else:
                            pe.wait_ge(cv_done, nth(12 * c + 4 * (j - 1) + q))
                        weights = [lambda k, j=j, a=a: w[:, j % 2, a, k] for a in range(2)]
                        product(pe, pj[:, q], weights, x, q * BANK, BANK, KT).then_inc(pj_mm, 1)
                    if j == 2:
                        pe.wait_ge(vv_done, nth(c))
                        pe.wait_ge(re_done, nth(4 * (c - 1) + 3))
                        pe.wait_ge(im_done, nth(4 * (c - 1) + 3))
                        for n in range(4):
                            pe.wait_ge(u_done, nth(4 * c + n - 2))
                            for a in range(4):
                                ins = pe.transpose(tr[:, n % 2, a * P:(a + 1) * P], vv[:, 4 * n + a::RIN], eye[:])
                            ins.then_inc(tr_mm, 1)
                pe.wait_ge(consts, 16 * 13)
                pe.wait_ge(u_done, nth(4 * c + 3))
                for n in range(4):
                    pe.wait_ge(re_done, nth(4 * c + n - 2))
                    pe.wait_ge(im_done, nth(4 * c + n - 2))
                    for r in range(2):
                        ins = pe.matmul(stage[n % 2][:, r], fwd[:, r], u[:, 4 * n:4 * n + 4].rearrange("p a c -> p (a c)"), start=True, stop=True)
                    ins.then_inc(st_mm, 1)

        @block.scalar
        def _(act):
            lead(act, z_done, u_done, re_done, cv_mid)
            act.wait_ge(consts, 16 * 13)
            with act.Fori(0, HY_T) as c:
                act.wait_ge(taps_ready, c + 1)
                for j in range(4):
                    if j == 0:
                        act.wait_ge(tr_mm, nth(4 * (c - 1) + 3))
                    elif j == 1:
                        act.wait_ge(vv_done, nth(c - 1))
                    elif j == 2:
                        act.wait_ge(gate_out, nth(c - 1, 16))
                    else:
                        act.wait_ge(gate_done, nth(c - 1))
                    for q in range(4):
                        act.wait_ge(pj_mm, nth(16 * c + 4 * j + q))
                        cols = part[:, j, q * BANK:(q + 1) * BANK]
                        if j == 3:
                            act.activation(cols, pj[:, q], ACT.Silu).then_inc(z_done, 1)
                        else:
                            act.activation(cols, pj[:, q], ACT.Identity, bias=taps_now[:, j, 3:4], scale=taps_now[:, j, 1:2]).then_inc(cv_mid, 1)
                    if j == 2:
                        act.wait_ge(st_mm, nth(4 * (c - 1) + 3))
                        for n in range(4):
                            act.wait_ge(tr_mm, nth(4 * c + n))
                            act.activation(u[:, 4 * n:4 * n + 4].rearrange("p a c -> p (a c)"), tr[:, n % 2], ACT.Copy).then_inc(u_done, 1)
                for n in range(4):
                    act.wait_ge(spec_out[n % 2], nth(c - 1, 64) + 32 * (n // 2))
                    act.wait_ge(st_mm, nth(4 * c + n))
                    act.activation(spec[:, n % 2, 0], stage[n % 2][:, 0], ACT.Copy).then_inc(re_done, 1)

        @block.vector
        def _(dve):
            lead(dve, cv_done, im_done, vv_done, gate_done)
            dve.wait_ge(consts, 16 * 13)
            with dve.Fori(0, HY_T) as c:
                dve.wait_ge(cv_mid, nth(12 * c - 1))
                dve.wait_ge(cv_done, nth(12 * c - 1))
                for j in range(3):
                    ins = dve.tensor_copy(taps_now[:, j], taps[:, CONV_AT[j], bass.ds(c, 1)].rearrange("p a k -> p (a k)"))
                ins.then_inc(taps_ready, 1)
                step = chained(dve, cv_side, 12 * c)
                dve.wait_ge(taps_ready, c + 1)
                for j in range(3):
                    for q in range(4):
                        n = 12 * c + 4 * j + q
                        dve.wait_ge(cv_mid, nth(n))
                        conv_taps(dve, step, part[:, j, q * BANK:(q + 1) * BANK], pj[:, q], taps_now[:, j], BANK // GRID_W, GRID_W).then_inc(cv_done, 1)
                    if j == 1:
                        dve.wait_ge(cv_done, nth(12 * c + 7))
                        dve.tensor_tensor(vv, part[:, 0], part[:, 1], ALU.mult).then_inc(vv_done, 1)
                dve.wait_ge(cv_done, nth(12 * c + 11))
                dve.wait_ge(z_done, nth(4 * c + 3))
                dve.tensor_tensor(gate, part[:, 2], part[:, 3], ALU.mult).then_inc(gate_done, 1)
                for n in range(4):
                    dve.wait_ge(spec_out[n % 2], nth(c - 1, 64) + 32 * (n // 2))
                    dve.wait_ge(st_mm, nth(4 * c + n))
                    dve.tensor_copy(spec[:, n % 2, 1], stage[n % 2][:, 1]).then_inc(im_done, 1)


def project_ssd(nc, t, keep):
    project_xbc(nc, t, keep, "s", 0, D // P, True)
    project_xbc(nc, t, keep, "b", D // P, XBC_T - D // P, False)


def project_xbc(nc, t, keep, pre, first, tiles, with_z):
    with ExitStack() as ph:
        def sem(name):
            return nc.alloc_semaphore(name)

        def sb(name, shape, dt=F32):
            return ph.enter_context(nc.sbuf_tensor(f"{pre}_{name}", shape, dt))

        def psum(name, shape):
            return ph.enter_context(nc.psum_tensor(f"{pre}_{name}", shape, F32))

        x, cx, eye, dt_raw = (keep["x_hi"], keep["x_lo"]), (keep["c_hi"], keep["c_lo"]), keep["eye"], keep["dt_raw"]
        MM = 9 if with_z else 5
        CONSTS = 16 * (4 if with_z else 5)
        QUADS = (NCH + 3) // 4
        KINDS = 2 if with_z else 1
        w_raw = sb("w_raw", [P, KT, P])
        w = sb("w", [P, 2, 2, KT, P], F32R)
        taps = sb("taps", [P, tiles, 4])
        taps_now = sb("taps_now", [P, 4])
        conv = sb("conv", [P, TOK])
        xt = sb("xt", [P, TOK])
        zt = sb("zt", [P, SEQ]) if with_z else None
        xk = sb("xk", [P, NCH, P])
        if not with_z:
            w_dt = sb("w_dt", [P, KT, 2 * HEADS])
            w_dt_parts = sb("w_dt_parts", [P, 2, KT, 2 * HEADS], F32R)
        dtT = conv[0:2 * HEADS]
        pj = psum("pj", [P, 4, BANK])
        pc = psum("pc", [P, BANK])
        tr = psum("tr", [P, 2, BANK])
        w_in_ = [sem(f"{pre}_w_in{s}") for s in range(2)]
        w_hi_done, w_split, w_dt_hi, w_dt_split, passed = (sem(f"{pre}_{n}") for n in (
            "w_hi_done", "w_split", "w_dt_hi", "w_dt_split", "passed"))
        consts, taps_ready, mm, cv_mid, cv_side, cv_done, x_done, z_done = (sem(f"{pre}_{n}") for n in (
            "consts", "taps_ready", "mm", "cv_mid", "cv_side", "cv_done", "x_done", "z_done"))
        tr_mm, xk_done, xt_out, xk_out, z_out, dt_done, dt_tr, dt_copied = (sem(f"{pre}_{n}") for n in (
            "tr_mm", "xk_done", "xt_out", "xk_out", "z_out", "dt_done", "dt_tr", "dt_copied"))
        w_cols = t["w_in"][0].rearrange("(k p) n -> p k n", p=P)
        block = ph.enter_context(nc.Block())
        chunks = [(q, q * BANK, BANK) for q in range(4)] + [(4, SEQ, CTX)]

        def bank(q):
            return pj[:, q] if q < 4 else pc[:, 0:CTX]

        @block.gpsimd
        def _(pool):
            def column(c, s):
                return (COL_XBC, COL_ZS)[s] + c * P if with_z else COL_XBC + (first + 2 * c + s) * P

            def load(c, s):
                pool.dma_start(w_raw[:], w_cols[:, :, bass.ds(column(c, s), P)]).then_inc(w_in_[s], 16)

            def split(c, s):
                pool.wait_ge(w_in_[s], 16 * c + 16)
                pool.wait_ge(mm, nth(MM * (c - 1) + (4, 8)[s]) if with_z else nth(5 * (2 * c + s - 2) + 4))
                pool.sem_inc(passed, 1)
                split_weights(pool, w[:, s], w_raw[:], w_hi_done, 2 * c + s + 1).then_inc(w_split, 1)
                pool.wait_ge(w_split, 2 * c + s + 1)

            ROUNDS = tiles if with_z else tiles // 2
            load(0, 0)
            if not with_z:
                pool.wait_ge(consts, CONSTS)
                split_weights(pool, w_dt_parts, w_dt[:], w_dt_hi, 1).then_inc(w_dt_split, 1)
            with pool.Fori(0, ROUNDS - 1) as c:
                for s in range(2):
                    split(c, s)
                    load(c + s, 1 - s)
            split(ROUNDS - 1, 0)
            load(ROUNDS - 1, 1)
            split(ROUNDS - 1, 1)

        @block.sync
        def _(sp):
            with nc.allow_non_contiguous_dma(reason="taps by channel"):
                cols = slice(first * P, (first + tiles) * P)
                for k in range(3):
                    sp.dma_start(taps[:, :, k], t["ssd_conv_w"][0, k, cols].rearrange("(m p) -> p m", p=P)).then_inc(consts, 16)
                sp.dma_start(taps[:, :, 3], t["ssd_conv_b"][0, cols].rearrange("(m p) -> p m", p=P)).then_inc(consts, 16)
                if not with_z:
                    sp.dma_start(w_dt[:], w_cols[:, :, COL_DT:COL_DT + 2 * HEADS]).then_inc(consts, 16)
            lead(sp, xt_out, xk_out, z_out, unit=16)
            with sp.Fori(0, tiles) as c:
                sp.wait_ge(x_done, nth(c))
                sp.dma_start(t["xbc_t"][first + c], xt[:]).then_inc(xt_out, 16)
                if with_z:
                    sp.wait_ge(z_done, nth(4 * c + 3))
                    sp.dma_start(t["zs_t"][c], zt[:]).then_inc(z_out, 16)
                sp.wait_ge(xk_done, nth(QUADS * c + QUADS - 1))
                sp.dma_start(t["xbc"][:, :, bass.ds((first + c) * P, P)].rearrange("n p c -> p n c"), xk[:]).then_inc(xk_out, 16)
            sp.wait_ge(xt_out, nth(tiles - 1, 16))
            sp.wait_ge(xk_out, nth(tiles - 1, 16))
            if with_z:
                sp.wait_ge(z_out, nth(tiles - 1, 16))

        @block.tensor
        def _(pe):
            lead(pe, mm, tr_mm)

            def tile(c, s, before):
                pe.wait_ge(w_split, 2 * c + 1 if with_z else c + 1)
                weights = [lambda k, a=a: w[:, s, a, k] for a in range(2)]
                for q, at, width in chunks:
                    if q < 4 and with_z:
                        pe.wait_ge(z_done, nth(4 * (c - 1) + q))
                    else:
                        pe.wait_ge(cv_done, nth(5 * (c - 1) + q))
                    src = x if q < 4 else cx
                    product(pe, bank(q), weights, src, at if q < 4 else 0, width, KT).then_inc(mm, 1)
                if before:
                    transposes(c - 1)
                if with_z:
                    pe.wait_ge(w_split, 2 * c + 2)
                    weights = [lambda k, a=a: w[:, 1, a, k] for a in range(2)]
                    for q in range(4):
                        pe.wait_ge(cv_done, nth(5 * c + q))
                        product(pe, pj[:, q], weights, x, q * BANK, BANK, KT).then_inc(mm, 1)

            def transposes(c):
                pe.wait_ge(x_done, nth(c))
                for n in range(QUADS):
                    pe.wait_ge(xk_done, nth(QUADS * c + (n - 2 if n > 1 else -1)))
                    for a in range(min(4, NCH - 4 * n)):
                        m = 4 * n + a
                        ins = pe.transpose(tr[:, n % 2, a * P:(a + 1) * P], xt[:, m * P:(m + 1) * P], eye[:])
                    ins.then_inc(tr_mm, 1)

            tile(0, 0, False)
            if with_z:
                with pe.Fori(1, tiles) as c:
                    tile(c, 0, True)
            else:
                for c in range(1, tiles):
                    tile(c, c % 2, True)
            transposes(tiles - 1)
            if not with_z:
                for q, at, width in chunks:
                    pe.wait_ge(cv_done, nth(5 * tiles - 5 + q))
                    if q == 0:
                        pe.wait_ge(w_dt_split, 1)
                    weights = [lambda k, a=a: w_dt_parts[:, a, k] for a in range(2)]
                    product(pe, bank(q)[0:2 * HEADS], weights, x if q < 4 else cx, at if q < 4 else 0, width, KT).then_inc(mm, 1)
                pe.wait_ge(dt_done, 5)
                pe.wait_ge(xk_done, nth(QUADS * tiles - 1))
                for n in range(NCH):
                    ins = pe.transpose(tr[:, n // 16, 32 * (n % 16):32 * (n % 16) + 32], dtT[:, n * P:(n + 1) * P], eye[0:32, 0:32])
                ins.then_inc(dt_tr, 1)

        @block.scalar
        def _(act):
            lead(act, z_done, x_done, cv_mid)
            act.wait_ge(consts, CONSTS)
            with act.Fori(0, tiles) as c:
                act.wait_ge(taps_ready, c + 1)
                act.wait_ge(x_done, nth(c - 1))
                for q, at, width in chunks:
                    act.wait_ge(mm, nth(MM * c + q))
                    act.activation(conv[:, at:at + width], bank(q), ACT.Identity, bias=taps_now[:, 3:4], scale=taps_now[:, 1:2]).then_inc(cv_mid, 1)
                act.wait_ge(cv_done, nth(5 * c + 4))
                act.wait_ge(tr_mm, nth(QUADS * c - 1))
                act.wait_ge(xt_out, nth(c - 1, 16))
                act.activation(xt[:], conv[:], ACT.Silu).then_inc(x_done, 1)
                if with_z:
                    act.wait_ge(z_out, nth(c - 1, 16))
                    for q in range(4):
                        act.wait_ge(mm, nth(MM * c + 5 + q))
                        act.activation(zt[:, q * BANK:(q + 1) * BANK], pj[:, q], ACT.Silu).then_inc(z_done, 1)
            if not with_z:
                for q, at, width in chunks:
                    act.wait_ge(mm, nth(MM * tiles + q))
                    act.wait_ge(x_done, nth(tiles - 1))
                    act.activation(dtT[:, at:at + width], bank(q)[0:2 * HEADS], ACT.Copy).then_inc(dt_done, 1)

        @block.vector
        def _(dve):
            lead(dve, cv_done, xk_done)
            dve.wait_ge(consts, CONSTS)

            def convolve(c):
                dve.wait_ge(cv_mid, nth(5 * c - 1))
                dve.wait_ge(cv_done, nth(5 * c - 1))
                dve.tensor_copy(taps_now[:], taps[:, bass.ds(c, 1)].rearrange("p a k -> p (a k)")).then_inc(taps_ready, 1)
                dve.wait_ge(taps_ready, c + 1)
                step = chained(dve, cv_side, 5 * c)
                for q, at, width in chunks:
                    dve.wait_ge(cv_mid, nth(5 * c + q))
                    row = GRID_W if q < 4 else CTX
                    conv_taps(dve, step, conv[:, at:at + width], bank(q), taps_now, width // row, row).then_inc(cv_done, 1)

            def copies(c):
                dve.wait_ge(xk_out, nth(c - 1, 16))
                for n in range(QUADS):
                    m = min(4, NCH - 4 * n)
                    dve.wait_ge(tr_mm, nth(QUADS * c + n))
                    dve.tensor_copy(xk[:, 4 * n:4 * n + m].rearrange("p a c -> p (a c)"), tr[:, n % 2, 0:m * P]).then_inc(xk_done, 1)
            convolve(0)
            with dve.Fori(1, tiles) as c:
                convolve(c)
                copies(c - 1)
            copies(tiles - 1)
            if not with_z:
                dve.wait_ge(dt_tr, 1)
                dve.tensor_copy(dt_raw[:].rearrange("p n h -> p (n h)")[:, 0:BANK], tr[:, 0])
                dve.tensor_copy(dt_raw[:].rearrange("p n h -> p (n h)")[:, BANK:32 * NCH], tr[:, 1, 0:32 * NCH - BANK]).then_inc(dt_copied, 1)
                dve.wait_ge(dt_copied, 1)
def spectra(nc, t, keep):
    with ExitStack() as ph:
        def sem(name):
            return nc.alloc_semaphore(name)

        def sb(name, shape, dt=F32):
            return ph.enter_context(nc.sbuf_tensor("g_" + name, shape, dt))

        def psum(name, shape):
            return ph.enter_context(nc.psum_tensor("g_" + name, shape, F32))

        SLOTS = 4
        sig = sb("sig", [P, SLOTS, D])
        fil = sb("fil", [P, SLOTS, D])
        mats = sb("mats", [P, SLOTS, 5, P])
        ab = sb("ab", [P, 2, 2, BANK])
        prod = sb("prod", [P, 2, 2, BANK])
        back = sb("back", [P, SLOTS, 2, BANK])
        xab = psum("xab", [P, 2, 3, BANK])
        v_ps = psum("v_ps", [P, 2, BANK])
        loaded = [sem(f"g_loaded{s}") for s in range(SLOTS)]
        stored = [sem(f"g_stored{s}") for s in range(SLOTS)]
        x_mm, ab_done, prod_done, v_mm, v_done = (sem("g_" + n) for n in ("x_mm", "ab_done", "prod_done", "v_mm", "v_done"))
        block = ph.enter_context(nc.Block())

        def rows(name, g, r):
            return t[name][:, r, bass.ds(g * FG, FG), :].rearrange("n k c -> k n c")

        @block.gpsimd
        def _(pool):
            with pool.Fori(0, NG // SLOTS) as i:
                for s in range(SLOTS):
                    g = SLOTS * i + s
                    pool.wait_ge(v_mm, nth(2 * (g - SLOTS) + 1))
                    for r in range(2):
                        pool.dma_start(sig[64 * r:64 * r + 64, s], rows("u_spec", g, r)).then_inc(loaded[s], 16)
                        pool.dma_start(fil[64 * r:64 * r + 64, s], rows("f_spec", g, r)).then_inc(loaded[s], 16)
                    pool.dma_start(mats[:, s], t["k_mats"][g]).then_inc(loaded[s], 16)

        @block.sync
        def _(sp):
            lead(sp, *stored, unit=32)
            with sp.Fori(0, NG // SLOTS) as i:
                for s in range(SLOTS):
                    g = SLOTS * i + s
                    sp.wait_ge(v_done, nth(2 * g + 1))
                    for r in range(2):
                        sp.dma_start(rows("v_spec", g, r), back[64 * r:64 * r + 64, s].rearrange("p h c -> p (h c)")).then_inc(stored[s], 32 // 2)
            for s in range(SLOTS):
                sp.wait_ge(stored[s], nth(NG // SLOTS - 1, 32))

        @block.tensor
        def _(pe):
            lead(pe, x_mm, v_mm)

            def forward(g, s, h):
                cols = slice(h * BANK, (h + 1) * BANK)
                pe.matmul(xab[:, h, 0], mats[:, s, 0], sig[:, s, cols], start=True, stop=True)
                for m in (1, 2):
                    ins = pe.matmul(xab[:, h, m], mats[:, s, m], fil[:, s, cols], start=True, stop=True)
                ins.then_inc(x_mm, 1)

            def backward(g, s, h):
                n = 2 * g + h
                pe.wait_ge(prod_done, nth(n))
                pe.wait_ge(v_done, nth(n - 2))
                for m in range(2):
                    ins = pe.matmul(v_ps[:, h], mats[:, s, 3 + m], prod[:, h, m], start=(m == 0), stop=(m == 1))
                ins.then_inc(v_mm, 1)

            def groups(i, first):
                for s in range(SLOTS):
                    g = SLOTS * i + s
                    pe.wait_ge(loaded[s], 80 * i + 80)
                    forward(g, s, 0)
                    if s or not first:
                        backward(g - 1, (s - 1) % SLOTS, 1)
                    forward(g, s, 1)
                    backward(g, s, 0)
            groups(0, True)
            with pe.Fori(1, NG // SLOTS) as i:
                groups(i, False)
            backward(NG - 1, SLOTS - 1, 1)

        @block.scalar
        def _(act):
            lead(act, ab_done, v_done)

            def filter_parts(n, h):
                act.wait_ge(x_mm, nth(n))
                act.wait_ge(prod_done, nth(n - 2))
                act.activation(ab[:, h], xab[:, h, 1:3], ACT.Copy).then_inc(ab_done, 1)

            def keep_back(n, i, s, h):
                act.wait_ge(v_mm, nth(n))
                act.wait_ge(stored[s], nth(i - 1, 32))
                act.activation(back[:, s, h], v_ps[:, h], ACT.Copy).then_inc(v_done, 1)

            def groups(i, first):
                for s in range(SLOTS):
                    n = 2 * (SLOTS * i + s)
                    filter_parts(n, 0)
                    if s:
                        keep_back(n - 1, i, s - 1, 1)
                    elif not first:
                        keep_back(n - 1, i - 1, SLOTS - 1, 1)
                    filter_parts(n + 1, 1)
                    keep_back(n, i, s, 0)
            groups(0, True)
            with act.Fori(1, NG // SLOTS) as i:
                groups(i, False)
            keep_back(2 * NG - 1, NG // SLOTS - 1, SLOTS - 1, 1)

        @block.vector
        def _(dve):
            lead(dve, prod_done)
            with dve.Fori(0, NG // SLOTS) as i:
                for s in range(SLOTS):
                    for h in range(2):
                        n = 2 * SLOTS * i + 2 * s + h
                        dve.wait_ge(ab_done, nth(n))
                        dve.wait_ge(v_mm, nth(n - 2))
                        dve.tensor_tensor(prod[:, h, 0], xab[:, h, 0], ab[:, h, 0], ALU.mult)
                        dve.tensor_tensor(prod[:, h, 1], xab[:, h, 0], ab[:, h, 1], ALU.mult).then_inc(prod_done, 1)


def hyena_back(nc, t, keep, ph, block):
    with ExitStack() as banks:
        def sem(name):
            return nc.alloc_semaphore(name)

        def sb(name, shape, dt=F32):
            return ph.enter_context(nc.sbuf_tensor("c_" + name, shape, dt))

        def psum(name, shape):
            return banks.enter_context(nc.psum_tensor("c_" + name, shape, F32))

        ssh = keep["ssh"]
        CT, SLOTS = D // P, 2
        back = sb("back", [P, 2, P])
        z = sb("z", [P, SLOTS, 2, RIN, P])
        gate = sb("gate", [P, SLOTS, SEQ])
        y = sb("y", [P, SLOTS, SEQ])
        sq = sb("sq", [P, SEQ])
        total = sb("total", [P, SEQ])
        ones = sb("ones", [P, 1])
        y_ps = psum("y_ps", [P, 4, BANK])
        s_ps = psum("s_ps", [P, BANK])
        loaded = [sem(f"c_loaded{s}") for s in range(SLOTS)]
        stored = [sem(f"c_stored{s}") for s in range(SLOTS)]
        consts, y_mm, y_read, sq_done, s_mm, s_done, ones_done = (sem("c_" + n) for n in (
            "consts", "y_mm", "y_read", "sq_done", "s_mm", "s_done", "ones_done"))
        y_done = keep["c_y_done"]

        @block.gpsimd
        def _(pool):
            with pool.Fori(0, CT // SLOTS) as i:
                for s in range(SLOTS):
                    c = SLOTS * i + s
                    pool.wait_ge(y_done, nth(c - SLOTS))
                    for r in range(2):
                        pool.dma_start(z[:, s, r], t["v_spec"][:, r, :, bass.ds(c * P, P)].rearrange("n k c -> k n c")).then_inc(loaded[s], 16)
                    pool.dma_start(gate[:, s], t["gate_t"][c]).then_inc(loaded[s], 16)

        @block.sync
        def _(sp):
            sp.dma_start(back[:], t["k_back"]).then_inc(consts, 16)
            lead(sp, *stored, unit=16)
            with sp.Fori(0, CT // SLOTS) as i:
                for s in range(SLOTS):
                    c = SLOTS * i + s
                    sp.wait_ge(y_done, nth(c))
                    sp.dma_start(t["yh_t"][c], y[:, s]).then_inc(stored[s], 16)
            for s in range(SLOTS):
                sp.wait_ge(stored[s], nth(CT // SLOTS - 1, 16))

        @block.tensor
        def _(pe):
            lead(pe, y_mm)
            pe.wait_ge(consts, 16)
            pe.wait_ge(keep["scales_read"], 2)
            pe.wait_ge(ones_done, 1)
            with pe.Fori(0, CT // SLOTS) as i:
                for s in range(SLOTS):
                    c = SLOTS * i + s
                    pe.wait_ge(loaded[s], 48 * i + 48)
                    for q in range(4):
                        pe.wait_ge(y_read, nth(4 * (c - 1) + q))
                        for a in range(4):
                            n2 = 4 * q + a
                            for r in range(2):
                                ins = pe.matmul(y_ps[:, q, a * P:(a + 1) * P], z[:, s, r, n2], back[:, r], start=(r == 0), stop=(r == 1))
                        ins.then_inc(y_mm, 1)
            pe.wait_ge(s_done, nth(CT - 1))
            for n in range(NC_LAT):
                ins = pe.matmul(s_ps[:, n:n + 1], total[:, n * P:(n + 1) * P], ones[:], start=True, stop=True)
            ins.then_inc(s_mm, 1)

        @block.scalar
        def _(act):
            lead(act, sq_done)
            with act.Fori(0, CT // SLOTS) as i:
                for s in range(SLOTS):
                    c = SLOTS * i + s
                    act.wait_ge(y_done, nth(c))
                    act.wait_ge(s_done, nth(c - 1))
                    act.activation(sq[:], y[:, s], ACT.Square).then_inc(sq_done, 1)

        @block.vector
        def _(dve):
            lead(dve, y_read, s_done)
            dve.memset(total[:], 0.0)
            dve.memset(ones[:], 1.0).then_inc(ones_done, 1)
            dve.wait_ge(ones_done, 1)
            with dve.Fori(0, CT // SLOTS) as i:
                for s in range(SLOTS):
                    c = SLOTS * i + s
                    dve.wait_ge(loaded[s], 48 * i + 48)
                    dve.wait_ge(stored[s], nth(i - 1, 16))
                    dve.wait_ge(sq_done, nth(c - SLOTS))
                    for q in range(4):
                        dve.wait_ge(y_mm, nth(4 * c + q))
                        def tok(a):
                            return a[:, s].rearrange("p (n k) -> p k n", k=RIN)[:, 4 * q:4 * q + 4]
                        dve.tensor_tensor(tok(y), y_ps[:, q].rearrange("p (k n) -> p k n", n=P), tok(gate), ALU.mult).then_inc(y_read, 1)
                    dve.wait_ge(y_read, nth(4 * c + 3))
                    dve.sem_inc(y_done, 1)
                    dve.wait_ge(sq_done, nth(c))
                    dve.wait_ge(s_done, nth(c - 1))
                    dve.tensor_tensor(total[:], total[:], sq[:], ALU.add).then_inc(s_done, 1)
            dve.wait_ge(s_mm, 1)
            dve.tensor_copy(ssh[:], s_ps[:, 0:NC_LAT])
ROWS_SHAPE = [NC_LAT, 2, 3, HEADS * CHUNK]
STEPS_LN = 8


def per_head(a, n, side):
    return a[:, bass.ds(n, 1), side * HEADS:(side + 1) * HEADS].rearrange("p a h -> p (a h)").unsqueeze(2).to_broadcast([P, HEADS, HEADDIM])


def by_head(a):
    return a.rearrange("p (h d) -> p h d", h=HEADS)


def ssd_scales(nc, t, keep, ph, block):
    with ExitStack() as banks:
        def sem(name):
            return nc.alloc_semaphore(name)

        def sb(name, shape, dt=F32):
            return ph.enter_context(nc.sbuf_tensor("q_" + name, shape, dt))

        def psum(name, shape):
            return banks.enter_context(nc.psum_tensor("q_" + name, shape, F32))

        dt, te, cd = keep["dt_raw"], keep["to_end"], keep["chunk_decay"]
        W = 2 * HEADS
        bias = sb("bias", [P, W])
        a_neg = sb("a_neg", [P, W])
        tri = sb("tri", [P, 2, P])
        ones = sb("ones", [P, P])
        e = sb("e", [P, NCH, W])
        s = sb("s", [P, NCH, W])
        q = sb("q", [P, NCH, W])
        pos = sb("pos", [P, NCH, W])
        da = sb("da", [P, NCH, W])
        rows = sb("rows", [HEADS, SEQ])
        parts = sb("parts", [HEADS, 2, 3, SEQ], BF16)
        cum_ps = psum("cum_ps", [P, 2, BANK])
        tot_ps = psum("tot_ps", [P, 2, BANK])
        row_ps = psum("row_ps", [HEADS, 4, BANK])
        consts, v_step, e_in, e_out, log_done, exp_a, da_done, sums, rows_mm, rows_used, expo, stored = (sem("q_" + n) for n in (
            "consts", "v_step", "e_in", "e_out", "log_done", "exp_a", "da_done", "sums", "rows_mm", "rows_used", "expo", "stored"))
        weights, a_ready, parts_done = sem("q_weights"), sem("q_a_ready"), sem("q_parts_done")
        keep["scales_read"] = parts_done

        @block.sync
        def _(sp):
            sp.dma_start(bias[:], t["dt_bias"][0].rearrange("s h -> (s h)").partition_broadcast(P)).then_inc(consts, 16)
            sp.dma_start(a_neg[:], t["a_log"][0].rearrange("s h -> (s h)").partition_broadcast(P)).then_inc(consts, 16)
            sp.dma_start(tri[:], t["k_tri"]).then_inc(consts, 16)
            sp.wait_ge(parts_done, 2)
            for side in range(2):
                for k in range(3):
                    sp.dma_start(t["rows"][:, side, k].rearrange("n (h i) -> h n i", h=HEADS),
                                 parts[:, side, k].rearrange("h (n i) -> h n i", n=NC_LAT)).then_inc(stored, 16)
            sp.wait_ge(stored, 96)

        @block.scalar
        def _(act):
            act.wait_ge(consts, 48)
            act.activation(a_neg[:], a_neg[:], ACT.Exp).then_inc(exp_a, 1)
            act.wait_ge(e_in, 1)
            act.activation(e[:], e[:], ACT.Exp).then_inc(e_out, 1)
            act.wait_ge(weights, 1)
            act.activation(te[:], te[:], ACT.Exp).then_inc(expo, 1)
            act.activation(cd[:], cd[:], ACT.Exp).then_inc(expo, 1)

        @block.tensor
        def _(pe):
            pe.wait_ge(da_done, 1)
            for side in range(2):
                cols = slice(side * HEADS, (side + 1) * HEADS)
                w = NCH * HEADS
                pe.matmul(cum_ps[:, side, 0:w], tri[:, side], da[:, :, cols], start=True, stop=True)
                ins = pe.matmul(tot_ps[:, side, 0:w], ones[:], da[:, :, cols], start=True, stop=True)
            ins.then_inc(sums, 1)
            for side in range(2):
                cols = slice(side * HEADS, (side + 1) * HEADS)
                if side:
                    pe.wait_ge(rows_used, 1)
                for n in range(NC_LAT):
                    ins = pe.matmul(row_ps[:, n // 4, (n % 4) * P:(n % 4 + 1) * P], da[:, n, cols], tri[:, side], start=True, stop=True)
                ins.then_inc(rows_mm, 1)

        @block.vector
        def _(dve):
            step = chained(dve, v_step)
            lead(dve, keep["c_y_done"])
            dve.memset(ones[:], 1.0)
            dve.wait_ge(consts, 48)
            step(dve.tensor_tensor(dt[:], dt[:], bias[:].unsqueeze(1).to_broadcast([P, NCH, W]), ALU.add))
            step(dve.tensor_scalar(pos[:], dt[:], 0.0, None, ALU.max))
            step(dve.tensor_scalar(e[:], dt[:], -1.0, None, ALU.mult))
            dve.tensor_tensor(e[:], e[:], dt[:], ALU.min).then_inc(e_in, 1)
            dve.wait_ge(e_out, 1)
            step(dve.tensor_scalar(s[:], e[:], 2.0, None, ALU.add))
            step(dve.reciprocal(s[:], s[:]))
            step(dve.tensor_tensor(s[:], s[:], e[:], ALU.mult))
            step(dve.tensor_tensor(q[:], s[:], s[:], ALU.mult))
            step(dve.tensor_scalar(e[:], q[:], 1.0 / (2 * STEPS_LN + 1), None, ALU.mult))
            for k in range(STEPS_LN - 1, 0, -1):
                step(dve.scalar_tensor_tensor(e[:], e[:], 1.0 / (2 * k + 1), q[:], ALU.add, ALU.mult))
            step(dve.scalar_tensor_tensor(e[:], e[:], 1.0, s[:], ALU.add, ALU.mult))
            step(dve.scalar_tensor_tensor(dt[:], e[:], 2.0, pos[:], ALU.mult, ALU.add))
            dve.wait_ge(exp_a, 1)
            step(dve.tensor_scalar(a_neg[:], a_neg[:], -1.0, None, ALU.mult))
            dve.tensor_tensor(da[:], dt[:], a_neg[:].unsqueeze(1).to_broadcast([P, NCH, W]), ALU.mult).then_inc(da_done, 1)
            dve.wait_ge(sums, 1)
            for side in range(2):
                cols = slice(side * HEADS, (side + 1) * HEADS)

                def chunks(a):
                    return a[:, side, 0:NCH * HEADS].rearrange("p (n h) -> p n h", n=NCH)
                step(dve.tensor_copy(cd[:, :, cols], chunks(tot_ps)))
                ins = dve.tensor_tensor(te[:, :, cols], cd[:, :, cols], chunks(cum_ps), ALU.subtract)
                if side == 0:
                    step(ins)
            ins.then_inc(weights, 1)
            for side in range(2):
                dve.wait_ge(rows_mm, side + 1)
                dve.tensor_copy(rows[:], row_ps[:].rearrange("p a b -> p (a b)")).then_inc(rows_used, 1)
                dve.wait_ge(rows_used, side + 1)
                step(dve.tensor_copy(parts[:, side, 0], rows[:]))
                step(dve.tensor_tensor(rows[:], rows[:], parts[:, side, 0], ALU.subtract))
                step(dve.tensor_copy(parts[:, side, 1], rows[:]))
                step(dve.tensor_tensor(rows[:], rows[:], parts[:, side, 1], ALU.subtract))
                dve.tensor_copy(parts[:, side, 2], rows[:]).then_inc(parts_done, 1)
                dve.wait_ge(parts_done, side + 1)
            dve.wait_ge(expo, 2)
            dve.tensor_tensor(te[:], te[:], dt[:], ALU.mult)


def ssd_backward_states(nc, t, keep):
    with ExitStack() as ph:
        def sem(name):
            return nc.alloc_semaphore(name)

        def sb(name, shape, dt=F32):
            return ph.enter_context(nc.sbuf_tensor("r_" + name, shape, dt))

        te, cd = keep["to_end"], keep["chunk_decay"]
        XB = D + GROUPS * STATE
        xb = sb("xb", [P, 2, XB])
        xw = sb("xw", [P, 2, D])
        h = sb("h", [P, 2, D])
        h_ps = ph.enter_context(nc.psum_tensor("r_h_ps", [P, 2, D], F32))
        loaded = [sem(f"r_loaded{s}") for s in range(2)]
        stored = [sem(f"r_stored{s}") for s in range(2)]
        xw_done, h_mm, h_decayed, h_done, h_zero, sp_passed, pool_passed, dve_passed = (sem("r_" + n) for n in (
            "xw_done", "h_mm", "h_decayed", "h_done", "h_zero", "sp_passed", "pool_passed", "dve_passed"))
        block = ph.enter_context(nc.Block())

        @block.gpsimd
        def _(pool):
            with pool.Fori(0, NCH // 2) as i:
                for s in range(2):
                    m = 2 * i + s
                    pool.wait_ge(h_mm, nth(m - 2))
                    pool.sem_inc(pool_passed, 1)
                    pool.dma_start(xb[:, s], t["xbc"][NCH - 1 - m][:, 0:XB]).then_inc(loaded[s], 16)

        @block.sync
        def _(sp):
            lead(sp, *stored, unit=16)
            with sp.Fori(0, NCH // 2) as i:
                for s in range(2):
                    m = 2 * i + s
                    sp.wait_ge(h_done, nth(m - 1))
                    sp.sem_inc(sp_passed, 1)
                    sp.dma_start(t["h_back"][NCH - 1 - m], h[:, s]).then_inc(stored[s], 16)
            for s in range(2):
                sp.wait_ge(stored[s], nth(NCH // 2 - 1, 16))

        @block.tensor
        def _(pe):
            lead(pe, h_mm)
            with pe.Fori(0, NCH // 2) as i:
                for s in range(2):
                    m = 2 * i + s
                    pe.wait_ge(loaded[s], 16 * i + 16)
                    pe.wait_ge(xw_done, nth(m))
                    pe.wait_ge(h_done, nth(m - 2))
                    for g in range(GROUPS):
                        ins = pe.matmul(h_ps[:, s, g * BANK:(g + 1) * BANK], xb[:, s, D + g * STATE:D + (g + 1) * STATE],
                                        xw[:, s, g * BANK:(g + 1) * BANK], start=True, stop=True)
                    ins.then_inc(h_mm, 1)

        @block.vector
        def _(dve):
            lead(dve, xw_done, h_decayed)
            dve.memset(h[:, 0], 0.0).then_inc(h_zero, 1)
            dve.wait_ge(h_zero, 1)
            lead(dve, h_done)
            with dve.Fori(0, NCH // 2) as i:
                for s in range(2):
                    m = 2 * i + s
                    n = NCH - 1 - m
                    dve.wait_ge(loaded[s], 16 * i + 16)
                    dve.wait_ge(h_mm, nth(m - 2))
                    dve.sem_inc(dve_passed, 1)
                    dve.tensor_tensor(by_head(xw[:, s]), by_head(xb[:, s, 0:D]), per_head(te, n, 1), ALU.mult).then_inc(xw_done, 1)
                    dve.wait_ge(stored[1 - s], nth(i - 1 + s, 16))
                    dve.sem_inc(dve_passed, 1)
                    dve.tensor_tensor(by_head(h[:, 1 - s]), by_head(h[:, s]), per_head(cd, n, 1), ALU.mult).then_inc(h_decayed, 1)
                    dve.wait_ge(h_decayed, nth(m))
                    dve.wait_ge(h_mm, nth(m))
                    dve.tensor_tensor(h[:, 1 - s], h[:, 1 - s], h_ps[:, s], ALU.add).then_inc(h_done, 1)
                    dve.wait_ge(h_done, nth(m))


def ssd_and_out(nc, t, keep):
    with ExitStack() as ph:
        def sem(name):
            return nc.alloc_semaphore(name)

        def sb(name, shape, dt=F32):
            return ph.enter_context(nc.sbuf_tensor("o_" + name, shape, dt))

        def psum(name, shape):
            return ph.enter_context(nc.psum_tensor("o_" + name, shape, F32))

        dt, te, cd, ssh, gate_row = keep["dt_raw"], keep["to_end"], keep["chunk_decay"], keep["ssh"], keep["gate_row"]
        XB = D + GROUPS * STATE
        HALF = BANK
        w_out = sb("w_out", [P, 2 * KT, D])
        gn = sb("gn", [P, 2 * KT])
        fw = sb("fw", [P, D])
        dk = sb("dk", [P, 2, KT])
        tri = sb("tri", [P, 2, P])
        ones = sb("ones", [P, 1])
        ones_b = sb("ones_b", [3, HEADDIM], BF16)
        halves = sb("halves", [P, NC_LAT])
        eps = sb("eps", [P, 1])
        xk = sb("xk", [P, 2, XB])
        bc = sb("bc", [P, 2, 2 * GROUPS, P])
        xt = sb("xt", [P, 2, KT, P])
        zs = sb("zs", [P, 2, KT, P])
        hb = sb("hb", [P, 2, D])
        yh = sb("yh", [P, KT, P])
        xres = sb("xres", [P, D])
        row_i = sb("row_i", [6, 2, HEADS * CHUNK], BF16)
        row_j = sb("row_j", [6, 2, HEADS * CHUNK], BF16)
        cb_now = sb("cb_now", [P, GROUPS, P])
        es = sb("es", [P, HEADS, P])
        wt = sb("wt", [P, HEADS, P])
        dt_now = sb("dt_now", [P, 2 * HEADS])
        ea = sb("ea", [P, 2, 2, HALF])
        xw = sb("xw", [P, D])
        h = sb("h", [P, D])
        ys = sb("ys", [P, KT, P])
        tmp = sb("tmp", [P, 2, BANK])
        sq = sb("sq", [P, KT, P])
        rs = sb("rs", [P, 4])
        o = sb("o", [P, D])
        ob = sb("ob", [P, D])
        o_ps = psum("o_ps", [P, 2, BANK])
        d_ps = psum("d_ps", [P, 2, BANK])
        in_ps = psum("in_ps", [P, 2, BANK])
        y_ps = psum("y_ps", [P, BANK])
        m_ps = psum("m_ps", [P, BANK])

        names = ("consts w_in_ w_ready prep h_zero xw_done cb_mm cb_done s_mm dc_done dm_done e_done wb_done w_step ml_done "
                 "r_mm y_read y_done v_step ys_done h_mm h_done sq_step sq_done sq_sum ss_mm ss_done rs_done o_mm oa_done ob_done "
                 "sp_passed o_pre fsq_done frs_done fin_done hn_done p_step rsh_done rows_set xt_done h_dec f_step")
        S = {n: sem("o_" + n) for n in names.split()}
        early = [sem(f"o_early{s}") for s in range(2)]
        ctx_in = [sem(f"o_ctx_in{s}") for s in range(2)]
        rows_in, late_in, stored = sem("o_rows_in"), sem("o_late_in"), sem("o_stored")
        EARLY = 16 * 5
        block = ph.enter_context(nc.Block())
        LAST = NC_LAT - 1

        def pairs(eng, body, head=0, count=NC_LAT // 2 - 1):
            with eng.Fori(0, count) as i:
                for j in range(2):
                    n = head + j
                    body(2 * i + n, i + n // 2, n % 2)
            for n in range(head + 2 * count, NC_LAT):
                body(n, n // 2, n % 2)

        @block.sync
        def _(sp):
            def load_early(n, s):
                sp.wait_ge(S["ys_done"], nth(2 * (n - 2) + 1))
                sp.sem_inc(S["sp_passed"], 1)
                sp.wait_ge(S["h_mm"], nth(n))
                sp.sem_inc(S["sp_passed"], 1)
                sp.dma_start(xk[:, s], t["xbc"][n][:, 0:XB]).then_inc(early[s], 16)
                cols = bass.ds(n * P, P)
                sp.dma_start(bc[:, s], t["xbc_t"][KT:XBC_T][:, :, cols].rearrange("m p t -> p m t")).then_inc(early[s], 16)
                sp.dma_start(xt[:, s], t["xbc_t"][0:KT][:, :, cols].rearrange("m p t -> p m t")).then_inc(early[s], 16)
                sp.dma_start(zs[:, s], t["zs_t"][:, :, cols].rearrange("m p t -> p m t")).then_inc(early[s], 16)
                sp.dma_start(hb[:, s], t["h_back"][n]).then_inc(early[s], 16)

            def load_rows(n):
                sp.wait_ge(S["s_mm"], nth(6 * (n - 1) + 5))
                sp.sem_inc(S["sp_passed"], 1)
                sp.wait_ge(S["rows_set"], 1)
                rows = t["rows"][n].rearrange("s k c -> k s c")
                sp.dma_start(row_i[0:3], rows).then_inc(rows_in, 16)
                sp.dma_start(row_j[3:6], rows).then_inc(rows_in, 16)

            def load_late(n):
                sp.wait_ge(S["o_mm"], nth(4 * (n - 1) + 2))
                sp.sem_inc(S["sp_passed"], 1)
                sp.wait_ge(S["o_pre"], nth(n - 1))
                sp.sem_inc(S["sp_passed"], 1)
                sp.dma_start(yh[:], t["yh_t"][:, :, bass.ds(n * P, P)].rearrange("m p t -> p m t")).then_inc(late_in, 16)
                sp.dma_start(xres[:], t["x"][0][bass.ds(n * P, P)]).then_inc(late_in, 16)

            def store(n):
                sp.wait_ge(S["fin_done"], nth(n))
                sp.sem_inc(S["sp_passed"], 1)
                sp.dma_start(t["out"][0][bass.ds(n * P, P)], ob[:]).then_inc(stored, 16)

            for s in range(2):
                sp.dma_start(xk[:, s], t["xbc"][NC_LAT + s][:, 0:XB]).then_inc(ctx_in[s], 16)
            with nc.allow_non_contiguous_dma(reason="small vectors"):
                sp.dma_start(gn[:], t["gnorm_w"][0].rearrange("(m p) -> p m", p=P)).then_inc(S["consts"], 16)
                sp.dma_start(fw[:], t["final_norm_w"].partition_broadcast(P)).then_inc(S["consts"], 16)
                for side in range(2):
                    for par in range(2):
                        sp.dma_start(dk[64 * par:64 * par + 64, side],
                                     t["d_skip"][0, side].rearrange("(m two) -> two m", two=2)[par].partition_broadcast(HEADDIM)).then_inc(S["consts"], 16)
                sp.dma_start(tri[:], t["k_tri"]).then_inc(S["consts"], 16)
            sp.dma_start(w_out[:], t["w_out"][0].rearrange("(k p) d -> p k d", p=P)).then_inc(S["w_in_"], 16)
            lead(sp, stored, unit=16)
            load_early(0, 0)
            load_rows(0)

            def body(n, i, s):
                load_early(n + 1, 1 - s)
                load_rows(n + 1)
                load_late(n)
                store(n - 1)
            load_early(1, 1)
            load_rows(1)
            load_late(0)
            with sp.Fori(0, LAST // 2) as i:
                for j in range(2):
                    n = 2 * i + 1 + j
                    body(n, None, (1 + j) % 2)
            load_late(LAST)
            store(LAST - 1)
            store(LAST)
            sp.wait_ge(stored, nth(LAST, 16))

        @block.gpsimd
        def _(pool):
            step = chained(pool, S["p_step"])
            pool.memset(halves[:], -0.5)
            pool.memset(eps[:], EPS)
            pool.memset(row_i[:], -1.0)
            step(pool.memset(row_j[:], 1.0))
            pool.sem_inc(S["rows_set"], 1)
            pool.wait_ge(S["consts"], 16 * 7)
            step(pool.tensor_tensor(dk[:, 0], dk[:, 0], dk[:, 1], ALU.add))
            step(pool.tensor_scalar(ssh[:], ssh[:], 1.0 / D, EPS, ALU.mult, ALU.add))
            pool.tensor_tensor(ssh[:], ssh[:], halves[:], ALU.pow).then_inc(S["rsh_done"], 1)
            lead(pool, S["xw_done"], S["rs_done"], S["frs_done"], S["xt_done"], S["ys_done"], S["sq_sum"])

            def weigh(n, s, m):
                pool.wait_ge(S["h_mm"], nth(m - 1))
                pool.tensor_tensor(by_head(xw[:]), by_head(xk[:, s, 0:D]), per_head(te, n, 0), ALU.mult).then_inc(S["xw_done"], 1)

            for s in range(2):
                pool.wait_ge(ctx_in[s], 16)
                weigh(NC_LAT + s, s, s)

            def chunk(n, i, s):
                pool.wait_ge(early[s], EARLY * i + EARLY)
                pool.tensor_tensor(xt[:, s], xt[:, s], dk[:, 0].unsqueeze(2).to_broadcast([P, KT, P]), ALU.mult).then_inc(S["xt_done"], 1)
                weigh(n, s, n + 2)

            def gather(n, s, f):
                q = slice(4 * f, 4 * f + 4)
                out = ys[:, q].rearrange("p m i -> p (m i)")
                pool.wait_ge(S["y_read"], nth(2 * n + f))
                step = chained(pool, S["y_done"], 4 * n + 2 * f)
                step(pool.tensor_tensor(out, out, tmp[:, f], ALU.add))
                step(pool.tensor_tensor(out, out, xt[:, s, q].rearrange("p m i -> p (m i)"), ALU.add))
                pool.tensor_tensor(out, out, zs[:, s, q].rearrange("p m i -> p (m i)"), ALU.mult).then_inc(S["ys_done"], 1)

            def sum_tiles(n):
                pool.wait_ge(S["sq_done"], nth(n))
                step = chained(pool, S["sq_step"], 2 * n)
                step(pool.tensor_tensor(sq[:, 0:4], sq[:, 0:4], sq[:, 4:8], ALU.add))
                step(pool.tensor_tensor(sq[:, 0:2], sq[:, 0:2], sq[:, 2:4], ALU.add))
                pool.tensor_tensor(sq[:, 0], sq[:, 0], sq[:, 1], ALU.add).then_inc(S["sq_sum"], 1)

            def ssd_power(n):
                pool.wait_ge(S["ss_done"], nth(n))
                pool.tensor_tensor(rs[:, 0:1], rs[:, 0:1], halves[:, 0:1], ALU.pow).then_inc(S["rs_done"], 1)

            def final_power(n):
                pool.wait_ge(S["fsq_done"], nth(n))
                pool.tensor_tensor(rs[:, 1:2], rs[:, 3:4], eps[:], ALU.add).then_inc(S["f_step"], 1)
                pool.wait_ge(S["f_step"], n + 1)
                pool.tensor_tensor(rs[:, 1:2], rs[:, 1:2], halves[:, 0:1], ALU.pow).then_inc(S["frs_done"], 1)

            chunk(0, 0, 0)

            def body(n, i, s):
                gather(n, s, 0)
                gather(n, s, 1)
                if not isinstance(n, int) or n > 0:
                    final_power(n - 1)
                sum_tiles(n)
                if not (isinstance(n, int) and n == LAST):
                    chunk(n + 1, i + s, 1 - s)
                ssd_power(n)
            body(0, 0, 0)
            pairs(pool, body, head=1)
            final_power(LAST)

        @block.tensor
        def _(pe):
            lead(pe, S["cb_mm"], S["s_mm"], S["r_mm"], S["h_mm"], S["ss_mm"], S["o_mm"])

            def state(s, m):
                pe.wait_ge(S["xw_done"], nth(m))
                for g in range(GROUPS):
                    ins = pe.matmul(in_ps[:, g], xk[:, s, D + g * STATE:D + (g + 1) * STATE], xw[:, g * BANK:(g + 1) * BANK], start=True, stop=True)
                ins.then_inc(S["h_mm"], 1)

            def cb(n, i, s):
                pe.wait_ge(early[s], EARLY * i + EARLY)
                pe.wait_ge(S["ss_done"], nth(n - 2))
                for g in range(GROUPS):
                    ins = pe.matmul(m_ps[:, g * P:(g + 1) * P], bc[:, s, g], bc[:, s, GROUPS + g], start=True, stop=True)
                ins.then_inc(S["cb_mm"], 1)

            def quad(n, k):
                if k == 0:
                    pe.wait_ge(rows_in, 32 * n + 32)
                pe.wait_ge(S["dc_done"], nth(6 * n + k - 1))
                pe.wait_ge(S["dm_done"], nth(4 * n + min(k, 4) - 1))
                for side in range(2):
                    if k < 4:
                        for a in range(4):
                            cols = slice((4 * k + a) * P, (4 * k + a + 1) * P)
                            ins = pe.matmul(d_ps[:, side, a * P:(a + 1) * P], row_j[:, side, cols], row_i[:, side, cols], start=True, stop=True)
                    else:
                        for par in range(2):
                            src = row_i[0:3, side].rearrange("q (m two i) -> q two m i", two=2, i=P)[:, par, 4 * (k - 4):4 * (k - 4) + 4]
                            ins = pe.matmul(d_ps[64 * par:64 * par + 64, side], ones_b[:], src, start=True, stop=True)
                ins.then_inc(S["s_mm"], 1)

            def rest(n, i, s):
                for f in range(2):
                    pe.wait_ge(S["y_read"], nth(2 * n + f - 1))
                    if f == 0:
                        pe.wait_ge(S["h_done"], nth(n + 1))
                    for a in range(4):
                        m = 4 * f + a
                        c_now = bc[:, s, GROUPS + m // 4]
                        out = slice(a * P, (a + 1) * P)
                        pe.matmul(in_ps[:, 0, out], h[:, m * P:(m + 1) * P], c_now, start=True, stop=True)
                        pe.matmul(in_ps[:, 1, out], hb[:, s, m * P:(m + 1) * P], c_now, start=True, stop=True)
                    pe.wait_ge(S["ml_done"], nth(4 * n + 2 * f + 1))
                    for a in range(4):
                        for par in range(2):
                            hd = 8 * f + 2 * a + par
                            out = y_ps[64 * par:64 * par + 64, a * P:(a + 1) * P]
                            cols = slice(hd * HEADDIM, (hd + 1) * HEADDIM)
                            ins = pe.matmul(out, xk[:, s, cols], es[:, hd], start=True, stop=True)
                    ins.then_inc(S["r_mm"], 1)

            def sum_squares(n):
                pe.wait_ge(S["sq_sum"], nth(n))
                if not (isinstance(n, int) and n == LAST):
                    pe.wait_ge(S["cb_done"], nth(n + 1))
                pe.matmul(m_ps[:, 0:1], sq[:, 0], ones[:], start=True, stop=True).then_inc(S["ss_mm"], 1)

            def quarter(n, k):
                half, part = k // 2, k % 2
                if k == 0:
                    pe.wait_ge(S["w_ready"], 1)
                    pe.wait_ge(late_in, 32 * n + 32)
                if k == 1:
                    pe.wait_ge(S["ys_done"], nth(2 * n + 1))
                pe.wait_ge(S[("oa_done", "ob_done")[part]], nth(2 * n + half - 1))
                for a in range(KT):
                    src = yh[:, a] if part == 0 else ys[:, a]
                    ins = pe.matmul(o_ps[:, part], src, w_out[:, (1 - part) * KT + a, half * BANK:(half + 1) * BANK], start=(a == 0), stop=(a == KT - 1))
                ins.then_inc(S["o_mm"], 1)

            pe.wait_ge(S["prep"], 1)
            for s in range(2):
                if s:
                    pe.wait_ge(S["h_done"], nth(0))
                state(s, s)
            cb(0, 0, 0)
            for k in range(6):
                quad(0, k)

            def body(n, i, s):
                last = isinstance(n, int) and n == LAST
                rest(n, i, s)
                if not last:
                    cb(n + 1, i + s, 1 - s)
                    quad(n + 1, 0)
                pe.wait_ge(S["y_read"], nth(2 * n + 1))
                state(s, n + 2)
                quarter(n, 0)
                for k in range(1, 4):
                    if not last:
                        quad(n + 1, k)
                    if k == 1:
                        sum_squares(n)
                    quarter(n, k)
                if not last:
                    quad(n + 1, 4)
                    quad(n + 1, 5)
            pairs(pe, body)

        @block.scalar
        def _(act):
            lead(act, S["wb_done"], S["dc_done"], S["e_done"], S["sq_done"], S["oa_done"], S["fsq_done"])

            def behind(n, k):
                act.wait_ge(S["cb_done"], nth(n))
                if k == 0:
                    act.wait_ge(S["ml_done"], nth(4 * (n - 1) + 3))
                for head in range(4 * k, 4 * k + 4):
                    ins = act.activation(wt[:, head], tri[:, 1], ACT.Identity, scale=dt_now[:, HEADS + head:HEADS + head + 1])
                ins.then_inc(S["wb_done"], 1)

            def copy(n, k):
                behind(n, k)
                act.wait_ge(S["s_mm"], nth(6 * n + k))
                if k == 0:
                    act.wait_ge(S["r_mm"], nth(2 * (n - 1) + 1))
                act.activation(es[:, 4 * k:4 * k + 4].rearrange("p h i -> p (h i)"), d_ps[:, 0], ACT.Copy).then_inc(S["dc_done"], 1)

            def exp(n, k):
                act.wait_ge(S["dm_done"], nth(4 * n + k))
                cols = es[:, 4 * k:4 * k + 4]
                act.activation(cols, cols, ACT.Exp).then_inc(S["e_done"], 1)

            def exp_sums(n, k):
                act.wait_ge(S["s_mm"], nth(6 * n + k))
                act.wait_ge(S["ys_done"], nth(2 * (n - 1) + 1))
                act.activation(ea[:, k - 4], d_ps[:], ACT.Exp).then_inc(S["dc_done"], 1)

            def out_part(n, half):
                act.wait_ge(S["o_mm"], nth(4 * n + 2 * half))
                if half == 0:
                    act.wait_ge(S["hn_done"], nth(n))
                    act.wait_ge(S["fin_done"], nth(n - 1))
                act.activation(o[:, half * BANK:(half + 1) * BANK], o_ps[:, 0], ACT.Identity, scale=rs[:, 2:3]).then_inc(S["oa_done"], 1)

            def head(n, with_out):
                copy(n, 0)
                exp(n, 0)
                if with_out:
                    out_part(n - 1, 0)
                copy(n, 1)
                exp(n, 1)
                copy(n, 2)
                exp(n, 2)
                if with_out:
                    out_part(n - 1, 1)
                copy(n, 3)
                exp(n, 3)
                exp_sums(n, 4)
                exp_sums(n, 5)

            def body(n, i, s):
                act.wait_ge(S["ys_done"], nth(2 * n + 1))
                act.wait_ge(S["ss_mm"], nth(n - 1))
                act.activation(sq[:], ys[:], ACT.Square).then_inc(S["sq_done"], 1)
                if isinstance(n, int) and n == LAST:
                    out_part(n, 0)
                    out_part(n, 1)
                else:
                    head(n + 1, True)
                act.wait_ge(S["o_pre"], nth(n))
                act.activation(ob[:], o[:], ACT.Square, scale=D ** -0.5, accum_out=rs[:, 3:4]).then_inc(S["fsq_done"], 1)
            head(0, False)
            pairs(act, body)

        @block.vector
        def _(dve):
            dve.memset(h[:], 0.0)
            dve.memset(ones_b[:], 1.0)
            dve.memset(ones[:], 1.0).then_inc(S["prep"], 1)
            lead(dve, *(S[n] for n in "cb_done dm_done ml_done y_read h_done ss_done ob_done o_pre fin_done h_dec hn_done".split()))
            dve.wait_ge(S["prep"], 1)

            def decay(n, m):
                if not isinstance(m, int) or m >= 2:
                    dve.wait_ge(S["r_mm"], nth(2 * n + 1))
                dve.tensor_tensor(by_head(h[:]), by_head(h[:]), per_head(cd, n, 0), ALU.mult).then_inc(S["h_dec"], 1)

            def add_state(m):
                dve.wait_ge(S["h_dec"], nth(m))
                dve.wait_ge(S["h_mm"], nth(m))
                dve.tensor_tensor(h[:], h[:], in_ps[:].rearrange("p a b -> p (a b)"), ALU.add).then_inc(S["h_done"], 1)
                dve.wait_ge(S["h_done"], nth(m))

            for s in range(2):
                decay(NC_LAT + s, s)
                add_state(s)

            def shared(n):
                dve.wait_ge(S["cb_mm"], nth(n))
                dve.wait_ge(S["consts"], 16 * 7)
                dve.tensor_copy(dt_now[:], dt[:, bass.ds(n, 1)].rearrange("p a h -> p (a h)"))
                dve.tensor_copy(cb_now[:].rearrange("p g i -> p (g i)"), m_ps[:, 0:GROUPS * P]).then_inc(S["cb_done"], 1)

            def least(n, k):
                dve.wait_ge(S["dc_done"], nth(6 * n + k))
                cols = es[:, 4 * k:4 * k + 4].rearrange("p h i -> p (h i)")
                dve.tensor_tensor(cols, cols, d_ps[:, 1], ALU.min).then_inc(S["dm_done"], 1)

            def weigh(n, k):
                step = chained(dve, S["w_step"], 2 * (4 * n + k))
                heads = slice(4 * k, 4 * k + 4)
                dve.wait_ge(S["cb_done"], nth(n))
                dve.wait_ge(S["wb_done"], nth(4 * n + k))
                for head in range(4 * k, 4 * k + 4):
                    ins = dve.scalar_tensor_tensor(wt[:, head], tri[:, 0], dt_now[:, head:head + 1], wt[:, head], ALU.mult, ALU.add)
                step(ins)
                step(dve.tensor_tensor(wt[:, heads], wt[:, heads], cb_now[:, k // 2].unsqueeze(1).to_broadcast([P, 4, P]), ALU.mult))
                dve.wait_ge(S["e_done"], nth(4 * n + k))
                dve.tensor_tensor(es[:, heads], es[:, heads], wt[:, heads], ALU.mult).then_inc(S["ml_done"], 1)

            def hyena_norm(n):
                dve.tensor_copy(rs[:, 2:3], ssh[:, bass.ds(n, 1)]).then_inc(S["hn_done"], 1)

            def sum_done(n):
                dve.wait_ge(S["ss_mm"], nth(n))
                dve.wait_ge(S["ob_done"], nth(2 * n - 1))
                dve.tensor_scalar(rs[:, 0:1], m_ps[:, 0:1], 1.0 / D, EPS, ALU.mult, ALU.add).then_inc(S["ss_done"], 1)

            def out_part(n, half):
                cols = slice(half * BANK, (half + 1) * BANK)
                dve.wait_ge(S["rs_done"], nth(n))
                dve.wait_ge(S["oa_done"], nth(2 * n + half))
                dve.wait_ge(S["o_mm"], nth(4 * n + 2 * half + 1))
                dve.scalar_tensor_tensor(o[:, cols], o_ps[:, 1], rs[:, 0:1], o[:, cols], ALU.mult, ALU.add).then_inc(S["ob_done"], 1)

            def residual(n):
                last = isinstance(n, int) and n == LAST
                if not last:
                    hyena_norm(n + 1)
                dve.wait_ge(S["ob_done"], nth(2 * n + 1))
                v = S["v_step"]
                dve.tensor_tensor(o[:], o[:], gate_row[:], ALU.mult).then_inc(v, 1)
                dve.wait_ge(v, n + 1)
                dve.wait_ge(late_in, 32 * n + 32)
                dve.wait_ge(stored, nth(n - 1, 16))
                dve.tensor_tensor(o[:], o[:], xres[:], ALU.add).then_inc(S["o_pre"], 1)

            def finish(n):
                dve.wait_ge(S["frs_done"], nth(n))
                dve.scalar_tensor_tensor(ob[:], o[:], rs[:, 1:2], fw[:], ALU.mult, ALU.mult).then_inc(S["fin_done"], 1)

            def terms(n, s, i):
                for f in range(2):
                    q = slice(4 * f, 4 * f + 4)
                    dve.wait_ge(S["r_mm"], nth(2 * n + f))
                    if f == 0:
                        dve.wait_ge(S["dc_done"], nth(6 * n + 5))
                        dve.wait_ge(S["xt_done"], nth(n))
                        dve.wait_ge(S["o_mm"], nth(4 * (n - 1) + 3))
                        dve.wait_ge(S["sq_done"], nth(n - 1))
                        dve.wait_ge(early[s], EARLY * i + EARLY)
                    dve.wait_ge(S["ys_done"], nth(2 * (n - 1) + f))
                    dve.tensor_tensor(ys[:, q].rearrange("p m i -> p (m i)"), in_ps[:, 0], ea[:, f, 0], ALU.mult)
                    dve.tensor_tensor(tmp[:, f], in_ps[:, 1], ea[:, f, 1], ALU.mult)
                    skip = xt[:, s, q].rearrange("p m i -> p (m i)")
                    dve.tensor_tensor(skip, y_ps[:], skip, ALU.add).then_inc(S["y_read"], 1)

            def head(n, with_out):
                if not with_out:
                    shared(n)
                least(n, 0)
                weigh(n, 0)
                if with_out:
                    sum_done(n - 1)
                least(n, 1)
                weigh(n, 1)
                if with_out:
                    out_part(n - 1, 0)
                least(n, 2)
                weigh(n, 2)
                least(n, 3)
                weigh(n, 3)
                if with_out:
                    out_part(n - 1, 1)
                    residual(n - 1)

            dve.wait_ge(S["rsh_done"], 1)
            hyena_norm(0)
            head(0, False)
            dve.wait_ge(S["w_in_"], 16)
            for k in range(2 * KT):
                ins = dve.tensor_scalar(w_out[:, k], w_out[:, k], gn[:, k:k + 1], None, ALU.mult)
            ins.then_inc(S["w_ready"], 1)

            def body(n, i, s):
                last = isinstance(n, int) and n == LAST
                terms(n, s, i)
                if not last:
                    shared(n + 1)
                decay(n, n + 2)
                add_state(n + 2)
                if not isinstance(n, int) or n > 0:
                    finish(n - 1)
                if last:
                    sum_done(n)
                    out_part(n, 0)
                    out_part(n, 1)
                    residual(n)
                    finish(n)
                else:
                    head(n + 1, True)
            body(0, 0, 0)
            pairs(dve, body, head=1)
INPUTS = ["x", "c", "ctx", "c_ctx", "norm_w", "ada_w", "ada_b", "w_in", "ssd_conv_w", "ssd_conv_b", "dt_bias", "a_log",
          "d_skip", "hy_conv_w", "hy_conv_b", "filt_w1", "filt_b1", "filt_w2", "filt_b2", "filt_w3", "filt_b3", "filt_w4",
          "filt_freq", "hy_bias", "gnorm_w", "w_out", "final_norm_w"]


def scales_and_hyena_back(nc, t, keep):
    with ExitStack() as ph:
        block = ph.enter_context(nc.Block())
        keep["c_y_done"] = nc.alloc_semaphore("c_y_done")
        ssd_scales(nc, t, keep, ph, block)
        hyena_back(nc, t, keep, ph, block)


def program(nc, t):
    with ExitStack() as ctx:
        def kept(name, shape, dt=F32):
            return ctx.enter_context(nc.sbuf_tensor(name, shape, dt))
        keep = {"eye": kept("eye", [P, P]), "gate_row": kept("gate_row", [P, D]), "ssh": kept("ssh", [P, NC_LAT]),
                "dt_raw": kept("dt_raw", [P, NCH, 2 * HEADS])}

        keep["ada_in"] = ctx.enter_context(nc.semaphore("ada_in"))
        keep["x_in"] = [ctx.enter_context(nc.semaphore(f"x_in{i}")) for i in range(2)]

        def phase(build):
            with nc.cleanup_on_exit():
                build(nc, t, keep)

        with nc.sbuf_tensor("early", [P, 2 * KT * TOK], F32) as keep["early"]:
            pass
        with nc.sbuf_tensor("x_hi", [P, KT, SEQ], F32R) as keep["x_hi"], nc.sbuf_tensor("x_lo", [P, KT, SEQ], F32R) as keep["x_lo"]:
            with nc.sbuf_tensor("c_hi", [P, KT, CTX], F32R) as keep["c_hi"], nc.sbuf_tensor("c_lo", [P, KT, CTX], F32R) as keep["c_lo"]:
                with nc.sbuf_tensor("xg", [P, 2, 4, D], F32) as keep["xg"]:
                    with nc.sbuf_tensor("hT", [FW, SEQ + RIN], F32) as keep["hT"]:
                        phase(filter_network)
                        phase(filter_first_stage)
                    phase(prepare)
                phase(project_ssd)
            phase(project_hyena)
        phase(spectra)
        keep["to_end"], keep["chunk_decay"] = kept("to_end", [P, NCH, 2 * HEADS]), kept("chunk_decay", [P, NCH, 2 * HEADS])
        phase(scales_and_hyena_back)
        phase(ssd_backward_states)
        phase(ssd_and_out)


SCRATCH = {
    "f_spec": [RIN, 2, P, D],
    "u_spec": [RIN, 2, P, D],
    "v_spec": [RIN, 2, P, D],
    "gate_t": [KT, P, SEQ],
    "yh_t": [KT, P, SEQ],
    "zs_t": [KT, P, SEQ],
    "xbc_t": [XBC_T, P, TOK],
    "xbc": [NCH, P, XBC_T * P],
    "h_back": [NCH, P, D],
}


def kernel(**inputs):
    import concourse.bacc as _bacc
    from concourse.bass_utils import run_bass_kernel_spmd as _run

    nc = _bacc.Bacc("TRN2", target_bir_lowering=False, num_devices=1)
    arrays = {n: np.ascontiguousarray(inputs[n]) for n in INPUTS}
    arrays.update(shape_constants())
    t = {}
    for name, a in arrays.items():
        t[name] = nc.dram_tensor("in_" + name, a.shape, mybir.dt.from_np(a.dtype), kind="ExternalInput").ap()
    for name, shape in SCRATCH.items():
        t[name] = nc.dram_tensor("scratch_" + name, shape, F32, kind="Internal").ap()
    t["rows"] = nc.dram_tensor("scratch_rows", ROWS_SHAPE, BF16, kind="Internal").ap()
    t["out"] = nc.dram_tensor("out_0", [1, SEQ, D], F32, kind="ExternalOutput").ap()
    program(nc, t)
    r = _run(nc, [{"in_" + n: a for n, a in arrays.items()}], core_ids=[0])
    return r.results[0]["out_0"]
```
